# Optimizing a Trainium2 kernel written in Bass

```python
import math
import jax, jax.numpy as jnp
from jax import lax
import numpy as np

D_MODEL = 1024
BATCH = 1
SEQ = 512
DEPTH = 1

CHUNK = 64
DN_HEADS = 8
DN_HEAD_DIM = 128
DN_WIDTH = DN_HEADS * DN_HEAD_DIM
CONV_WIDTH = 4
AT_HEADS = 8
AT_HEAD_DIM = 64
AT_WIDTH = AT_HEADS * AT_HEAD_DIM
LEFT_CHUNKS = 8
BAND = LEFT_CHUNKS + 1
REL_CLIP = 256
N_EXPERTS = 64
TOP_K = 6
EXPERT_DIM = 256
SHARED_DIM = 256
ROUTED_SCALE = 2.5
MOE_BLOCK = 128
ALPHA = (2 * DEPTH) ** 0.25
BETA_INIT = (8 * DEPTH) ** -0.25
LN_EPS = 1e-5
RMS_EPS = 1e-6
L2_EPS = 1e-6
NEG_INF = -1e30

_IN_SPLITS = (DN_WIDTH, DN_WIDTH, DN_WIDTH, DN_WIDTH, DN_HEADS, DN_HEADS,
              AT_WIDTH, AT_WIDTH, AT_WIDTH, D_MODEL, D_MODEL)
IN_COLS = sum(_IN_SPLITS)
SPLIT_POINTS = tuple(int(v) for v in np.cumsum(_IN_SPLITS)[:-1])

kernel_name = "hybrid_deltanet_chunkattn_moe_deepnorm"

def layer_norm(x, g, b):
    xf = x.astype(jnp.float32)
    mu = jnp.mean(xf, axis=-1, keepdims=True)
    var = jnp.mean(jnp.square(xf - mu), axis=-1, keepdims=True)
    y = (xf - mu) * lax.rsqrt(var + LN_EPS) * g.astype(jnp.float32) + b.astype(jnp.float32)
    return y.astype(x.dtype)

def causal_depthwise_conv(x, w):
    T = x.shape[1]
    xp = jnp.pad(x, ((0, 0), (CONV_WIDTH - 1, 0), (0, 0)))
    return sum(xp[:, i:i + T] * w[i] for i in range(CONV_WIDTH))

def l2_normalize(x):
    return x * lax.rsqrt(jnp.sum(jnp.square(x), axis=-1, keepdims=True) + L2_EPS)

def delta_rule_chunked(q, k, v, g, beta):
    B, T, H, dk = q.shape
    dv = v.shape[-1]
    nc = T // CHUNK

    def chunks(a):
        return jnp.moveaxis(a.reshape(B, nc, CHUNK, H, -1), 3, 1)

    q, k, v = chunks(q), chunks(k), chunks(v)
    g = jnp.moveaxis(g.reshape(B, nc, CHUNK, H), 3, 1)
    beta = jnp.moveaxis(beta.reshape(B, nc, CHUNK, H), 3, 1)
    gc = jnp.cumsum(g, axis=-1)
    pos = jnp.arange(CHUNK)
    incl = pos[:, None] >= pos[None, :]
    strict = pos[:, None] > pos[None, :]
    decay = jnp.exp(jnp.where(incl, gc[..., :, None] - gc[..., None, :], -jnp.inf))

    kb = k * beta[..., None]
    lower = jnp.where(strict, jnp.einsum('bhnid,bhnjd->bhnij', kb, k) * decay, 0.0)
    eye = jnp.broadcast_to(jnp.eye(CHUNK, dtype=lower.dtype), lower.shape)
    t_inv = lax.linalg.triangular_solve(eye + lower, eye, left_side=True, lower=True,
                                        unit_diagonal=True)
    w = t_inv @ (kb * jnp.exp(gc)[..., None])
    u = t_inv @ (v * beta[..., None])
    qk = jnp.einsum('bhnid,bhnjd->bhnij', q, k) * decay
    q_dec = q * jnp.exp(gc)[..., None]
    k_dec = k * jnp.exp(gc[..., -1:] - gc)[..., None]
    chunk_decay = jnp.exp(gc[..., -1])

    xs = tuple(jnp.moveaxis(a, 2, 0) for a in (u, w, q_dec, qk, k_dec, chunk_decay))

    def step(S, inp):
        u_n, w_n, qd_n, qk_n, kd_n, dec_n = inp
        v_new = u_n - w_n @ S
        o_n = qd_n @ S + qk_n @ v_new
        S = S * dec_n[..., None, None] + jnp.swapaxes(kd_n, -1, -2) @ v_new
        return S, o_n

    S0 = jnp.zeros((B, H, dk, dv), jnp.float32)
    _, o = lax.scan(step, S0, xs)
    return o.transpose(1, 0, 3, 2, 4).reshape(B, T, H, dv)

def gated_deltanet(q_in, k_in, v_in, z, b_in, a_in, conv_w, a_log, dt_bias, norm_w):
    B, T, _ = q_in.shape
    qkv = jax.nn.silu(causal_depthwise_conv(jnp.concatenate([q_in, k_in, v_in], axis=-1), conv_w))
    qkv = qkv.astype(jnp.float32).reshape(B, T, 3, DN_HEADS, DN_HEAD_DIM)
    q = l2_normalize(qkv[:, :, 0]) * (DN_HEAD_DIM ** -0.5)
    k = l2_normalize(qkv[:, :, 1])
    v = qkv[:, :, 2]
    beta = jax.nn.sigmoid(b_in.astype(jnp.float32))
    g = -jnp.exp(a_log.astype(jnp.float32)) * jax.nn.softplus(a_in.astype(jnp.float32)
                                                              + dt_bias.astype(jnp.float32))
    o = delta_rule_chunked(q, k, v, g, beta)
    o = o * lax.rsqrt(jnp.mean(jnp.square(o), axis=-1, keepdims=True) + RMS_EPS)
    o = o * norm_w.astype(jnp.float32) * jax.nn.silu(z.astype(jnp.float32).reshape(o.shape))
    return o.reshape(B, T, DN_WIDTH).astype(q_in.dtype)

def chunk_band_attention(q_in, k_in, v_in, rel_table):
    B, T, _ = q_in.shape
    nc = T // CHUNK
    q = q_in.reshape(B, nc, CHUNK, AT_HEADS, AT_HEAD_DIM)
    pad = ((0, 0), (LEFT_CHUNKS, 0), (0, 0), (0, 0), (0, 0))
    k = jnp.pad(k_in.reshape(B, nc, CHUNK, AT_HEADS, AT_HEAD_DIM), pad)
    v = jnp.pad(v_in.reshape(B, nc, CHUNK, AT_HEADS, AT_HEAD_DIM), pad)
    band_idx = jnp.arange(nc)[:, None] + jnp.arange(BAND)[None, :]
    kb = k[:, band_idx].reshape(B, nc, BAND * CHUNK, AT_HEADS, AT_HEAD_DIM)
    vb = v[:, band_idx].reshape(B, nc, BAND * CHUNK, AT_HEADS, AT_HEAD_DIM)
    scores = jnp.einsum('bnqhd,bnkhd->bhnqk', q, kb).astype(jnp.float32) * (AT_HEAD_DIM ** -0.5)
    q_pos = jnp.arange(CHUNK)
    k_pos = jnp.arange(BAND * CHUNK) - LEFT_CHUNKS * CHUNK
    rel = jnp.clip(k_pos[None, :] - q_pos[:, None], -REL_CLIP, REL_CLIP) + REL_CLIP
    bias = rel_table.astype(jnp.float32)[:, rel]
    key_valid = jnp.repeat(band_idx >= LEFT_CHUNKS, CHUNK, axis=1)
    scores = jnp.where(key_valid[None, None, :, None, :], scores + bias[None, :, None], NEG_INF)
    p = jax.nn.softmax(scores, axis=-1).astype(vb.dtype)
    o = jnp.einsum('bhnqk,bnkhd->bnqhd', p, vb)
    return o.reshape(B, T, AT_WIDTH)

def moe_ffn(x, router_w, router_bias, w_gate_up, w_down, ws_gate_up, ws_down):
    B, T, D = x.shape
    N = B * T
    xt = x.reshape(N, D)
    scores = jax.nn.sigmoid((xt @ router_w).astype(jnp.float32))
    _, sel = lax.top_k(scores + router_bias.astype(jnp.float32), TOP_K)
    wsel = jnp.take_along_axis(scores, sel, axis=-1)
    wsel = wsel / jnp.sum(wsel, axis=-1, keepdims=True) * ROUTED_SCALE

    nk = N * TOP_K
    flat_e = sel.reshape(nk)
    flat_t = jnp.repeat(jnp.arange(N, dtype=jnp.int32), TOP_K)
    flat_w = wsel.reshape(nk)
    order = jnp.argsort(flat_e)
    e_s, t_s, w_s = flat_e[order], flat_t[order], flat_w[order]
    counts = jnp.bincount(flat_e, length=N_EXPERTS)
    start = jnp.cumsum(counts) - counts
    padded = (counts + MOE_BLOCK - 1) // MOE_BLOCK * MOE_BLOCK
    pend = jnp.cumsum(padded)
    pstart = pend - padded
    dest = pstart[e_s] + (jnp.arange(nk) - start[e_s])
    n_blocks = -(-(nk + N_EXPERTS * (MOE_BLOCK - 1)) // MOE_BLOCK)
    n_rows = n_blocks * MOE_BLOCK
    row_tok = jnp.full((n_rows,), N, jnp.int32).at[dest].set(t_s)
    row_w = jnp.zeros((n_rows,), jnp.float32).at[dest].set(w_s)
    blk_e = jnp.minimum(jnp.searchsorted(pend, jnp.arange(n_blocks) * MOE_BLOCK, side='right'),
                        N_EXPERTS - 1)
    x_pad = jnp.concatenate([xt, jnp.zeros((1, D), xt.dtype)], axis=0)

    def block_fn(args):
        tok, wt, e = args
        gu = x_pad[tok] @ w_gate_up[e]
        h = jax.nn.silu(gu[:, :EXPERT_DIM]) * gu[:, EXPERT_DIM:]
        return (h @ w_down[e]) * wt[:, None]

    y_rows = lax.map(block_fn, (row_tok.reshape(n_blocks, MOE_BLOCK),
                                row_w.reshape(n_blocks, MOE_BLOCK), blk_e))
    routed = jax.ops.segment_sum(y_rows.reshape(n_rows, D), row_tok, num_segments=N + 1)[:N]
    gus = xt @ ws_gate_up
    shared = (jax.nn.silu(gus[:, :SHARED_DIM]) * gus[:, SHARED_DIM:]) @ ws_down
    return (routed.astype(x.dtype) + shared).reshape(B, T, D)

def setup_inputs(seed: int = 0) -> dict:
    key = jax.random.key(seed)
    ks = jax.random.split(key, 24)
    L, D = DEPTH, D_MODEL
    nrm = jax.random.normal
    dt = jnp.exp(jax.random.uniform(ks[4], (L, DN_HEADS)) * (math.log(0.1) - math.log(0.001))
                 + math.log(0.001))
    return {
        'x': nrm(ks[0], (BATCH, SEQ, D), jnp.float32),
        'w_in': nrm(ks[1], (L, D, IN_COLS), jnp.float32) * D ** -0.5,
        'conv_w': nrm(ks[2], (L, CONV_WIDTH, 3 * DN_WIDTH), jnp.float32) * CONV_WIDTH ** -0.5,
        'a_log': jnp.log(jax.random.uniform(ks[3], (L, DN_HEADS), jnp.float32, 1.0, 16.0)),
        'dt_bias': dt + jnp.log(-jnp.expm1(-dt)),
        'dn_norm_w': 1.0 + 0.02 * nrm(ks[5], (L, DN_HEAD_DIM), jnp.float32),
        'rel_table': 0.5 * nrm(ks[6], (L, AT_HEADS, 2 * REL_CLIP + 1), jnp.float32),
        'w_branch_a': nrm(ks[7], (L, DN_WIDTH, D), jnp.float32) * DN_WIDTH ** -0.5,
        'w_branch_b': nrm(ks[8], (L, AT_WIDTH, D), jnp.float32) * AT_WIDTH ** -0.5,
        'w_out': nrm(ks[9], (L, D, D), jnp.float32) * D ** -0.5 * BETA_INIT,
        'ln1_g': 1.0 + 0.02 * nrm(ks[10], (L, D), jnp.float32),
        'ln1_b': 0.02 * nrm(ks[11], (L, D), jnp.float32),
        'router_w': nrm(ks[12], (L, D, N_EXPERTS), jnp.float32) * D ** -0.5,
        'router_bias': 0.01 * nrm(ks[13], (L, N_EXPERTS), jnp.float32),
        'expert_w_gate_up': nrm(ks[14], (L, N_EXPERTS, D, 2 * EXPERT_DIM), jnp.float32) * D ** -0.5,
        'expert_w_down': nrm(ks[15], (L, N_EXPERTS, EXPERT_DIM, D), jnp.float32)
                         * EXPERT_DIM ** -0.5 * BETA_INIT,
        'shared_w_gate_up': nrm(ks[16], (L, D, 2 * SHARED_DIM), jnp.float32) * D ** -0.5,
        'shared_w_down': nrm(ks[17], (L, SHARED_DIM, D), jnp.float32) * SHARED_DIM ** -0.5 * BETA_INIT,
        'ln2_g': 1.0 + 0.02 * nrm(ks[18], (L, D), jnp.float32),
        'ln2_b': 0.02 * nrm(ks[19], (L, D), jnp.float32),
    }

def reference(x, w_in, conv_w, a_log, dt_bias, dn_norm_w, rel_table, w_branch_a, w_branch_b,
              w_out, ln1_g, ln1_b, router_w, router_bias, expert_w_gate_up, expert_w_down,
              shared_w_gate_up, shared_w_down, ln2_g, ln2_b):
    for l in range(DEPTH):
        proj = x @ w_in[l]
        dq, dk, dv, dz, db, da, aq, ak, av, ga, gb = jnp.split(proj, SPLIT_POINTS, axis=-1)
        ya = gated_deltanet(dq, dk, dv, dz, db, da, conv_w[l], a_log[l], dt_bias[l],
                            dn_norm_w[l]) @ w_branch_a[l]
        yb = chunk_band_attention(aq, ak, av, rel_table[l]) @ w_branch_b[l]
        mix = (jax.nn.sigmoid(ga) * ya + jax.nn.sigmoid(gb) * yb) @ w_out[l]
        x = layer_norm(ALPHA * x + mix, ln1_g[l], ln1_b[l])
        ffn = moe_ffn(x, router_w[l], router_bias[l], expert_w_gate_up[l], expert_w_down[l],
                      shared_w_gate_up[l], shared_w_down[l])
        x = layer_norm(ALPHA * x + ffn, ln2_g[l], ln2_b[l])
    return x


_drawn_inputs = setup_inputs


def setup_inputs(seed=0):
    import zlib

    import numpy as np

    out = dict(_drawn_inputs(seed))
    spreads = {}
    factors = {'dn_norm_w': 2.776, 'ln2_g': 2.908, 'ln2_b': 2.842}
    for name, (base, spread) in spreads.items():
        noise = np.random.default_rng([zlib.crc32(name.encode()), seed]).standard_normal(out[name].shape)
        drawn = base * np.exp(spread * noise) if base else spread * noise
        out[name] = __import__('jax').numpy.asarray(drawn.astype(out[name].dtype))
    for name, factor in factors.items():
        out[name] = (out[name] * factor).astype(out[name].dtype)
    return out
```

```python
from contextlib import ExitStack

import concourse.bass as bass
from concourse import mybir

F32 = mybir.dt.float32
BF16 = mybir.dt.bfloat16
I32 = mybir.dt.int32
ALU = mybir.AluOpType
ACT = mybir.ActivationFunctionType
AX = mybir.AxisListType

P = 128
D = 1024
SEQ = 512
KC = D // P
TT = SEQ // P
HEADS = 8
CONV = 4
LEVELS = 7
AHEADS = 8
AD = 64
AW = AHEADS * AD
CLIP = 256
ACHUNK = 64
NE = 64
TOPK = 6
ED = 256
BLK = 64
NBLK = SEQ // BLK
MAXOVER = SEQ * TOPK // BLK
GROUP = 4
LISTS = NE + MAXOVER + GROUP
OOB = float(1 << 20)
ROUTED_SCALE = 2.5
ALPHA = 2.0 ** 0.25
LN_EPS = 1e-5
RMS_EPS = 1e-6
L2_EPS = 1e-6
NEG = -1e30

Q0, K0, V0, Z0 = 0, D, 2 * D, 3 * D
BA0 = 4 * D
AQ0 = BA0 + 2 * HEADS
AK0 = AQ0 + AW
AV0 = AK0 + AW
GA0 = AV0 + AW
GB0 = GA0 + D


class Memory:

    def __init__(self, nc, ctx):
        self.nc, self.ctx, self.allocated = nc, ctx, []

    def sb(self, name, shape, dt=F32):
        return self.ctx.enter_context(self.nc.sbuf_tensor(name, shape, dt))

    def sem(self, name):
        self.allocated.append(self.nc.alloc_semaphore(name))
        return self.allocated[-1]

    def sems(self, name, n):
        return [self.sem(f"{name}{i}") for i in range(n)]


def run_phase(nc, phase, *args):
    with ExitStack() as ctx:
        mem = Memory(nc, ctx)
        phase(nc, mem, *args)
        nc.clear_and_free_semaphores(mem.allocated)
        nc.all_engine_barrier()


def setup_phase(nc, mem, T, ps, x, w_in, conv_w, a_log, dt_bias, dn_norm_w):
    zero_done = mem.sem("zero_done")
    const_ready = mem.sem("const_ready")
    pool_step = mem.sem("pool_step")
    x_in = mem.sem("x_in")
    small_in = mem.sem("small_in")
    ba_in = mem.sem("ba_in")
    xT_psum = mem.sem("xT_psum")
    xT_copied = mem.sem("xT_copied")
    ba_psum = mem.sem("ba_psum")
    ba_copied = mem.sem("ba_copied")
    cum_psum = mem.sem("cum_psum")
    gates_act = mem.sem("gates_act")
    gates_dve = mem.sem("gates_dve")
    gates_ready = mem.sem("gates_ready")
    cw_psum = mem.sem("cw_psum")
    cw_ready = mem.sem("cw_ready")

    ident, upper, ones = T["ident"], T["upper"], T["ones"]
    xs, xT, GT = T["x"], T["xT"], T["GT"]
    cw_rows, cw = T["cw_rows"], T["cw"]
    w_ba = T["w_ba"]
    gw = T["gate_work"]
    bias_row = T["bias_row"]
    masks = T["masks"]

    with nc.Block() as block:

        @block.sync
        def _(sp):
            for t in range(TT):
                sp.dma_start(xs[:, t, :], x[0, t * P:(t + 1) * P, :]).then_inc(x_in, 16)
            sp.dma_start(w_ba[:, :, :],
                         w_in[:, BA0:AQ0].rearrange("(c p) n -> p c n", p=P)).then_inc(ba_in, 16)

        @block.gpsimd
        def _(pool):
            steps = 0
            nc.gpsimd.memset(ones[:, :], 1.0).then_inc(pool_step, 1)
            nc.gpsimd.memset(ident[:, :], 0.0).then_inc(pool_step, 1)
            nc.gpsimd.memset(masks[:, :, :], 0.0).then_inc(pool_step, 1)
            for i, value in enumerate((L2_EPS, RMS_EPS, LN_EPS)):
                nc.gpsimd.memset(T["eps"][:, i:i + 1], value)
            steps = 3
            pool.wait_ge(pool_step, steps)
            nc.gpsimd.affine_select(out=ident[:, :], in_=ident[:, :], compare_op=ALU.not_equal, fill=1.0,
                                    base=0, pattern=[[-1, P]], channel_multiplier=1).then_inc(const_ready, 1)
            nc.gpsimd.affine_select(out=upper[:, :], in_=ones[:, :], compare_op=ALU.is_ge, fill=0.0,
                                    base=0, pattern=[[1, P]], channel_multiplier=-1).then_inc(const_ready, 1)
            for l in range(LEVELS):
                b = 1 << l
                half = masks[:, l, :].rearrange("p (m r) -> p m r", r=2 * b)[:, :, b:2 * b]
                pool.wait_ge(pool_step, steps)
                nc.gpsimd.memset(half, 1.0).then_inc(pool_step, 1)
                pool.wait_ge(pool_step, steps + 1)
                nc.gpsimd.affine_select(out=half, in_=half, compare_op=ALU.is_ge, fill=0.0, base=0,
                                        pattern=[[-2 * b, P // (2 * b)], [0, b]],
                                        channel_multiplier=1).then_inc(pool_step, 1)
                pool.wait_ge(pool_step, steps + 2)
                nc.gpsimd.affine_select(out=half, in_=half, compare_op=ALU.is_ge, fill=0.0, base=b - 1,
                                        pattern=[[2 * b, P // (2 * b)], [0, b]],
                                        channel_multiplier=-1).then_inc(pool_step, 1)
                steps += 3

        @block.tensor
        def _(pe):
            pe.wait_ge(const_ready, 2)
            pe.wait_ge(x_in, 16 * TT)
            for c in range(KC):
                if c >= 4:
                    pe.wait_ge(xT_copied, c - 3)
                for t in range(TT):
                    mm = nc.tensor.transpose(ps[c % 4][:, t * P:(t + 1) * P], xs[:, t, c * P:(c + 1) * P], ident[:, :])
                mm.then_inc(xT_psum, 1)
            pe.wait_ge(small_in, 16 * 4)
            nc.tensor.transpose(ps[7][:, 0:96], cw_rows[:, :], ident[0:96, 0:96]).then_inc(cw_psum, 1)
            pe.wait_ge(xT_copied, KC)
            pe.wait_ge(ba_in, 16)
            for t in range(TT):
                for c in range(KC):
                    mm = nc.tensor.matmul(ps[4][:, t * 16:t * 16 + 16], xT[:, c, t * P:(t + 1) * P], w_ba[:, c, :],
                                          start=(c == 0), stop=(c == KC - 1))
            mm.then_inc(ba_psum, 1)
            pe.wait_ge(gates_ready, 1)
            nc.tensor.matmul(ps[5][:, 0:32], upper[:, :], gw[:, 4, :], start=True, stop=True)
            nc.tensor.matmul(ps[6][:, 0:32], ones[:, :], gw[:, 4, :], start=True, stop=True).then_inc(cum_psum, 1)

        @block.scalar
        def _(act):
            act.dma_start(cw_rows[:, :], conv_w.rearrange("i (g c) -> (i g) c", c=P)).then_inc(small_in, 16)
            act.dma_start(bias_row[:, 0:HEADS], dt_bias[0:1, :].partition_broadcast(P)).then_inc(small_in, 16)
            act.dma_start(bias_row[:, HEADS:2 * HEADS], a_log[0:1, :].partition_broadcast(P)).then_inc(small_in, 16)
            act.dma_start(T["dn_w"][:, :], dn_norm_w.rearrange("a p -> p a")).then_inc(small_in, 16)
            for c in range(0, KC, 2):
                act.wait_ge(xT_psum, c + 1)
                nc.scalar.copy(xT[:, c, :], ps[c % 4][:, :]).then_inc(xT_copied, 1)
                act.wait_ge(xT_copied, c + 2)
            b_in = T["ba"][:, :].rearrange("p (t n) -> p n t", n=16)[:, 0:HEADS, :]
            act.wait_ge(ba_copied, 1)
            act.wait_ge(small_in, 16 * 4)
            nc.scalar.activation(gw[:, 0, :].rearrange("p (h t) -> p h t", t=TT), b_in, ACT.Exp,
                                 scale=-1.0).then_inc(gates_act, 1)
            nc.scalar.activation(bias_row[:, 2 * HEADS:3 * HEADS], bias_row[:, HEADS:2 * HEADS],
                                 ACT.Exp).then_inc(gates_act, 1)
            act.wait_ge(gates_dve, 2)
            nc.scalar.activation(gw[:, 3, :], gw[:, 2, :], ACT.Exp, scale=-1.0).then_inc(gates_act, 1)
            act.wait_ge(gates_dve, 3)
            nc.scalar.activation(gw[:, 5, :], gw[:, 3, :], ACT.Ln).then_inc(gates_act, 1)
            act.wait_ge(gates_dve, 8)
            nc.scalar.activation(GT[:, :, 2, :], gw[:, 0, :].rearrange("p (h t) -> p h t", t=TT), ACT.Exp).then_inc(gates_act, 1)
            nc.scalar.activation(GT[:, :, 4, :], gw[:, 5, :].rearrange("p (h t) -> p h t", t=TT),
                                 ACT.Exp).then_inc(gates_act, 1)
            nc.scalar.activation(GT[:, :, 3, :], gw[:, 1, :].rearrange("p (h t) -> p h t", t=TT), ACT.Exp).then_inc(gates_act, 1)

        @block.vector
        def _(dve):
            for c in range(1, KC, 2):
                dve.wait_ge(xT_psum, c + 1)
                dve.wait_ge(xT_copied, c)
                nc.vector.tensor_copy(xT[:, c, :], ps[c % 4][:, :]).then_inc(xT_copied, 1)
            dve.wait_ge(cw_psum, 1)
            nc.vector.tensor_copy(cw[:, :], ps[7][:, 0:96]).then_inc(cw_ready, 1)
            dve.wait_ge(ba_psum, 1)
            nc.vector.tensor_copy(T["ba"][:, :], ps[4][:, 0:64]).then_inc(ba_copied, 1)
            dve.wait_ge(ba_copied, 1)
            dve.wait_ge(small_in, 16 * 4)
            a_in = T["ba"][:, :].rearrange("p (t n) -> p n t", n=16)[:, HEADS:2 * HEADS, :]
            v = lambda k: gw[:, k, :].rearrange("p (h t) -> p h t", t=TT)
            row = lambda k: bias_row[:, k * HEADS:(k + 1) * HEADS].unsqueeze(2).broadcast_to([P, HEADS, TT])
            nc.vector.tensor_tensor(v(1), a_in, row(0), ALU.add).then_inc(gates_dve, 1)
            dve.wait_ge(gates_dve, 1)
            nc.vector.scalar_tensor_tensor(out=gw[:, 2, :], in0=gw[:, 1, :], scalar=-1.0, in1=gw[:, 1, :],
                                           op0=ALU.mult, op1=ALU.max).then_inc(gates_dve, 1)
            dve.wait_ge(gates_act, 3)
            nc.vector.tensor_scalar(gw[:, 3, :], gw[:, 3, :], 1.0, None, ALU.add).then_inc(gates_dve, 1)
            dve.wait_ge(gates_act, 4)
            nc.vector.scalar_tensor_tensor(out=gw[:, 2, :], in0=gw[:, 1, :], scalar=0.0, in1=gw[:, 5, :],
                                           op0=ALU.max, op1=ALU.add).then_inc(gates_dve, 1)
            dve.wait_ge(gates_dve, 4)
            nc.vector.scalar_tensor_tensor(out=v(4), in0=v(2), scalar=-1.0, in1=row(2),
                                           op0=ALU.mult, op1=ALU.mult).then_inc(gates_ready, 1)
            nc.vector.tensor_scalar(gw[:, 0, :], gw[:, 0, :], 1.0, None, ALU.add).then_inc(gates_dve, 1)
            dve.wait_ge(gates_dve, 5)
            nc.vector.reciprocal(GT[:, :, 1, :], v(0)).then_inc(gates_dve, 1)
            dve.wait_ge(gates_ready, 1)
            nc.vector.tensor_copy(GT[:, :, 5, :], v(4)).then_inc(gates_ready, 1)
            dve.wait_ge(cum_psum, 1)
            dve.wait_ge(gates_dve, 6)
            nc.vector.tensor_copy(gw[:, 0, :], ps[5][:, 0:32]).then_inc(gates_dve, 1)
            dve.wait_ge(gates_dve, 7)
            nc.vector.tensor_copy(GT[:, :, 0, :], v(0)).then_inc(gates_ready, 1)
            nc.vector.tensor_copy(gw[:, 5, :], ps[6][:, 0:32]).then_inc(gates_ready, 1)
            dve.wait_ge(gates_ready, 4)
            nc.vector.tensor_tensor(gw[:, 1, :], gw[:, 5, :], gw[:, 0, :], ALU.subtract).then_inc(gates_dve, 1)


def delta_phase(nc, mem, T, ps, w_in):
    S = mem.sem
    w_ready = mem.sems("w_ready", 4)
    proj_done = mem.sems("proj_done", 4)
    tap_done = [mem.sems(f"tap{g}_", CONV) for g in range(3)]
    silu_done = mem.sems("silu_done", 4)
    ug_ready = S("ug_ready")
    tok_psum = mem.sems("tok_psum", 3)
    gcrow_psum = S("gcrow_psum")
    hc_ready = S("hc_ready")
    cwh_ready = S("cwh_ready")
    d_ready = S("d_ready")
    ssq_ready = S("ssq_ready")
    lnr_ready = S("lnr_ready")
    r_ready = S("r_ready")
    coef1 = S("coef1")
    coef2 = S("coef2")
    lnrk_ready = S("lnrk_ready")
    decay_ready = S("decay_ready")
    k_scaled = S("k_scaled")
    kall_scaled = S("kall_scaled")
    q_scaled = S("q_scaled")
    v_scaled = S("v_scaled")
    back_psum = mem.sems("back_psum", 3)
    back_copied = mem.sems("back_copied", 3)
    lt_psum = S("lt_psum")
    qk_psum = S("qk_psum")
    lt_ready = S("lt_ready")
    qk_raw = S("qk_raw")
    qk_ready = S("qk_ready")
    loff_ready = mem.sems("loff_ready", LEVELS)
    xt_ready = mem.sems("xt_ready", LEVELS)
    x_psum = S("x_psum")
    x_ready = mem.sems("x_ready", LEVELS)
    y_psum = mem.sems("y_psum", LEVELS)
    y_ready = mem.sems("y_ready", LEVELS)
    z_psum = mem.sems("z_psum", LEVELS)
    zt_psum = mem.sems("zt_psum", LEVELS)
    wt_psum = S("wt_psum")
    wt_ready = S("wt_ready")
    v_psum = mem.sems("v_psum", TT)
    v_ready = mem.sems("v_ready", TT)
    s_psum = mem.sems("s_psum", TT)
    s_ready = mem.sems("s_ready", TT)
    o_psum = S("o_psum")
    osq_ready = S("osq_ready")
    lno_ready = S("lno_ready")
    ro_ready = S("ro_ready")
    o_ready = S("o_ready")
    ot_psum = S("ot_psum")
    dn_done = S("dn_done")

    ident, upper, ones, masks = T["ident"], T["upper"], T["ones"], T["masks"]
    xT, GT, cw, dnT, eps = T["xT"], T["GT"], T["cw"], T["dnT"], T["eps"]
    w_head = mem.sb("w_head", [P, 4, KC, P])
    ch = mem.sb("by_channel", [P, 3, SEQ])
    zs = mem.sb("z_silu", [P, SEQ])
    hc = mem.sb("head_gates", [P, 6, TT])
    cwh = mem.sb("head_taps", [P, CONV * 3])
    ug = mem.sb("ug", [P, TT, P])
    dd = mem.sb("decay", [P, TT, P])
    ssq = mem.sb("ssq", [P, 2 * TT])
    lnr = mem.sb("lnr", [P, 2 * TT])
    rr = mem.sb("rr", [P, 2 * TT])
    coef = mem.sb("coef", [P, 6, TT])
    kb = mem.sb("kb", [P, TT, P])
    kbe = mem.sb("kbe", [P, TT, P])
    kd = mem.sb("kd", [P, TT, P])
    qn = mem.sb("qn", [P, TT, P])
    qd = mem.sb("qd", [P, TT, P])
    vb = mem.sb("vb", [P, TT, P])
    kbT = mem.sb("kbT", [P, TT, P])
    qnT = mem.sb("qnT", [P, TT, P])
    qdT = mem.sb("qdT", [P, TT, P])
    LT = mem.sb("LT", [P, TT, P])
    QK = mem.sb("QK", [P, TT, P])
    LO = mem.sb("LO", [P, LEVELS, TT, P])
    X = mem.sb("X", [P, TT, P])
    XT = mem.sb("XT", [P, TT, P])
    Y = mem.sb("Y", [P, TT, P])
    wTn = mem.sb("wTn", [P, TT, P])
    vn = mem.sb("vn", [P, TT, P])
    St = mem.sb("state", [P, 2, P])
    on = mem.sb("on", [P, TT, P])
    sq = mem.sb("sq_scratch", [P, 3, TT, P])
    osq = mem.sb("osq", [P, 3, TT])

    tiles = lambda bank: bank[:, :].rearrange("p (n i) -> p n i", n=TT)
    per_tile = lambda col: col.unsqueeze(2).broadcast_to([P, TT, P])
    all_tiles = lambda m: m.unsqueeze(1).broadcast_to([P, TT, P])
    cols = [Q0, K0, V0, Z0]

    with nc.Block() as block:

        @block.sync
        def _(sp):
            def load(g, m):
                sp.dma_start(w_head[:, g, :, :], w_in[:, bass.ds(cols[g] + m * P, P)].rearrange(
                    "(c p) n -> p c n", p=P)).then_inc(w_ready[g], 16)

            for g in range(4):
                load(g, 0)
            with sp.Fori(1, HEADS) as m:
                for g in range(4):
                    sp.wait_ge(proj_done[g], m)
                    load(g, m)

        @block.tensor
        def _(pe):
            def projection(g, c, head1):
                if c == 0:
                    pe.wait_ge(w_ready[g], 16 * head1)
                mm = nc.tensor.matmul(ps[g % 2][:, :], w_head[:, g, c, :], xT[:, c, :],
                                      start=(c == 0), stop=(c == KC - 1))
                if c == KC - 1:
                    mm.then_inc(proj_done[g], 1)

            for g in range(4):
                if g == 2:
                    pe.wait_ge(tap_done[0][3], 1)
                if g == 3:
                    pe.wait_ge(tap_done[1][3], 1)
                for c in range(KC):
                    projection(g, c, 1)

            def body(h, fillers):
                now = h + 1
                queue = [(g, c) for g in range(4) for c in range(KC)] if fillers else []

                def fill(n):
                    for _ in range(min(n, len(queue))):
                        g, c = queue.pop(0)
                        if c == 0:
                            if g == 0:
                                pe.wait_ge(tap_done[2][3], now)
                            elif g == 1:
                                pe.wait_ge(silu_done[3], now)
                            elif g == 2:
                                pe.wait_ge(tap_done[0][3], now + 1)
                            else:
                                pe.wait_ge(tap_done[1][3], now + 1)
                        projection(g, c, now + 1)

                for g in range(3):
                    pe.wait_ge(silu_done[g], now)
                    for n in range(TT):
                        mm = nc.tensor.transpose(ps[2 + g][:, n * P:(n + 1) * P], ch[:, g, n * P:(n + 1) * P], ident[:, :])
                    mm.then_inc(tok_psum[g], 1)
                pe.wait_ge(ug_ready, now)
                nc.tensor.matmul(ps[5][:, :], ones[:, :], ug[:, :, :], start=True, stop=True).then_inc(gcrow_psum, 1)
                fill(4)
                for i, (src, bank, ready) in enumerate([(kb, 7, k_scaled), (qn, 2, q_scaled), (qd, 3, None)]):
                    if ready is not None:
                        pe.wait_ge(ready, now)
                    if i == 1:
                        pe.wait_ge(kall_scaled, now)
                    for n in range(TT):
                        mm = nc.tensor.transpose(ps[bank][:, n * P:(n + 1) * P], src[:, n, :], ident[:, :])
                    mm.then_inc(back_psum[i], 1)
                fill(2)
                pe.wait_ge(back_copied[0], now)
                pe.wait_ge(v_scaled, now)
                for n in range(TT):
                    mm = nc.tensor.matmul(ps[4][:, n * P:(n + 1) * P], ch[:, 1, n * P:(n + 1) * P], kbT[:, n, :],
                                          start=True, stop=True)
                mm.then_inc(lt_psum, 1)
                pe.wait_ge(back_copied[1], now)
                for n in range(TT):
                    mm = nc.tensor.matmul(ps[5][:, n * P:(n + 1) * P], ch[:, 1, n * P:(n + 1) * P], qnT[:, n, :],
                                          start=True, stop=True)
                mm.then_inc(qk_psum, 1)
                fill(2)
                pe.wait_ge(xt_ready[0], now)
                for n in range(TT):
                    mm = nc.tensor.transpose(ps[6][:, n * P:(n + 1) * P], XT[:, n, :], ident[:, :])
                mm.then_inc(x_psum, 1)
                fill(1)
                for l in range(1, LEVELS):
                    pe.wait_ge(x_ready[l - 1], now)
                    pe.wait_ge(loff_ready[l], now)
                    for n in range(TT):
                        mm = nc.tensor.matmul(ps[7][:, n * P:(n + 1) * P], LO[:, l, n, :], X[:, n, :],
                                              start=True, stop=True)
                    mm.then_inc(y_psum[l], 1)
                    fill(1)
                    pe.wait_ge(y_ready[l], now)
                    pe.wait_ge(xt_ready[l - 1], now)
                    if l == 1:
                        pe.wait_ge(back_copied[2], now)
                    if l < LEVELS - 1:
                        for n in range(TT):
                            mm = nc.tensor.matmul(ps[2][:, n * P:(n + 1) * P], XT[:, n, :], Y[:, n, :],
                                                  start=True, stop=True)
                        mm.then_inc(z_psum[l], 1)
                    for n in range(TT):
                        mm = nc.tensor.matmul(ps[3][:, n * P:(n + 1) * P], Y[:, n, :], XT[:, n, :],
                                              start=True, stop=True)
                    mm.then_inc(zt_psum[l], 1)
                    fill(1)
                pe.wait_ge(xt_ready[LEVELS - 1], now)
                for n in range(TT):
                    mm = nc.tensor.matmul(ps[4][:, n * P:(n + 1) * P], kbe[:, n, :], XT[:, n, :], start=True, stop=True)
                mm.then_inc(wt_psum, 1)
                pe.wait_ge(qk_raw, now)
                for n in range(TT):
                    at = slice(n * P, (n + 1) * P)
                    mm = nc.tensor.matmul(ps[5][:, at], XT[:, n, :], vb[:, n, :], start=True, stop=(n == 0))
                    if n:
                        if n == 1:
                            pe.wait_ge(wt_ready, now)
                        pe.wait_ge(s_ready[n - 1], now)
                        mm = nc.tensor.matmul(ps[5][:, at], wTn[:, n, :], St[:, (n - 1) % 2, :], start=False, stop=True)
                    mm.then_inc(v_psum[n], 1)
                    fill(1)
                    pe.wait_ge(v_ready[n], now)
                    if n < TT - 1:
                        nc.tensor.matmul(ps[6][:, 0:P], kd[:, n, :], vn[:, n, :], start=True, stop=True).then_inc(s_psum[n], 1)
                    if n == 0:
                        pe.wait_ge(qk_ready, now)
                    else:
                        nc.tensor.matmul(ps[7][:, at], qdT[:, n, :], St[:, (n - 1) % 2, :], start=True, stop=False)
                    mm = nc.tensor.matmul(ps[7][:, at], QK[:, n, :], vn[:, n, :], start=(n == 0), stop=True)
                    if n == TT - 1:
                        mm.then_inc(o_psum, 1)
                    fill(1)
                fill(3)
                pe.wait_ge(o_ready, now)
                for n in range(TT):
                    mm = nc.tensor.transpose(ps[6][:, n * P:(n + 1) * P], on[:, n, :], ident[:, :])
                mm.then_inc(ot_psum, 1)
                fill(32)

            with pe.Fori(0, HEADS - 1) as h:
                body(h, True)
            body(HEADS - 1, False)

        @block.gpsimd
        def _(pool):
            def make_ug(h, now):
                nc.gpsimd.tensor_tensor(ug[:, :, :], all_tiles(upper[:, :]), per_tile(GT[:, h, 5, :]),
                                        ALU.mult).then_inc(ug_ready, 1)

            make_ug(0, None)

            def body(h, last):
                now = h + 1
                pool.wait_ge(lt_ready, now)
                for l in range(LEVELS):
                    nc.gpsimd.tensor_tensor(LO[:, l, :, :], LT[:, :, :], all_tiles(masks[:, l, :]),
                                            ALU.mult).then_inc(loff_ready[l], 1)
                    if l == 1:
                        pool.wait_ge(qk_raw, now)
                        nc.gpsimd.tensor_tensor(QK[:, :, :], QK[:, :, :], all_tiles(upper[:, :]),
                                                ALU.mult).then_inc(qk_ready, 1)
                if not last:
                    pool.wait_ge(gcrow_psum, now)
                    make_ug(h + 1, now)

            with pool.Fori(0, HEADS - 1) as h:
                body(h, False)
            body(HEADS - 1, True)

        @block.scalar
        def _(act):
            def silus(h, head1, first):
                for g in range(3):
                    act.wait_ge(tap_done[g][3], head1)
                    nc.scalar.activation(ch[:, g, :], ch[:, g, :], ACT.Silu).then_inc(silu_done[g], 1)
                act.wait_ge(proj_done[3], head1)
                if not first:
                    act.wait_ge(dn_done, h + 1)
                nc.scalar.activation(zs[:, :], ps[1][:, :], ACT.Silu).then_inc(silu_done[3], 1)

            silus(None, 1, True)

            def body(h, last):
                now = h + 1
                for g in range(2):
                    act.wait_ge(tok_psum[g], now)
                    for n in range(TT):
                        a = nc.scalar.activation(sq[:, g, n, :], ps[2 + g][:, n * P:(n + 1) * P], ACT.Square,
                                                 accum_out=ssq[:, g * TT + n:g * TT + n + 1])
                a.then_inc(ssq_ready, 1)
                act.wait_ge(ssq_ready, now)
                nc.scalar.activation(lnr[:, :], ssq[:, :], ACT.Ln, bias=eps[:, 0:1]).then_inc(lnr_ready, 1)
                act.wait_ge(lnr_ready, now)
                nc.scalar.activation(rr[:, :], lnr[:, :], ACT.Exp, scale=-0.5).then_inc(r_ready, 1)
                act.wait_ge(d_ready, now)
                act.wait_ge(lnrk_ready, now)
                for n in range(TT):
                    a = nc.scalar.activation(dd[:, n, :], dd[:, n, :], ACT.Exp, bias=coef[:, 5, n:n + 1])
                a.then_inc(decay_ready, 1)
                for i, (dst, bank) in enumerate([(kbT, 7), (qnT, 2), (qdT, 3)]):
                    act.wait_ge(back_psum[i], now)
                    nc.scalar.copy(dst[:, :, :], tiles(ps[bank])).then_inc(back_copied[i], 1)
                act.wait_ge(x_psum, now)
                nc.scalar.copy(X[:, :, :], tiles(ps[6])).then_inc(x_ready[0], 1)
                for l in range(1, LEVELS):
                    act.wait_ge(y_psum[l], now)
                    nc.scalar.copy(Y[:, :, :], tiles(ps[7])).then_inc(y_ready[l], 1)
                act.wait_ge(wt_psum, now)
                nc.scalar.mul(wTn[:, :, :], tiles(ps[4]), -1.0).then_inc(wt_ready, 1)
                for n in range(TT):
                    act.wait_ge(v_psum[n], now)
                    nc.scalar.copy(vn[:, n, :], ps[5][:, n * P:(n + 1) * P]).then_inc(v_ready[n], 1)
                act.wait_ge(o_psum, now)
                for n in range(TT):
                    a = nc.scalar.activation(sq[:, 2, n, :], ps[7][:, n * P:(n + 1) * P], ACT.Square,
                                             accum_out=osq[:, 0, n:n + 1])
                a.then_inc(osq_ready, 1)
                act.wait_ge(osq_ready, now)
                nc.scalar.activation(osq[:, 1, :], osq[:, 0, :], ACT.Ln, bias=eps[:, 1:2], scale=1.0 / P).then_inc(lno_ready, 1)
                act.wait_ge(lno_ready, now)
                nc.scalar.activation(osq[:, 2, :], osq[:, 1, :], ACT.Exp, scale=-0.5).then_inc(ro_ready, 1)
                if not last:
                    silus(h, now + 1, False)

            with act.Fori(0, HEADS - 1) as h:
                body(h, False)
            body(HEADS - 1, True)

        @block.vector
        def _(dve):
            def tap(g, k, head1):
                if k == 0:
                    dve.wait_ge(proj_done[g], head1)
                else:
                    dve.wait_ge(tap_done[g][k - 1], head1)
                w = cwh[:, (CONV - 1 - k) * 3 + g:(CONV - 1 - k) * 3 + g + 1]
                if k == 0:
                    nc.vector.tensor_scalar(ch[:, g, :], ps[g % 2][:, :], w, None, ALU.mult).then_inc(tap_done[g][0], 1)
                else:
                    nc.vector.scalar_tensor_tensor(out=ch[:, g, k:SEQ], in0=ps[g % 2][:, 0:SEQ - k], scalar=w,
                                                   in1=ch[:, g, k:SEQ], op0=ALU.mult, op1=ALU.add).then_inc(tap_done[g][k], 1)

            def take_taps(h, head1):
                nc.vector.tensor_copy(cwh[:, :], cw[:, :].rearrange("p (k h) -> p k h", h=HEADS)[:, :, h]).then_inc(cwh_ready, 1)
                dve.wait_ge(cwh_ready, head1)

            take_taps(0, 1)
            for g in range(3):
                for k in range(CONV):
                    tap(g, k, 1)

            def body(h, last):
                now = h + 1
                if h is not None and not last:
                    dve.wait_ge(tap_done[2][3], now)
                    take_taps(h + 1, now + 1)
                gate = lambda k: hc[:, k, :]
                nc.vector.tensor_copy(hc[:, :, :], GT[:, h, :, :]).then_inc(hc_ready, 1)
                dve.wait_ge(hc_ready, now)
                dve.wait_ge(gcrow_psum, now)
                for n in range(TT):
                    a = nc.vector.tensor_scalar(dd[:, n, :], ps[5][:, n * P:(n + 1) * P], hc[:, 0, n:n + 1], 0.0,
                                                ALU.subtract, ALU.min)
                a.then_inc(d_ready, 1)
                dve.wait_ge(r_ready, now)
                nc.vector.tensor_scalar(coef[:, 5, :], lnr[:, TT:2 * TT], -0.5, None, ALU.mult).then_inc(lnrk_ready, 1)
                nc.vector.tensor_tensor(coef[:, 0, :], rr[:, TT:2 * TT], gate(1), ALU.mult)
                nc.vector.tensor_tensor(coef[:, 2, :], rr[:, TT:2 * TT], gate(3), ALU.mult)
                nc.vector.tensor_scalar(coef[:, 3, :], rr[:, 0:TT], P ** -0.5, None, ALU.mult).then_inc(coef1, 1)
                dve.wait_ge(coef1, now)
                nc.vector.tensor_tensor(coef[:, 1, :], coef[:, 0, :], gate(2), ALU.mult)
                nc.vector.tensor_tensor(coef[:, 4, :], coef[:, 3, :], gate(2), ALU.mult).then_inc(coef2, 1)
                nc.vector.tensor_tensor(kb[:, :, :], tiles(ps[3]), per_tile(coef[:, 0, :]), ALU.mult).then_inc(k_scaled, 1)
                dve.wait_ge(coef2, now)
                nc.vector.tensor_tensor(kbe[:, :, :], tiles(ps[3]), per_tile(coef[:, 1, :]), ALU.mult)
                nc.vector.tensor_tensor(kd[:, :, :], tiles(ps[3]), per_tile(coef[:, 2, :]), ALU.mult).then_inc(kall_scaled, 1)
                nc.vector.tensor_tensor(qn[:, :, :], tiles(ps[2]), per_tile(coef[:, 3, :]), ALU.mult)
                nc.vector.tensor_tensor(qd[:, :, :], tiles(ps[2]), per_tile(coef[:, 4, :]), ALU.mult).then_inc(q_scaled, 1)
                dve.wait_ge(tok_psum[2], now)
                nc.vector.tensor_tensor(vb[:, :, :], tiles(ps[4]), per_tile(gate(1)), ALU.mult).then_inc(v_scaled, 1)
                dve.wait_ge(lt_psum, now)
                dve.wait_ge(decay_ready, now)
                nc.vector.tensor_tensor(LT[:, :, :], tiles(ps[4]), dd[:, :, :], ALU.mult).then_inc(lt_ready, 1)
                dve.wait_ge(qk_psum, now)
                nc.vector.tensor_tensor(QK[:, :, :], tiles(ps[5]), dd[:, :, :], ALU.mult).then_inc(qk_raw, 1)
                dve.wait_ge(loff_ready[0], now)
                nc.vector.tensor_tensor(XT[:, :, :], all_tiles(ident[:, :]), LO[:, 0, :, :], ALU.subtract).then_inc(xt_ready[0], 1)
                for l in range(1, LEVELS):
                    if l < LEVELS - 1:
                        dve.wait_ge(z_psum[l], now)
                        dve.wait_ge(x_ready[l - 1], now)
                        nc.vector.tensor_tensor(X[:, :, :], X[:, :, :], tiles(ps[2]), ALU.subtract).then_inc(x_ready[l], 1)
                    dve.wait_ge(zt_psum[l], now)
                    dve.wait_ge(xt_ready[l - 1], now)
                    nc.vector.tensor_tensor(XT[:, :, :], XT[:, :, :], tiles(ps[3]), ALU.subtract).then_inc(xt_ready[l], 1)
                    if not last and l in (1, 2):
                        tap(0, 2 * l - 2, now + 1)
                        tap(0, 2 * l - 1, now + 1)
                    if not last and l in (5, 6):
                        tap(1, 2 * l - 10, now + 1)
                        tap(1, 2 * l - 9, now + 1)
                for n in range(TT):
                    if n < TT - 1:
                        dve.wait_ge(s_psum[n], now)
                        if n == 0:
                            nc.vector.tensor_copy(St[:, 0, :], ps[6][:, 0:P]).then_inc(s_ready[0], 1)
                        else:
                            dve.wait_ge(s_ready[n - 1], now)
                            nc.vector.scalar_tensor_tensor(out=St[:, n % 2, :], in0=St[:, (n - 1) % 2, :],
                                                           scalar=hc[:, 4, n:n + 1], in1=ps[6][:, 0:P],
                                                           op0=ALU.mult, op1=ALU.add).then_inc(s_ready[n], 1)
                    if not last and n in (2, 3):
                        tap(2, 2 * n - 4, now + 1)
                        tap(2, 2 * n - 3, now + 1)
                dve.wait_ge(ro_ready, now)
                nc.vector.tensor_tensor(on[:, :, :], tiles(ps[7]), per_tile(osq[:, 2, :]), ALU.mult).then_inc(o_ready, 1)
                dve.wait_ge(ot_psum, now)
                dve.wait_ge(silu_done[3], now)
                nc.vector.scalar_tensor_tensor(out=dnT[:, h, :], in0=ps[6][:, :], scalar=T["dn_w"][:, 0:1], in1=zs[:, :],
                                               op0=ALU.mult, op1=ALU.mult).then_inc(dn_done, 1)

            with dve.Fori(0, HEADS - 1) as h:
                body(h, False)
            body(HEADS - 1, True)


def attention_phase(nc, mem, T, ps, w_in, rel_table, rel_scratch):
    S = mem.sem
    rel_in, rel_built, rel_out, bias_in, bias_ready = (S(n) for n in ("rel_in", "rel_built", "rel_out", "bias_in", "bias_ready"))
    aw_in = S("aw_in")
    av_in = S("av_in")
    av_psum = mem.sems("av_psum", TT)
    av_ready = mem.sems("av_ready", TT)
    pair_in = mem.sems("pair_in", 2)
    pair_psum = mem.sems("pair_psum", 2)
    pair_ready = mem.sems("pair_ready", 2)
    avh_ready = S("avh_ready")
    bp_ready = S("bp_ready")
    sc_psum = [mem.sems(f"sc_psum{e}_", TT) for e in range(2)]
    sc_ready = [mem.sems(f"sc_ready{e}_", TT) for e in range(2)]
    nm_ready = [mem.sems(f"nm_ready{e}_", TT) for e in range(2)]
    ex_ready = [mem.sems(f"ex_ready{e}_", TT) for e in range(2)]
    rs_ready = [mem.sems(f"rs_ready{e}_", TT) for e in range(2)]
    pr_ready = [mem.sems(f"pr_ready{e}_", TT) for e in range(2)]
    pt_psum = [mem.sems(f"pt_psum{e}_", TT) for e in range(2)]
    pt_ready = [mem.sems(f"pt_ready{e}_", TT) for e in range(2)]
    ao_psum = mem.sems("ao_psum", 2)
    ao_ready = mem.sems("ao_ready", 2)

    PAIRS = AHEADS // 2
    EXT = SEQ + P
    ident, xT, aoT = T["ident"], T["xT"], T["aoT"]
    w_av = mem.sb("w_av", [P, KC, AW])
    w_pair = mem.sb("w_pair", [P, 2, KC, P])
    av = mem.sb("av", [P, TT, AW])
    avh = mem.sb("av_pair", [P, TT, P])
    qkT = mem.sb("attn_qk", [P, 2, SEQ])
    tab = mem.sb("rel_tab", [AHEADS, 2 * CLIP + 1])
    ext = mem.sb("rel_ext", [AHEADS, EXT])
    bias = mem.sb("rel_bias", [P, AHEADS, SEQ])
    bias_pair = mem.sb("bias_pair", [P, 2, SEQ])
    sc = mem.sb("scores", [P, 2, TT, SEQ])
    small = mem.sb("softmax_small", [P, 4, 2 * TT])
    PT = mem.sb("weightsT", [P, 2, SEQ])
    tiles = lambda bank: bank[:, :].rearrange("p (n i) -> p n i", n=TT)
    cols = [AQ0, AK0]

    with nc.Block() as block:

        @block.sync
        def _(sp):
            sp.dma_start(w_av[:, :, :], w_in[:, AV0:GA0].rearrange("(c p) n -> p c n", p=P)).then_inc(av_in, 16)
            sp.dma_start(tab[:, :], rel_table).then_inc(rel_in, 16)

            def load(g, j):
                sp.dma_start(w_pair[:, g, :, :], w_in[:, bass.ds(cols[g] + j * P, P)].rearrange(
                    "(c p) n -> p c n", p=P)).then_inc(pair_in[g], 16)

            load(0, 0)
            load(1, 0)
            sp.wait_ge(rel_built, 2)
            sp.dma_start(rel_scratch[:, :], ext[:, :]).then_inc(rel_out, 16)
            sp.wait_ge(rel_out, 16)
            for h in range(AHEADS):
                window = bass.AP(tensor=rel_scratch.tensor, offset=h * EXT, ap=[[1, P], [1, SEQ]])
                sp.dma_start(bias[:, h, :], window).then_inc(bias_in, 16)
            with sp.Fori(1, PAIRS) as j:
                for g in range(2):
                    sp.wait_ge(pair_psum[g], j)
                    load(g, j)

        @block.gpsimd
        def _(pool):
            pool.wait_ge(bias_in, 16 * AHEADS)
            nc.gpsimd.memset(bias[0:ACHUNK, :, 0:ACHUNK], NEG).then_inc(bias_ready, 1)

            for t in range(TT):
                pool.wait_ge(av_ready[t], 1)
            pool.wait_ge(bias_ready, 1)
            nc.gpsimd.tensor_copy(bias_pair[:, :, :], bias[:, 0:2, :]).then_inc(bp_ready, 1)
            nc.gpsimd.tensor_copy(avh[:, :, :], av[:, :, 0:P]).then_inc(avh_ready, 1)
            with pool.Fori(1, PAIRS) as j:
                pool.wait_ge(sc_ready[1][TT - 1], j)
                nc.gpsimd.tensor_copy(bias_pair[:, :, :], bias[:, bass.ds(2 * j, 2), :]).then_inc(bp_ready, 1)
                pool.wait_ge(ao_psum[1], j)
                nc.gpsimd.tensor_copy(avh[:, :, :], av[:, :, bass.ds(j * P, P)]).then_inc(avh_ready, 1)

        @block.tensor
        def _(pe):
            def projection(g, c, pair1):
                if c == 0:
                    pe.wait_ge(pair_in[g], 16 * pair1)
                mm = nc.tensor.matmul(ps[g][:, :], w_pair[:, g, c, :], xT[:, c, :], start=(c == 0), stop=(c == KC - 1))
                if c == KC - 1:
                    mm.then_inc(pair_psum[g], 1)

            pe.wait_ge(av_in, 16)
            for t in range(TT):
                for c in range(KC):
                    mm = nc.tensor.matmul(ps[4 + t][:, :], xT[:, c, t * P:(t + 1) * P], w_av[:, c, :],
                                          start=(c == 0), stop=(c == KC - 1))
                mm.then_inc(av_psum[t], 1)
            for g in range(2):
                for c in range(KC):
                    projection(g, c, 1)

            def body(j, fillers):
                now = j + 1
                queue = [(g, c) for g in range(2) for c in range(KC)] if fillers else []

                def fill(n):
                    for _ in range(min(n, len(queue))):
                        g, c = queue.pop(0)
                        if c == 0:
                            pe.wait_ge(pair_ready[g], now)
                        projection(g, c, now + 1)

                for g in range(2):
                    pe.wait_ge(pair_ready[g], now)
                for e in range(2):
                    rows = slice(AD * e, AD * e + AD)
                    for n in range(TT):
                        if n >= 2:
                            pe.wait_ge(sc_ready[e][n - 2], now)
                        elif e:
                            pe.wait_ge(sc_ready[0][n + 2], now)
                        nc.tensor.matmul(ps[2 + n % 2][:, 0:(n + 1) * P], qkT[rows, 0, n * P:(n + 1) * P],
                                         qkT[rows, 1, 0:(n + 1) * P], start=True, stop=True).then_inc(sc_psum[e][n], 1)
                        fill(1)
                for e in range(2):
                    for kt in range(TT):
                        i = e * TT + kt
                        if i >= 2:
                            pe.wait_ge(pt_ready[(i - 2) // TT][(i - 2) % TT], now)
                        for n in range(kt, TT):
                            pe.wait_ge(pr_ready[e][n], now)
                            mm = nc.tensor.transpose(ps[4 + i % 2][:, n * P:(n + 1) * P], sc[:, e, n, kt * P:(kt + 1) * P],
                                                     ident[:, :])
                        mm.then_inc(pt_psum[e][kt], 1)
                        fill(1)
                        pe.wait_ge(pt_ready[e][kt], now)
                        if kt == 0:
                            if e == 0:
                                pe.wait_ge(avh_ready, now)
                        mm = nc.tensor.matmul(ps[6 + e][AD * e:AD * e + AD, kt * P:SEQ], avh[:, kt, AD * e:AD * e + AD],
                                              PT[:, i % 2, kt * P:SEQ], start=(kt == 0), stop=(kt == TT - 1))
                    mm.then_inc(ao_psum[e], 1)
                fill(32)

            for t in range(TT):
                pe.wait_ge(av_ready[t], 1)
            with pe.Fori(0, PAIRS - 1) as j:
                body(j, True)
            body(PAIRS - 1, False)

        @block.scalar
        def _(act):
            for t in range(0, TT, 2):
                act.wait_ge(av_psum[t], 1)
                nc.scalar.copy(av[:, t, :], ps[4 + t][:, :]).then_inc(av_ready[t], 1)

            def body(j):
                now = j + 1
                for g in range(2):
                    act.wait_ge(pair_psum[g], now)
                    if g == 0:
                        nc.scalar.mul(qkT[:, 0, :], ps[0][:, :], AD ** -0.5).then_inc(pair_ready[0], 1)
                    else:
                        nc.scalar.copy(qkT[:, 1, :], ps[1][:, :]).then_inc(pair_ready[1], 1)
                for e in range(2):
                    for n in range(TT):
                        act.wait_ge(nm_ready[e][n], now)
                        s = e * TT + n
                        nc.scalar.activation(sc[:, e, n, 0:(n + 1) * P], sc[:, e, n, 0:(n + 1) * P], ACT.Exp,
                                             bias=small[:, 1, s:s + 1],
                                             accum_out=small[:, 2, s:s + 1]).then_inc(ex_ready[e][n], 1)
                for e in range(2):
                    for kt in range(TT):
                        i = e * TT + kt
                        act.wait_ge(pt_psum[e][kt], now)
                        nc.scalar.copy(PT[:, i % 2, kt * P:SEQ], ps[4 + i % 2][:, kt * P:SEQ]).then_inc(pt_ready[e][kt], 1)
                    act.wait_ge(ao_psum[e], now)
                    nc.scalar.copy(aoT[AD * e:AD * e + AD, j, :], ps[6 + e][AD * e:AD * e + AD, :]).then_inc(ao_ready[e], 1)

            with act.Fori(0, PAIRS) as j:
                body(j)

        @block.vector
        def _(dve):
            for t in range(1, TT, 2):
                dve.wait_ge(av_psum[t], 1)
                nc.vector.tensor_copy(av[:, t, :], ps[4 + t][:, :]).then_inc(av_ready[t], 1)
            dve.wait_ge(rel_in, 16)
            n_tab = CLIP + P
            nc.vector.tensor_copy(ext[:, 0:n_tab], tab[:, 0:n_tab][:, ::-1]).then_inc(rel_built, 1)
            nc.vector.tensor_copy(ext[:, n_tab:EXT], tab[:, 0:1].broadcast_to([AHEADS, EXT - n_tab])).then_inc(rel_built, 1)

            def body(j):
                now = j + 1
                dve.wait_ge(bp_ready, now)
                for e in range(2):
                    for n in range(TT):
                        s = e * TT + n
                        L = (n + 1) * P
                        dve.wait_ge(sc_psum[e][n], now)
                        nc.vector.tensor_tensor(sc[:, e, n, 0:L], ps[2 + n % 2][:, 0:L], bias_pair[:, e, 0:L][:, ::-1],
                                                ALU.add).then_inc(sc_ready[e][n], 1)
                        dve.wait_ge(sc_ready[e][n], now)
                        nc.vector.tensor_reduce(small[:, 1, s:s + 1], sc[:, e, n, 0:L], AX.X, ALU.max,
                                                negate=True).then_inc(nm_ready[e][n], 1)
                for e in range(2):
                    for n in range(TT):
                        s = e * TT + n
                        L = (n + 1) * P
                        dve.wait_ge(ex_ready[e][n], now)
                        nc.vector.reciprocal(small[:, 3, s:s + 1], small[:, 2, s:s + 1]).then_inc(rs_ready[e][n], 1)
                        dve.wait_ge(rs_ready[e][n], now)
                        nc.vector.tensor_scalar(sc[:, e, n, 0:L], sc[:, e, n, 0:L], small[:, 3, s:s + 1], None,
                                                ALU.mult).then_inc(pr_ready[e][n], 1)

            with dve.Fori(0, PAIRS) as j:
                body(j)


def merge_phase(nc, mem, T, ps, w_in, w_a, w_b, w_out, ln_g, ln_b, x1_rows):
    w_in4 = [mem.sems(f"mw{p}_", 4) for p in range(2)]
    prod = [mem.sems(f"mprod{p}_", 4) for p in range(2)]
    sig_ready = [mem.sems(f"msig{p}_", 2) for p in range(2)]
    gated = [mem.sems(f"mgated{p}_", 2) for p in range(2)]
    merged = mem.sems("merged", 2)
    wo_in, ln_in = mem.sem("wo_in"), mem.sem("ln_in")
    mix_psum = mem.sems("mix_psum", TT)
    z_done = mem.sems("z_done", TT)
    st_done, ag_done, ln_ln, ln_rs, ln_n, ln_m, ln_done = (
        mem.sems(n, TT) for n in ("st_done", "ag_done", "ln_ln", "ln_rs", "ln_n", "ln_m", "ln_done"))
    x1_out = T["x1_out"]
    x1t_psum, x1t_ready = mem.sem("x1t_psum"), mem.sem("x1t_ready")

    xs, xT, dnT, aoT, ident, eps = T["x"], T["xT"], T["dnT"], T["aoT"], T["ident"], T["eps"]
    w_t = mem.sb("w_tile", [P, 2, 4, KC, P])
    sg = mem.sb("sig", [P, 2, 2, SEQ])
    mT = mem.sb("mergedT", [P, KC, SEQ])
    wo = mem.sb("wo", [P, KC, D])
    g_row, b_row = mem.sb("ln1_g_row", [P, D]), mem.sb("ln1_b_row", [P, D])
    stats = mem.sb("ln1_stats", [P, TT, 2, 6])
    mv = mem.sb("ln1_mv", [P, TT, 4])
    sources = [(w_in, GA0, KC), (w_a, 0, KC), (w_in, GB0, KC), (w_b, 0, AW // P)]
    moving = [xT, dnT, xT, aoT]
    HALF = D // 2

    with nc.Block() as block:

        @block.sync
        def _(sp):
            def load(p, k, start):
                src, at, n = sources[k]
                sp.dma_start(w_t[:, p, k, 0:n, :], src[:, at:at + D][:, bass.ds(start, P)].rearrange(
                    "(c p) n -> p c n", p=P)).then_inc(w_in4[p][k], 16)

            for p in range(2):
                for k in range(4):
                    load(p, k, p * P)
            with sp.Fori(1, KC // 2) as i:
                starts = [sp.snap((2 * i + p) * P) for p in range(2)]
                for p in range(2):
                    sp.wait_ge(prod[p][3], i)
                    for k in range(4):
                        load(p, k, starts[p])
            sp.dma_start(wo[:, :, :], w_out.rearrange("(c p) n -> p c n", p=P)).then_inc(wo_in, 16)
            sp.dma_start(g_row[:, :], ln_g.partition_broadcast(P)).then_inc(ln_in, 16)
            sp.dma_start(b_row[:, :], ln_b.partition_broadcast(P)).then_inc(ln_in, 16)
            for t in range(TT):
                sp.wait_ge(ln_done[t], 1)
                sp.dma_start(x1_rows[t * P:(t + 1) * P, :], xs[:, t, :]).then_inc(x1_out, 16)

        @block.tensor
        def _(pe):
            def body(i, first):
                for p in range(2):
                    for k in range(4):
                        n = sources[k][2]
                        pe.wait_ge(w_in4[p][k], 16 * (i + 1))
                        if not first:
                            pe.wait_ge(gated[p][k // 2] if k % 2 else sig_ready[p][k // 2], i)
                        for c in range(n):
                            mm = nc.tensor.matmul(ps[4 * p + k][:, :], w_t[:, p, k, c, :], moving[k][:, c, :],
                                                  start=(c == 0), stop=(c == n - 1))
                        mm.then_inc(prod[p][k], 1)

            body(0, True)
            with pe.Fori(1, KC // 2) as i:
                body(i, False)
            pe.wait_ge(wo_in, 16)
            for p in range(2):
                pe.wait_ge(merged[p], KC // 2)
            for t in range(TT):
                for half in range(2):
                    for c in range(KC):
                        mm = nc.tensor.matmul(ps[2 * t + half][:, :], mT[:, c, t * P:(t + 1) * P],
                                              wo[:, c, half * HALF:(half + 1) * HALF], start=(c == 0), stop=(c == KC - 1))
                mm.then_inc(mix_psum[t], 1)
            for c in range(KC):
                for t in range(TT):
                    if c == 0:
                        pe.wait_ge(ln_done[t], 1)
                    if c >= 4:
                        pe.wait_ge(x1t_ready, c - 3)
                    mm = nc.tensor.transpose(ps[c % 4][:, t * P:(t + 1) * P], xs[:, t, c * P:(c + 1) * P], ident[:, :])
                mm.then_inc(x1t_psum, 1)

        @block.scalar
        def _(act):
            def body(i):
                for p in range(2):
                    for k in range(2):
                        act.wait_ge(prod[p][2 * k], i + 1)
                        act.wait_ge(merged[p], i)
                        nc.scalar.activation(sg[:, p, k, :], ps[4 * p + 2 * k][:, :], ACT.Sigmoid).then_inc(sig_ready[p][k], 1)

            for p in range(2):
                for k in range(2):
                    act.wait_ge(prod[p][2 * k], 1)
                    nc.scalar.activation(sg[:, p, k, :], ps[4 * p + 2 * k][:, :], ACT.Sigmoid).then_inc(sig_ready[p][k], 1)
            with act.Fori(1, KC // 2) as i:
                body(i)
            for t in range(TT):
                act.wait_ge(ag_done[t], 1)
                nc.scalar.activation(mv[:, t, 2:3], mv[:, t, 1:2], ACT.Ln, bias=eps[:, 2:3]).then_inc(ln_ln[t], 1)
                act.wait_ge(ln_ln[t], 1)
                nc.scalar.activation(mv[:, t, 3:4], mv[:, t, 2:3], ACT.Exp, scale=-0.5).then_inc(ln_rs[t], 1)
            for c in range(KC):
                act.wait_ge(x1t_psum, c + 1)
                nc.scalar.copy(xT[:, c, :], ps[c % 4][:, :]).then_inc(x1t_ready, 1)

        @block.gpsimd
        def _(pool):
            pool.wait_ge(ln_in, 32)
            for t in range(TT):
                pool.wait_ge(ln_m[t], 1)
                nc.gpsimd.tensor_tensor(xs[:, t, :], xs[:, t, :], b_row[:, :], ALU.add).then_inc(ln_done[t], 1)

        @block.vector
        def _(dve):
            def body(i):
                for p in range(2):
                    for k in range(2):
                        dve.wait_ge(prod[p][2 * k + 1], i + 1)
                        dve.wait_ge(sig_ready[p][k], i + 1)
                        nc.vector.tensor_tensor(sg[:, p, k, :], sg[:, p, k, :], ps[4 * p + 2 * k + 1][:, :],
                                                ALU.mult).then_inc(gated[p][k], 1)
                    dve.wait_ge(gated[p][1], i + 1)
                    nc.vector.tensor_tensor(mT[:, 2 * i + p, :], sg[:, p, 0, :], sg[:, p, 1, :], ALU.add).then_inc(merged[p], 1)

            with dve.Fori(0, KC // 2) as i:
                body(i)
            for t in range(TT):
                dve.wait_ge(mix_psum[t], 1)
                for half in range(2):
                    at = slice(half * HALF, (half + 1) * HALF)
                    nc.vector.scalar_tensor_tensor(out=xs[:, t, at], in0=xs[:, t, at], scalar=ALPHA, in1=ps[2 * t + half][:, :],
                                                   op0=ALU.mult, op1=ALU.add).then_inc(z_done[t], 1)
                for half in range(2):
                    dve.wait_ge(z_done[t], half + 1)
                    nc.vector.bn_stats(stats[:, t, half, :], xs[:, t, half * HALF:(half + 1) * HALF]).then_inc(st_done[t], 1)
                dve.wait_ge(st_done[t], 2)
                nc.vector.bn_aggr(mv[:, t, 0:2], stats[:, t, :, :]).then_inc(ag_done[t], 1)
                if t == 0:
                    dve.wait_ge(ln_in, 32)
                dve.wait_ge(ln_rs[t], 1)
                nc.vector.tensor_scalar(xs[:, t, :], xs[:, t, :], mv[:, t, 0:1], mv[:, t, 3:4],
                                        ALU.subtract, ALU.mult).then_inc(ln_n[t], 1)
                dve.wait_ge(ln_n[t], 1)
                nc.vector.tensor_tensor(xs[:, t, :], xs[:, t, :], g_row[:, :], ALU.mult).then_inc(ln_m[t], 1)


def route_phase(nc, mem, T, ps, router_w, router_bias, ws_gu, ws_down):
    S = mem.sem
    r_in, s_in = S("r_in"), S("s_in")
    lg_psum, sc_done, bi_done = S("lg_psum"), S("sc_done"), S("bi_done")
    rt = S("rt")
    gs = S("gs")
    m_ready, pos_psum = S("m_ready"), S("pos_psum")
    vals_ready = S("vals_ready")
    ov_ready, ov_psum, ov_rows = S("ov_ready"), S("ov_psum"), S("ov_rows")
    sel_ready = mem.sems("sel_ready", 2)
    sel_used = mem.sems("sel_used", 2)
    sg_psum = mem.sems("sg_psum", 4)
    sg_act = mem.sems("sg_act", 2)
    sh_ready = mem.sems("sh_ready", 2)
    sd_psum = mem.sems("sd_psum", TT)
    sd_done = mem.sems("sd_done", TT)
    x1_out = T["x1_out"]

    xs, xT, ident, upper, ones = T["x"], T["xT"], T["ident"], T["upper"], T["ones"]
    wr = mem.sb("wr", [P, KC, NE])
    brow = mem.sb("brow", [P, NE])
    wg = mem.sb("ws_gu", [P, KC, 2 * ED])
    wd = mem.sb("ws_down", [P, ED // P, D])
    hT = mem.sb("shared_hT", [P, 2, SEQ])
    score = mem.sb("score", [P, TT, NE])
    biased = mem.sb("biased", [P, TT, NE])
    top = mem.sb("top", [P, TT, 8])
    topi = mem.sb("topi", [P, TT, 8], mybir.dt.uint32)
    topf = mem.sb("topf", [P, TT, 8])
    hot = mem.sb("hot", [P, TOPK, TT, NE])
    M = mem.sb("M", [P, TT, NE])
    kidx = mem.sb("kidx", [P, TT, NE])
    wsel = mem.sb("wsel", [P, TT, NE])
    wsum = mem.sb("wsum", [P, TT, 2])
    rest = mem.sb("rest", [P, TT, NE])
    strict = mem.sb("strict", [P, P])
    iota_e, place = mem.sb("iota_e", [P, NE]), mem.sb("place", [P, 3])
    slot = mem.sb("slot", [P, NBLK + 1, BLK])
    thr = mem.sb("thr", [P, NE, NBLK])
    e_of = mem.sb("e_of", [P, NE, NBLK])
    b_of = mem.sb("b_of", [P, NE, NBLK])
    over = mem.sb("over", [P, NE, NBLK])
    incl = mem.sb("incl", [P, NE, NBLK])
    hit = mem.sb("hit", [P, NE, NBLK])
    groups = mem.sb("groups", [P, MAXOVER // GROUP + 1])
    ov = mem.sb("ov", [P, 8])
    posm, vals, cnt = mem.sb("posm", [P, TT, NE]), mem.sb("vals", [P, TT, NE, 8], BF16), mem.sb("cnt", [P, NE])
    listed = mem.sb("listed", [P, LISTS, 8])
    work = mem.sb("list_work", [P, 3, LISTS])
    low = mem.sb("low", [BLK, LISTS, 8])
    twice = mem.sb("twice", [BLK, P])
    half_listed, listed_psum = S("half_listed"), S("listed_psum")
    blk_b = mem.sb("blk_b", [1, P], I32)
    blk_e, trips = T["blk_e"], T["trips"]
    tile_no = mem.sb("tile_no", [P, TT])
    sel = mem.sb("sel", [P, 2, TT, BLK], BF16)
    HALF = D // 2
    by_expert = lambda a: a.unsqueeze(1).broadcast_to([P, TT, NE])
    by_tile = lambda a: a.unsqueeze(2).broadcast_to([P, TT, NE])

    with nc.Block() as block:

        @block.sync
        def _(sp):
            sp.dma_start(wr[:, :, :], router_w.rearrange("(c p) n -> p c n", p=P)).then_inc(r_in, 16)
            sp.dma_start(brow[:, :], router_bias.partition_broadcast(P)).then_inc(r_in, 16)
            sp.dma_start(wg[:, :, :], ws_gu.rearrange("(c p) n -> p c n", p=P)).then_inc(s_in, 16)
            sp.dma_start(wd[:, :, :], ws_down.rearrange("(c p) n -> p c n", p=P)).then_inc(s_in, 16)
            for s in range(GROUP):
                T["load_expert"](sp, s, s)

        @block.gpsimd
        def _(pool):
            nc.gpsimd.iota(iota_e[:, :], pattern=[[1, NE]], base=0, channel_multiplier=0,
                           allow_small_or_imprecise_dtypes=True).then_inc(gs, 1)
            nc.gpsimd.iota(place[:, 0:1], pattern=[[0, 1]], base=0, channel_multiplier=1,
                           allow_small_or_imprecise_dtypes=True).then_inc(gs, 1)
            nc.gpsimd.iota(slot[:, :, :], pattern=[[BLK, NBLK + 1], [1, BLK]], base=0, channel_multiplier=0,
                           allow_small_or_imprecise_dtypes=True).then_inc(gs, 1)
            nc.gpsimd.iota(tile_no[:, :], pattern=[[1, TT]], base=0, channel_multiplier=0,
                           allow_small_or_imprecise_dtypes=True).then_inc(gs, 1)
            nc.gpsimd.tensor_tensor(strict[:, :], upper[:, :], ident[:, :], ALU.subtract).then_inc(gs, 1)
            for table, pattern in ((thr, [[0, NE], [BLK, NBLK]]), (e_of, [[1, NE], [0, NBLK]]),
                                   (b_of, [[0, NE], [1, NBLK]]), (groups, [[GROUP, MAXOVER // GROUP + 1]])):
                nc.gpsimd.iota(table[:], pattern=pattern, base=0, channel_multiplier=0,
                               allow_small_or_imprecise_dtypes=True).then_inc(gs, 1)

        @block.tensor
        def _(pe):
            pe.wait_ge(r_in, 32)
            for t in range(TT):
                for c in range(KC):
                    mm = nc.tensor.matmul(ps[0][:, t * NE:(t + 1) * NE], xT[:, c, t * P:(t + 1) * P], wr[:, c, :],
                                          start=(c == 0), stop=(c == KC - 1))
            mm.then_inc(lg_psum, 1)
            pe.wait_ge(s_in, 32)
            for g in range(4):
                for c in range(KC):
                    mm = nc.tensor.matmul(ps[2 + g][:, :], wg[:, c, g * P:(g + 1) * P], xT[:, c, :],
                                          start=(c == 0), stop=(c == KC - 1))
                mm.then_inc(sg_psum[g], 1)
            pe.wait_ge(m_ready, 1)
            pe.wait_ge(gs, 5)
            for t in range(TT):
                for u in range(t):
                    nc.tensor.matmul(ps[0][:, t * NE:(t + 1) * NE], ones[:, :], M[:, u, :], start=(u == 0), stop=False)
                nc.tensor.matmul(ps[0][:, t * NE:(t + 1) * NE], strict[:, :], M[:, t, :], start=(t == 0), stop=True)
            for u in range(TT):
                mm = nc.tensor.matmul(ps[0][:, TT * NE:(TT + 1) * NE], ones[:, :], M[:, u, :], start=(u == 0),
                                      stop=(u == TT - 1))
            mm.then_inc(pos_psum, 1)
            for t in range(TT):
                for half in range(2):
                    for k in range(2):
                        pe.wait_ge(sh_ready[k], 1)
                        if t > 0:
                            pe.wait_ge(sd_done[t - 1], 1 + half)
                        mm = nc.tensor.matmul(ps[6 + half][:, :], hT[:, k, t * P:(t + 1) * P],
                                              wd[:, k, half * HALF:(half + 1) * HALF], start=(k == 0), stop=(k == 1))
                    mm.then_inc(sd_psum[t], 1)
            pe.wait_ge(ov_ready, 1)
            nc.tensor.transpose(ps[3][0:1, 0:P], ov[:, 0:1], ident[:, :])
            nc.tensor.transpose(ps[3][0:1, P:2 * P], ov[:, 1:2], ident[:, :]).then_inc(ov_psum, 1)
            pe.wait_ge(vals_ready, 1)

            def lists(i, first):
                for q in range(2):
                    e = 2 * i + q
                    pe.wait_ge(sel_ready[q], i + 1)
                    for t in range(TT):
                        mm = nc.tensor.matmul(ps[1][0:BLK, bass.ds(8 * e, 8)], sel[:, q, t, :], vals[:, t, e, :],
                                              start=(t == 0), stop=(t == TT - 1))
                    mm.then_inc(sel_used[q], 1)

            with pe.Fori(0, NE // 2) as i:
                lists(i, False)
            pe.wait_ge(ov_rows, 1)
            turns = pe.value_load(trips[0:1, 1:2], min_val=1, max_val=MAXOVER // GROUP + 1)
            with pe.Fori(0, turns) as i:
                for k in range(GROUP):
                    q = k % 2
                    e = pe.value_load(blk_e[0:1, bass.ds(GROUP * i + (NE + k), 1)], min_val=0, max_val=NE - 1)
                    pe.wait_ge(sel_ready[q], 2 * i + (NE // 2 + k // 2 + 1))
                    for t in range(TT):
                        mm = nc.tensor.matmul(ps[2][0:BLK, bass.ds(8 * GROUP * i + 8 * k, 8)], sel[:, q, t, :],
                                              vals[:, t, bass.ds(e, 1), :], start=(t == 0), stop=(t == TT - 1))
                    mm.then_inc(sel_used[q], 1)
            pe.wait_ge(half_listed, 2)
            nc.tensor.matmul(ps[4][:, :], twice[:, :], low[:, 0:NE, :], start=True, stop=True)
            nc.tensor.matmul(ps[5][:, 0:8 * (LISTS - NE)], twice[:, :], low[:, NE:LISTS, :], start=True,
                             stop=True).then_inc(listed_psum, 1)

        @block.scalar
        def _(act):
            act.wait_ge(lg_psum, 1)
            nc.scalar.activation(score[:, :, :], ps[0][:, 0:TT * NE].rearrange("p (t n) -> p t n", n=NE),
                                 ACT.Sigmoid).then_inc(sc_done, 1)
            for k in range(2):
                act.wait_ge(sg_psum[k], 1)
                nc.scalar.activation(hT[:, k, :], ps[2 + k][:, :], ACT.Silu).then_inc(sg_act[k], 1)

        @block.vector
        def _(dve):
            step = [0]

            def then(instruction):
                step[0] += 1
                instruction.then_inc(rt, 1)
                dve.wait_ge(rt, step[0])

            dve.wait_ge(sc_done, 1)
            dve.wait_ge(r_in, 32)
            then(nc.vector.tensor_tensor(biased[:, :, :], score[:, :, :], by_expert(brow[:, :]), ALU.add))
            for t in range(TT):
                last = nc.vector.max(top[:, t, :], biased[:, t, :])
            then(last)
            for t in range(TT):
                last = nc.vector.max_index(topi[:, t, :], top[:, t, :], biased[:, t, :])
            then(last)
            then(nc.vector.tensor_copy(topf[:, :, :], topi[:, :, :]))
            dve.wait_ge(gs, 9)
            nc.vector.tensor_scalar(place[:, 1:2], place[:, 0:1], 1.0, None, ALU.add)
            nc.vector.tensor_scalar(place[:, 2:3], place[:, 0:1], float(BLK), None, ALU.is_ge)
            nc.vector.memset(ov[:, :], 0.0)
            for h in range(2):
                nc.vector.tensor_copy(twice[:, h * BLK:(h + 1) * BLK], ident[0:BLK, 0:BLK])
            for k in range(TOPK):
                last = nc.vector.tensor_tensor(hot[:, k, :, :], by_expert(iota_e[:, :]), by_tile(topf[:, :, k]), ALU.is_equal)
            then(last)
            then(nc.vector.tensor_tensor(M[:, :, :], hot[:, 0, :, :], hot[:, 1, :, :], ALU.add))
            for k in range(2, TOPK):
                last = nc.vector.tensor_tensor(M[:, :, :], M[:, :, :], hot[:, k, :, :], ALU.add)
                if k < TOPK - 1:
                    then(last)
            last.then_inc(m_ready, 1)
            flat = lambda a: a.rearrange("p t n -> p (t n)")
            then(nc.vector.scalar_tensor_tensor(out=flat(kidx[:, :, :]), in0=flat(hot[:, 2, :, :]), scalar=2.0,
                                                in1=flat(hot[:, 1, :, :]), op0=ALU.mult, op1=ALU.add))
            for k in range(3, TOPK):
                then(nc.vector.scalar_tensor_tensor(out=flat(kidx[:, :, :]), in0=flat(hot[:, k, :, :]), scalar=float(k),
                                                    in1=flat(kidx[:, :, :]), op0=ALU.mult, op1=ALU.add))
            dve.wait_ge(m_ready, 1)
            then(nc.vector.tensor_tensor(wsel[:, :, :], score[:, :, :], M[:, :, :], ALU.mult))
            then(nc.vector.tensor_reduce(wsum[:, :, 0], wsel[:, :, :], AX.X, ALU.add))
            then(nc.vector.reciprocal(wsum[:, :, 1], wsum[:, :, 0]))
            then(nc.vector.tensor_scalar(wsum[:, :, 0], wsum[:, :, 1], ROUTED_SCALE, None, ALU.mult))
            then(nc.vector.tensor_tensor(wsel[:, :, :], wsel[:, :, :], by_tile(wsum[:, :, 0]), ALU.mult))
            nc.vector.tensor_copy(vals[:, :, :, 0], by_tile(tile_no[:, :]))
            nc.vector.tensor_copy(vals[:, :, :, 1], place[:, 0:1].unsqueeze(2).broadcast_to([P, TT, NE]))
            nc.vector.tensor_copy(vals[:, :, :, 2], kidx[:, :, :])
            nc.vector.memset(vals[:, :, :, 3], 1.0)
            nc.vector.memset(vals[:, :, :, 7], 0.0)
            then(nc.vector.tensor_copy(vals[:, :, :, 4], wsel[:, :, :]))
            then(nc.vector.tensor_tensor(rest[:, :, :], wsel[:, :, :], vals[:, :, :, 4], ALU.subtract))
            then(nc.vector.tensor_copy(vals[:, :, :, 5], rest[:, :, :]))
            then(nc.vector.tensor_tensor(rest[:, :, :], rest[:, :, :], vals[:, :, :, 5], ALU.subtract))
            nc.vector.tensor_copy(vals[:, :, :, 6], rest[:, :, :]).then_inc(vals_ready, 1)
            dve.wait_ge(pos_psum, 1)
            pos = ps[0][:, 0:TT * NE].rearrange("p (t n) -> p t n", n=NE)
            nc.vector.tensor_copy(cnt[:, :], ps[0][:, TT * NE:(TT + 1) * NE])
            then(nc.vector.scalar_tensor_tensor(out=posm[:, :, :].rearrange("p t n -> p (t n)"), in0=ps[0][:, 0:TT * NE],
                                                scalar=1.0, in1=flat(M[:, :, :]), op0=ALU.add, op1=ALU.mult))
            then(nc.vector.tensor_scalar(posm[:, :, :], posm[:, :, :], -1.0, None, ALU.add))
            wide = lambda a: a.unsqueeze(2).broadcast_to([P, NE, NBLK])
            line = lambda a: a.rearrange("p e b -> p (e b)")
            then(nc.vector.tensor_tensor(over[:, :, :], wide(cnt[:, :]), thr[:, :, :], ALU.is_gt))
            then(nc.vector.memset(over[:, :, 0], 0.0))
            then(nc.vector.memset(hit[:, :, :], 1.0))
            then(nc.vector.tensor_tensor_scan(line(incl[:, :, :]), line(hit[:, :, :]), line(over[:, :, :]), 0.0,
                                              ALU.mult, ALU.add))
            then(nc.vector.tensor_tensor(over[:, :, :], over[:, :, :], incl[:, :, :], ALU.mult))
            then(nc.vector.tensor_scalar(hit[:, :, :], over[:, :, :], place[:, 1:2], None, ALU.is_equal))
            then(nc.vector.tensor_tensor(over[:, :, :], hit[:, :, :], e_of[:, :, :], ALU.mult))
            then(nc.vector.tensor_reduce(ov[:, 0:1], line(over[:, :, :]), AX.X, ALU.add))
            then(nc.vector.tensor_tensor(over[:, :, :], hit[:, :, :], b_of[:, :, :], ALU.mult))
            then(nc.vector.tensor_reduce(ov[:, 2:3], line(over[:, :, :]), AX.X, ALU.add))
            then(nc.vector.tensor_reduce(ov[:, 3:4], line(hit[:, :, :]), AX.X, ALU.add))
            then(nc.vector.tensor_scalar(ov[:, 3:4], ov[:, 3:4], -float(NBLK), float(NBLK), ALU.mult, ALU.add))
            nc.vector.tensor_tensor(ov[:, 1:2], ov[:, 2:3], ov[:, 3:4], ALU.add).then_inc(ov_ready, 1)
            then(nc.vector.tensor_scalar(groups[:, :], groups[:, :], incl[:, NE - 1, NBLK - 1:NBLK], None, ALU.is_lt))
            then(nc.vector.tensor_reduce(ov[:, 4:5], groups[:, :], AX.X, ALU.add))
            then(nc.vector.tensor_scalar(ov[:, 5:6], ov[:, 4:5], 1.0, None, ALU.max))
            then(nc.vector.tensor_scalar(trips[:, 0:1], ov[0:1, 4:5], float(NE // GROUP), None, ALU.add))
            then(nc.vector.tensor_copy(trips[:, 1:2], ov[0:1, 5:6]))
            then(nc.vector.tensor_scalar(trips[:, 2:3], ov[0:1, 4:5], float(NE // GROUP - 1), None, ALU.add))
            for k in range(2):
                dve.wait_ge(sg_act[k], 1)
                dve.wait_ge(sg_psum[2 + k], 1)
                nc.vector.tensor_tensor(hT[:, k, :], hT[:, k, :], ps[4 + k][:, :], ALU.mult).then_inc(sh_ready[k], 1)
            for t in range(TT):
                for half in range(2):
                    at = slice(half * HALF, (half + 1) * HALF)
                    dve.wait_ge(sd_psum[t], half + 1)
                    if t == 0 and half == 0:
                        dve.wait_ge(x1_out, 16 * TT)
                    nc.vector.scalar_tensor_tensor(out=xs[:, t, at], in0=xs[:, t, at], scalar=ALPHA, in1=ps[6 + half][:, :],
                                                   op0=ALU.mult, op1=ALU.add).then_inc(sd_done[t], 1)
            dve.wait_ge(ov_psum, 1)
            then(nc.vector.tensor_copy(blk_e[:, 0:NE], iota_e[0:1, :]))
            then(nc.vector.tensor_copy(blk_e[:, NE:LISTS], ps[3][0:1, 0:LISTS - NE]))
            nc.vector.tensor_copy(blk_b[:, :], ps[3][0:1, P:2 * P]).then_inc(ov_rows, 1)

            def select(q, row, where):
                nc.vector.tensor_tensor(sel[:, q, :, :], row.broadcast_to([P, TT, BLK]), where.broadcast_to([P, TT, BLK]),
                                        ALU.is_equal).then_inc(sel_ready[q], 1)

            def first_block(i, q):
                select(q, slot[:, 0:1, :], posm[:, :, bass.ds(2 * i + q, 1)])

            for q in range(2):
                first_block(0, q)
            with dve.Fori(1, NE // 2) as i:
                for q in range(2):
                    dve.wait_ge(sel_used[q], i)
                    first_block(i, q)
            dve.wait_ge(ov_rows, 1)
            turns = dve.value_load(trips[0:1, 1:2], min_val=1, max_val=MAXOVER // GROUP + 1)

            def later(i, k):
                e = dve.value_load(blk_e[0:1, bass.ds(GROUP * i + (NE + k), 1)], min_val=0, max_val=NE - 1)
                b = dve.value_load(blk_b[0:1, bass.ds(GROUP * i + k, 1)], min_val=0, max_val=NBLK)
                select(k % 2, slot[:, bass.ds(b, 1), :], posm[:, :, bass.ds(e, 1)])

            with dve.Fori(0, turns) as i:
                for k in range(GROUP):
                    dve.wait_ge(sel_used[k % 2], 2 * i + (NE // 2 + k // 2))
                    later(i, k)
            for q in range(2):
                dve.wait_ge(sel_used[q], 2 * turns + NE // 2)
            by_block = lambda bank, n: bank[:, 0:8 * n].rearrange("p (e v) -> p e v", v=8)
            nc.vector.tensor_copy(low[:, 0:NE, :], by_block(ps[1][0:BLK, :], NE)).then_inc(half_listed, 1)
            nc.vector.tensor_copy(low[:, NE:LISTS, :], by_block(ps[2][0:BLK, :], LISTS - NE)).then_inc(half_listed, 1)
            dve.wait_ge(listed_psum, 1)
            nc.vector.tensor_copy(listed[:, 0:NE, :], by_block(ps[4], NE))
            then(nc.vector.tensor_copy(listed[:, NE:LISTS, :], by_block(ps[5], LISTS - NE)))
            col = lambda k: listed[:, :, k]
            then(nc.vector.scalar_tensor_tensor(out=work[:, 0, :], in0=col(0), scalar=float(P), in1=col(1),
                                                op0=ALU.mult, op1=ALU.add))
            then(nc.vector.tensor_scalar(work[:, 1, :], col(3), -OOB, OOB, ALU.mult, ALU.add))
            then(nc.vector.tensor_scalar(work[:, 2, :], col(2), 2.0, place[:, 2:3], ALU.mult, ALU.add))
            then(nc.vector.scalar_tensor_tensor(out=work[:, 2, :], in0=work[:, 0, :], scalar=2.0 * TOPK,
                                                in1=work[:, 2, :], op0=ALU.mult, op1=ALU.add))
            for a in range(2):
                part, every = slice(a * BLK, (a + 1) * BLK), bass.ds(a, LISTS // 2, 2)
                nc.vector.tensor_tensor(T["tok_idx"][part, :], work[part, 0, every], work[part, 1, every], ALU.add)
            nc.vector.tensor_tensor(T["row_idx"][:, :], work[:, 2, :], work[:, 1, :], ALU.add)
            then(nc.vector.tensor_tensor(T["slot_w"][:, :], col(4), col(5), ALU.add))
            nc.vector.tensor_tensor(T["slot_w"][:, :], T["slot_w"][:, :], col(6), ALU.add)


def experts_phase(nc, mem, T, ps, w_gu, w_down, x1_rows, y_rows):
    PAIRS = GROUP // 2
    gu_in, dn_in = T["gu_in"], T["dn_in"]
    first_col = mem.sems("first_col", PAIRS)
    col_ready = mem.sems("col_ready", PAIRS)
    gathered = mem.sems("gathered", PAIRS)
    xt_psum = mem.sems("ext_psum", GROUP)
    xt_ready = mem.sems("ext_ready", GROUP)
    gu_psum = mem.sems("gu_psum", GROUP)
    gate_ready = mem.sems("gate_ready", GROUP)
    h_ready = mem.sems("h_ready", GROUP)
    h_psum = mem.sems("h_psum", GROUP)
    ht_ready = mem.sems("ht_ready", GROUP)
    y_psum = mem.sems("ey_psum", GROUP)
    y_ready = mem.sems("ey_ready", GROUP)
    col2_ready = mem.sems("col2_ready", GROUP)
    scattered = mem.sems("scattered", GROUP)
    blank = mem.sem("blank")

    ident, wgu, wdn = T["ident"], T["wgu"], T["wdn"]
    blk_e, trips, tok_idx, row_idx, slot_w = T["blk_e"], T["trips"], T["tok_idx"], T["row_idx"], T["slot_w"]
    x1_out = T["x1_out"]
    xg = mem.sb("gathered_x", [P, PAIRS, D])
    xgT = mem.sb("gathered_xT", [P, PAIRS, KC, P])
    gate = mem.sb("gate", [P, 2, P])
    h = mem.sb("hidden", [P, 2, P])
    hT = mem.sb("hiddenT", [P, 2, P])
    y = mem.sb("expert_y", [P, GROUP, D // 2])
    col = mem.sb("tok_col", [P, PAIRS], I32)
    col2 = mem.sb("row_col", [P, GROUP], I32)
    MAXTURNS = LISTS // GROUP
    parts = [slice(0, BLK), slice(BLK, P)]

    def block_at(i, s):
        return s % GROUP, i + (s // GROUP + 1)

    with nc.Block() as block:

        @block.sync
        def _(sp):
            turns = sp.value_load(trips[0:1, 0:1], min_val=NE // GROUP, max_val=MAXTURNS)
            with sp.Fori(1, turns) as i:
                for s in range(GROUP):
                    e = sp.value_load(blk_e[0:1, bass.ds(GROUP * i + s, 1)], min_val=0, max_val=NE - 1)
                    T["load_expert"](sp, s, e, lambda: sp.wait_ge(gu_psum[s], i), lambda: sp.wait_ge(y_psum[s], i))

        @block.gpsimd
        def _(pool):
            nc.gpsimd.memset(xg[:, :, :], 0.0).then_inc(blank, 1)
            pool.wait_ge(blank, 1)
            last_token, last_row = pool.to_reg(SEQ - 1), pool.to_reg(2 * SEQ * TOPK - 1)
            last_turn = pool.value_load(trips[0:1, 2:3], min_val=NE // GROUP - 1, max_val=MAXTURNS - 1)

            def gather(i, q, first=False):
                if not first:
                    for a in range(2):
                        pool.wait_ge(xt_psum[2 * q + a], i)
                copied = first_col[q] if first else col_ready[q]
                nc.gpsimd.tensor_copy(col[:, q:q + 1], tok_idx[:, bass.ds(PAIRS * i + q, 1)]).then_inc(copied, 1)
                pool.wait_ge(x1_out, 16 * TT)
                pool.wait_ge(copied, 1 if first else i)
                nc.gpsimd.indirect_dma_start(
                    out=xg[:, q, :], out_offset=None, in_=x1_rows[:, :],
                    in_offset=bass.IndirectOffsetOnAxis(ap=col[:, q:q + 1], axis=0),
                    bounds_check=last_token, oob_is_err=False).then_inc(gathered[q], 16)

            def scatter(i, s):
                k, now = block_at(i, s)
                pool.wait_ge(y_ready[k], now)
                nc.gpsimd.tensor_copy(col2[:, k:k + 1], row_idx[:, bass.ds(GROUP * i + s, 1)]).then_inc(col2_ready[k], 1)
                pool.wait_ge(blank, 1)
                pool.wait_ge(col2_ready[k], now)
                nc.gpsimd.indirect_dma_start(
                    out=y_rows[:, :], out_offset=bass.IndirectOffsetOnAxis(ap=col2[:, k:k + 1], axis=0),
                    in_=y[:, k, :], in_offset=None,
                    bounds_check=last_row, oob_is_err=False).then_inc(scattered[k], 16)

            def turn(i, first=False, last=False):
                for s in range(GROUP):
                    if not (first and s == 0):
                        scatter(i, s - 1)
                    if s % 2 == 0 and not last:
                        gather(i + 1, s // 2)

            for q in range(PAIRS):
                gather(0, q, True)
            turn(0, first=True)
            with pool.Fori(1, last_turn) as i:
                turn(i)
            turn(last_turn, last=True)
            scatter(last_turn, GROUP - 1)
            for k in range(GROUP):
                pool.wait_ge(scattered[k], 16 * (last_turn + 1))

        @block.tensor
        def _(pe):
            last_turn = pe.value_load(trips[0:1, 2:3], min_val=NE // GROUP - 1, max_val=MAXTURNS - 1)

            def transposes(i, q, a, first=False):
                pe.wait_ge(gathered[q], 16 * i + 16)
                if not first:
                    before, then_ = (q - 1) % PAIRS, i + (q - 1) // PAIRS + 1
                    pe.wait_ge(xt_ready[2 * before + a], then_)
                for c in range(KC // 2):
                    chunk = a * KC // 2 + c
                    mm = nc.tensor.transpose(ps[2 + a][:, c * P:(c + 1) * P], xg[:, q, chunk * P:(chunk + 1) * P], ident[:, :])
                mm.then_inc(xt_psum[2 * q + a], 1)

            def gate_up(i, s, first=False):
                k, now = block_at(i, s)
                pe.wait_ge(gu_in[k], 16 * now)
                if s % 2 == 0:
                    for a in range(2):
                        pe.wait_ge(xt_ready[s + a], now)
                if not first:
                    before, then_ = block_at(i, s - 2)
                    pe.wait_ge(h_ready[before], then_)
                for c in range(KC):
                    halves = wgu[:, k, c, :].rearrange("p (g a n) -> p a g n", g=2, a=2)
                    for a in range(2):
                        mm = nc.tensor.matmul(ps[k % 2][parts[a], 0:2 * P], xgT[:, s // 2, c, parts[s % 2]], halves[:, a, :, :],
                                              start=(c == 0), stop=(c == KC - 1))
                mm.then_inc(gu_psum[k], 1)

            def hidden(i, s, first=False):
                k, now = block_at(i, s)
                pe.wait_ge(h_ready[k], now)
                nc.tensor.transpose(ps[4 + k % 2][:, 0:P], h[:, k % 2, :], ident[:, :]).then_inc(h_psum[k], 1)

            def down(i, s, first=False):
                k, now = block_at(i, s)
                pe.wait_ge(dn_in[k], 16 * now)
                pe.wait_ge(ht_ready[k], now)
                if not first:
                    before, then_ = block_at(i, s - 2)
                    pe.wait_ge(y_ready[before], then_)
                for c in range(2):
                    for a in range(2):
                        mm = nc.tensor.matmul(ps[6 + k % 2][parts[a], :], hT[:, k % 2, c * BLK:(c + 1) * BLK],
                                              wdn[:, k, c, a * (D // 2):(a + 1) * (D // 2)], start=(c == 0), stop=(c == 1))
                mm.then_inc(y_psum[k], 1)

            def turn(i, first=False, last=False):
                for s in range(GROUP):
                    gate_up(i, s, first and s < 2)
                    if not (last and s >= GROUP - 2):
                        q = s // 2 + 1
                        transposes(i + q // PAIRS, q % PAIRS, s % 2)
                    if not (first and s == 0):
                        down(i, s - 1, first and s < 3)
                    hidden(i, s, first and s < 2)

            for a in range(2):
                transposes(0, 0, a, True)
            turn(0, first=True)
            with pe.Fori(1, last_turn) as i:
                turn(i)
            turn(last_turn, last=True)
            down(last_turn, GROUP - 1)

        @block.scalar
        def _(act):
            last_turn = act.value_load(trips[0:1, 2:3], min_val=NE // GROUP - 1, max_val=MAXTURNS - 1)

            def copy_hidden(i, s):
                k, now = block_at(i, s)
                act.wait_ge(h_psum[k], now)
                nc.scalar.copy(hT[:, k % 2, :], ps[4 + k % 2][:, 0:P]).then_inc(ht_ready[k], 1)

            def turn(i, first=False, unused=False):
                for s in range(GROUP):
                    k, now = block_at(i, s)
                    act.wait_ge(gu_psum[k], now)
                    nc.scalar.activation(gate[:, k % 2, :], ps[k % 2][:, 0:P], ACT.Silu).then_inc(gate_ready[k], 1)
                    if not (first and s == 0):
                        b, then_ = block_at(i, s - 1)
                        act.wait_ge(y_psum[b], then_)
                        if not (first or unused and s == 0):
                            act.wait_ge(scattered[b], 16 * (then_ - 1))
                        nc.scalar.copy(y[:, b, :], ps[6 + b % 2][:, :]).then_inc(y_ready[b], 1)
                    copy_hidden(i, s)

            turn(0, first=True)
            turn(1, unused=True)
            with act.Fori(2, last_turn + 1) as i:
                turn(i)
            b, then_ = block_at(last_turn, GROUP - 1)
            act.wait_ge(y_psum[b], then_)
            act.wait_ge(scattered[b], 16 * (then_ - 1))
            nc.scalar.copy(y[:, b, :], ps[6 + b % 2][:, :]).then_inc(y_ready[b], 1)

        @block.vector
        def _(dve):
            last_turn = dve.value_load(trips[0:1, 2:3], min_val=NE // GROUP - 1, max_val=MAXTURNS - 1)

            def copy_x(i, q, a):
                dve.wait_ge(xt_psum[2 * q + a], i + 1)
                nc.vector.tensor_copy(xgT[:, q, a * KC // 2:(a + 1) * KC // 2, :],
                                      ps[2 + a][:, :].rearrange("p (c n) -> p c n", n=P)).then_inc(xt_ready[2 * q + a], 1)

            def turn(i, last=False):
                for s in range(GROUP):
                    k, now = block_at(i, s)
                    dve.wait_ge(gate_ready[k], now)
                    nc.vector.scalar_tensor_tensor(out=h[:, k % 2, :], in0=gate[:, k % 2, :],
                                                   scalar=slot_w[:, bass.ds(GROUP * i + s, 1)], in1=ps[k % 2][:, P:2 * P],
                                                   op0=ALU.mult, op1=ALU.mult).then_inc(h_ready[k], 1)
                    if not (last and s >= GROUP - 2):
                        q = s // 2 + 1
                        copy_x(i + q // PAIRS, q % PAIRS, s % 2)

            for a in range(2):
                copy_x(0, 0, a)
            with dve.Fori(0, last_turn) as i:
                turn(i)
            turn(last_turn, last=True)


def final_phase(nc, mem, T, ps, ln_g, ln_b, y_rows, out):
    y_in, s_done, pair_done, s2_done = (mem.sems(n, TT) for n in ("y_in", "s_done", "pair_done", "s2_done"))
    ln_in = mem.sem("fln_in")
    st_done, ag_done, ln_ln, ln_rs, ln_n, ln_m, ln_done, out_done = (
        mem.sems(n, TT) for n in ("fst", "fag", "fll", "frs", "fln", "flm", "fld", "out_done"))
    xs, eps = T["x"], T["eps"]
    yt = mem.sb("choices", [P, TT, TOPK, D])
    g_row, b_row = mem.sb("ln2_g_row", [P, D]), mem.sb("ln2_b_row", [P, D])
    stats = mem.sb("ln2_stats", [P, TT, 2, 6])
    mv = mem.sb("ln2_mv", [P, TT, 4])
    rows = y_rows.rearrange("(t p r) c -> t p (r c)", t=TT, p=P)

    with nc.Block() as block:

        @block.sync
        def _(sp):
            for t in range(TT):
                sp.dma_start(yt[:, t, :, :], rows[t]).then_inc(y_in[t], 16)
            for t in range(TT):
                sp.wait_ge(ln_done[t], 1)
                sp.dma_start(out[0, t * P:(t + 1) * P, :], xs[:, t, :]).then_inc(out_done[t], 16)
            for t in range(TT):
                sp.wait_ge(out_done[t], 16)

        @block.scalar
        def _(act):
            act.dma_start(g_row[:, :], ln_g.partition_broadcast(P)).then_inc(ln_in, 16)
            act.dma_start(b_row[:, :], ln_b.partition_broadcast(P)).then_inc(ln_in, 16)
            for t in range(TT):
                act.wait_ge(ag_done[t], 1)
                nc.scalar.activation(mv[:, t, 2:3], mv[:, t, 1:2], ACT.Ln, bias=eps[:, 2:3]).then_inc(ln_ln[t], 1)
                act.wait_ge(ln_ln[t], 1)
                nc.scalar.activation(mv[:, t, 3:4], mv[:, t, 2:3], ACT.Exp, scale=-0.5).then_inc(ln_rs[t], 1)

        @block.gpsimd
        def _(pool):
            for t in range(TT):
                pool.wait_ge(y_in[t], 16)
                nc.gpsimd.tensor_tensor(yt[:, t, 4, :], yt[:, t, 4, :], yt[:, t, 5, :], ALU.add).then_inc(pair_done[t], 1)
            pool.wait_ge(ln_in, 32)
            for t in range(TT):
                pool.wait_ge(ln_m[t], 1)
                nc.gpsimd.tensor_tensor(xs[:, t, :], xs[:, t, :], b_row[:, :], ALU.add).then_inc(ln_done[t], 1)

        @block.vector
        def _(dve):
            HALF = D // 2
            for t in range(TT):
                dve.wait_ge(y_in[t], 16)
                for k in range(5):
                    if k == 4:
                        dve.wait_ge(pair_done[t], 1)
                    if k:
                        dve.wait_ge(s_done[t], k)
                    nc.vector.tensor_tensor(xs[:, t, :], xs[:, t, :], yt[:, t, k, :], ALU.add).then_inc(s_done[t], 1)
                dve.wait_ge(s_done[t], 5)
                for half in range(2):
                    nc.vector.bn_stats(stats[:, t, half, :], xs[:, t, half * HALF:(half + 1) * HALF]).then_inc(st_done[t], 1)
                dve.wait_ge(st_done[t], 2)
                nc.vector.bn_aggr(mv[:, t, 0:2], stats[:, t, :, :]).then_inc(ag_done[t], 1)
                if t == 0:
                    dve.wait_ge(ln_in, 32)
                dve.wait_ge(ln_rs[t], 1)
                nc.vector.tensor_scalar(xs[:, t, :], xs[:, t, :], mv[:, t, 0:1], mv[:, t, 3:4],
                                        ALU.subtract, ALU.mult).then_inc(ln_n[t], 1)
                dve.wait_ge(ln_n[t], 1)
                nc.vector.tensor_tensor(xs[:, t, :], xs[:, t, :], g_row[:, :], ALU.mult).then_inc(ln_m[t], 1)


def program(nc, x, w_in, conv_w, a_log, dt_bias, dn_norm_w, rel_table, w_branch_a, w_branch_b, w_out, ln1_g, ln1_b,
            router_w, router_bias, expert_w_gate_up, expert_w_down, shared_w_gate_up, shared_w_down, ln2_g, ln2_b,
            out):
    with ExitStack() as ctx:
        mem = Memory(nc, ctx)
        ps = [ctx.enter_context(nc.psum_tensor(f"bank{i}", [P, 512], F32)) for i in range(8)]
        branches = ctx.enter_context(ExitStack())
        front = Memory(nc, branches)
        T = {
            "ident": mem.sb("ident", [P, P]),
            "upper": mem.sb("upper", [P, P]),
            "ones": mem.sb("ones", [P, P]),
            "eps": mem.sb("eps", [P, 3]),
            "x": mem.sb("x_rows", [P, TT, D]),
            "xT": mem.sb("xT", [P, KC, SEQ]),
            "masks": front.sb("masks", [P, LEVELS, P]),
            "GT": front.sb("gate_table", [P, HEADS, 6, TT]),
            "gate_work": front.sb("gate_work", [P, 6, HEADS * TT]),
            "bias_row": front.sb("bias_row", [P, 3 * HEADS]),
            "w_ba": front.sb("w_ba", [P, KC, 2 * HEADS]),
            "ba": front.sb("ba", [P, TT * 2 * HEADS]),
            "cw_rows": front.sb("cw_rows", [CONV * 3 * HEADS, P]),
            "cw": front.sb("cw", [P, CONV * 3 * HEADS]),
            "dn_w": front.sb("dn_w", [P, 1]),
            "dnT": front.sb("dnT", [P, HEADS, SEQ]),
            "aoT": front.sb("aoT", [P, AHEADS // 2, SEQ]),
        }
        w_in, conv_w, rel_table = w_in[0], conv_w[0], rel_table[0]
        rel_scratch = nc.dram_tensor("rel_scratch", [AHEADS, SEQ + P], F32, kind="Internal").ap()
        x1_rows = nc.dram_tensor("x1_rows", [SEQ, D], F32, kind="Internal").ap()
        run_phase(nc, setup_phase, T, ps, x, w_in, conv_w, a_log, dt_bias, dn_norm_w)
        run_phase(nc, delta_phase, T, ps, w_in)
        run_phase(nc, attention_phase, T, ps, w_in, rel_table, rel_scratch)
        T["x1_out"] = mem.sem("x1_out")
        run_phase(nc, merge_phase, T, ps, w_in, w_branch_a[0], w_branch_b[0], w_out[0], ln1_g[0:1, :], ln1_b[0:1, :],
                  x1_rows)
        branches.close()
        expert_buffers = ctx.enter_context(ExitStack())
        experts = Memory(nc, expert_buffers)
        T["wgu"] = experts.sb("expert_gu", [P, GROUP, KC, 2 * ED])
        T["wdn"] = experts.sb("expert_down", [P, GROUP, ED // P, D])
        T["blk_e"] = experts.sb("blk_e", [1, LISTS], I32)
        T["trips"] = experts.sb("trips", [1, 3], I32)
        T["tok_idx"] = experts.sb("tok_idx", [P, LISTS // 2], I32)
        T["row_idx"] = experts.sb("row_idx", [P, LISTS], I32)
        T["slot_w"] = experts.sb("slot_w", [P, LISTS])
        T["gu_in"], T["dn_in"] = mem.sems("gu_in", GROUP), mem.sems("dn_in", GROUP)

        def load_expert(sp, s, e, gu_free=None, down_free=None):
            gu = expert_w_gate_up[0][bass.ds(e, 1)].rearrange("e (c p) n -> p (e c) n", p=P)
            dn = expert_w_down[0][bass.ds(e, 1)].rearrange("e (c p) n -> p (e c) n", p=P)
            if gu_free:
                gu_free()
            sp.dma_start(T["wgu"][:, s, :, :], gu).then_inc(T["gu_in"][s], 16)
            if down_free:
                down_free()
            sp.dma_start(T["wdn"][:, s, :, :], dn).then_inc(T["dn_in"][s], 16)

        T["load_expert"] = load_expert
        y_rows = nc.dram_tensor("y_rows", [2 * SEQ * TOPK, D // 2], F32, kind="Internal").ap()
        run_phase(nc, route_phase, T, ps, router_w[0], router_bias[0:1, :], shared_w_gate_up[0], shared_w_down[0])
        run_phase(nc, experts_phase, T, ps, expert_w_gate_up[0], expert_w_down[0], x1_rows, y_rows)
        expert_buffers.close()
        run_phase(nc, final_phase, T, ps, ln2_g[0:1, :], ln2_b[0:1, :], y_rows, out)


_INS = ["x", "w_in", "conv_w", "a_log", "dt_bias", "dn_norm_w", "rel_table", "w_branch_a", "w_branch_b", "w_out",
        "ln1_g", "ln1_b", "router_w", "router_bias", "expert_w_gate_up", "expert_w_down", "shared_w_gate_up",
        "shared_w_down", "ln2_g", "ln2_b"]
_OUTS = [((1, SEQ, D), "float32")]


def kernel(**inputs):
    import numpy as _np
    import concourse.bacc as _bacc
    from concourse import mybir as _mybir
    from concourse.bass_utils import run_bass_kernel_spmd as _run

    nc = _bacc.Bacc("TRN2", target_bir_lowering=False, num_devices=1)
    arrays, args = {}, []
    for name in _INS:
        a = _np.ascontiguousarray(inputs[name])
        arrays[f"in_{name}_dram"] = a
        args.append(nc.dram_tensor(f"in_{name}_dram", a.shape, _mybir.dt.from_np(a.dtype), kind="ExternalInput").ap())
    for i, (shape, dtype) in enumerate(_OUTS):
        dt = _mybir.dt.from_np(_np.dtype(dtype))
        args.append(nc.dram_tensor(f"out_{i}_dram", shape, dt, kind="ExternalOutput").ap())
    program(nc, *args)
    r = _run(nc, [arrays], core_ids=[0])
    got = tuple(r.results[0][f"out_{i}_dram"] for i in range(len(_OUTS)))
    return got[0]
```

```python
from contextlib import ExitStack

import concourse.bass as bass
from concourse import mybir

F32 = mybir.dt.float32
F32R = mybir.dt.float32r
BF16 = mybir.dt.bfloat16
I32 = mybir.dt.int32
ALU = mybir.AluOpType
ACT = mybir.ActivationFunctionType
AX = mybir.AxisListType

P = 128
D = 1024
SEQ = 512
KC = D // P
TT = SEQ // P
HEADS = 8
CONV = 4
LEVELS = 7
AHEADS = 8
AD = 64
AW = AHEADS * AD
CLIP = 256
ACHUNK = 64
NE = 64
TOPK = 6
ED = 256
BLK = 64
NBLK = SEQ // BLK
MAXOVER = SEQ * TOPK // BLK
GROUP = 4
LISTS = NE + MAXOVER + GROUP
OOB = float(1 << 20)
ROUTED_SCALE = 2.5
ALPHA = 2.0 ** 0.25
LN_EXP = "natural_log_exp_and_others"
LN_EPS = 1e-5
RMS_EPS = 1e-6
L2_EPS = 1e-6
NEG = -1e30

Q0, K0, V0, Z0 = 0, D, 2 * D, 3 * D
BA0 = 4 * D
AQ0 = BA0 + 2 * HEADS
AK0 = AQ0 + AW
AV0 = AK0 + AW
GA0 = AV0 + AW
GB0 = GA0 + D


class Memory:

    def __init__(self, nc, ctx):
        self.nc, self.ctx, self.allocated = nc, ctx, []

    def sb(self, name, shape, dt=F32):
        return self.ctx.enter_context(self.nc.sbuf_tensor(name, shape, dt))

    def sem(self, name):
        self.allocated.append(self.nc.alloc_semaphore(name))
        return self.allocated[-1]

    def sems(self, name, n):
        return [self.sem(f"{name}{i}") for i in range(n)]


def run_phase(nc, phase, *args):
    with ExitStack() as ctx:
        mem = Memory(nc, ctx)
        phase(nc, mem, *args)
        nc.clear_and_free_semaphores(mem.allocated)
        nc.all_engine_barrier()


def setup_phase(nc, mem, T, ps, x, w_in, conv_w, a_log, dt_bias, dn_norm_w):
    const_ready = mem.sem("const_ready")
    pool_step = mem.sem("pool_step")
    x_in = mem.sem("x_in")
    small_in = mem.sem("small_in")
    ba_in = mem.sem("ba_in")
    xT_psum = mem.sem("xT_psum")
    xT_copied = mem.sem("xT_copied")
    ba_psum = mem.sem("ba_psum")
    ba_copied = mem.sem("ba_copied")
    cum_psum = mem.sem("cum_psum")
    gates_act = mem.sem("gates_act")
    gates_dve = mem.sem("gates_dve")
    gates_ready = mem.sem("gates_ready")
    cw_psum = mem.sem("cw_psum")
    cw_ready = mem.sem("cw_ready")

    ident, upper, ones = T["ident"], T["upper"], T["ones"]
    xs, xT, GT = T["x"], T["xT"], T["GT"]
    cw_rows, cw = T["cw_rows"], T["cw"]
    w_ba = T["w_ba"]
    gw = T["gate_work"]
    bias_row = T["bias_row"]
    masks = T["masks"]
    w_head, w_ready, proj_done = T["w_head"], T["w_ready"], T["proj_done"]

    with nc.Block() as block:

        @block.sync
        def _(sp):
            for t in range(TT):
                sp.dma_start(xs[:, t, :], x[0, t * P:(t + 1) * P, :]).then_inc(x_in, 16)
            sp.dma_start(w_ba[:, :, :],
                         w_in[:, BA0:AQ0].rearrange("(c p) n -> p c n", p=P)).then_inc(ba_in, 16)
            for g, at in enumerate((Q0, K0, V0, Z0)):
                sp.dma_start(w_head[:, g, :, :], w_in[:, at:at + P].rearrange("(c p) n -> p c n", p=P)) \
                    .then_inc(w_ready[g], 16)

        @block.gpsimd
        def _(pool):
            steps = 0
            nc.gpsimd.memset(ones[:, :], 1.0).then_inc(pool_step, 1)
            nc.gpsimd.memset(ident[:, :], 0.0).then_inc(pool_step, 1)
            nc.gpsimd.memset(masks[:, :, :], 0.0).then_inc(pool_step, 1)
            for i, value in enumerate((L2_EPS, RMS_EPS, LN_EPS)):
                nc.gpsimd.memset(T["eps"][:, i:i + 1], value)
            steps = 3
            pool.wait_ge(pool_step, steps)
            nc.gpsimd.affine_select(out=ident[:, :], in_=ident[:, :], compare_op=ALU.not_equal, fill=1.0,
                                    base=0, pattern=[[-1, P]], channel_multiplier=1).then_inc(const_ready, 1)
            nc.gpsimd.affine_select(out=upper[:, :], in_=ones[:, :], compare_op=ALU.is_ge, fill=0.0,
                                    base=0, pattern=[[1, P]], channel_multiplier=-1).then_inc(const_ready, 1)
            for l in range(LEVELS):
                b = 1 << l
                half = masks[:, l, :].rearrange("p (m r) -> p m r", r=2 * b)[:, :, b:2 * b]
                pool.wait_ge(pool_step, steps)
                nc.gpsimd.memset(half, 1.0).then_inc(pool_step, 1)
                pool.wait_ge(pool_step, steps + 1)
                nc.gpsimd.affine_select(out=half, in_=half, compare_op=ALU.is_ge, fill=0.0, base=0,
                                        pattern=[[-2 * b, P // (2 * b)], [0, b]],
                                        channel_multiplier=1).then_inc(pool_step, 1)
                pool.wait_ge(pool_step, steps + 2)
                nc.gpsimd.affine_select(out=half, in_=half, compare_op=ALU.is_ge, fill=0.0, base=b - 1,
                                        pattern=[[2 * b, P // (2 * b)], [0, b]],
                                        channel_multiplier=-1).then_inc(pool_step, 1)
                steps += 3

        @block.tensor
        def _(pe):
            pe.wait_ge(const_ready, 2)
            pe.wait_ge(x_in, 16 * TT)
            for c in range(KC):
                if c >= 4:
                    pe.wait_ge(xT_copied, c - 3)
                for t in range(TT):
                    mm = nc.tensor.transpose(ps[c % 4][:, t * P:(t + 1) * P], xs[:, t, c * P:(c + 1) * P], ident[:, :])
                mm.then_inc(xT_psum, 1)
            pe.wait_ge(small_in, 16 * 4)
            nc.tensor.transpose(ps[7][:, 0:96], cw_rows[:, :], ident[0:96, 0:96]).then_inc(cw_psum, 1)
            pe.wait_ge(xT_copied, KC)
            pe.wait_ge(ba_in, 16)
            for t in range(TT):
                for c in range(KC):
                    mm = nc.tensor.matmul(ps[4][:, t * 16:t * 16 + 16], xT[:, c, t * P:(t + 1) * P], w_ba[:, c, :],
                                          start=(c == 0), stop=(c == KC - 1))
            mm.then_inc(ba_psum, 1)

            def projection(g):
                pe.wait_ge(w_ready[g], 16)
                for c in range(KC):
                    mm = nc.tensor.matmul(ps[g][:, :], w_head[:, g, c, :], xT[:, c, :], start=(c == 0), stop=(c == KC - 1))
                mm.then_inc(proj_done[g], 1)

            projection(0)
            pe.wait_ge(gates_ready, 1)
            nc.tensor.matmul(ps[5][:, 0:32], upper[:, :], gw[:, 4, :], start=True, stop=True)
            nc.tensor.matmul(ps[6][:, 0:32], ones[:, :], gw[:, 4, :], start=True, stop=True).then_inc(cum_psum, 1)
            projection(1)

        @block.scalar
        def _(act):
            act.dma_start(cw_rows[:, :], conv_w.rearrange("i (g c) -> (i g) c", c=P)).then_inc(small_in, 16)
            act.dma_start(bias_row[:, 0:HEADS], dt_bias[0:1, :].partition_broadcast(P)).then_inc(small_in, 16)
            act.dma_start(bias_row[:, HEADS:2 * HEADS], a_log[0:1, :].partition_broadcast(P)).then_inc(small_in, 16)
            act.dma_start(T["dn_w"][:, :], dn_norm_w.rearrange("a p -> p a")).then_inc(small_in, 16)
            for c in range(0, KC, 2):
                act.wait_ge(xT_psum, c + 1)
                nc.scalar.copy(xT[:, c, :], ps[c % 4][:, :]).then_inc(xT_copied, 1)
                act.wait_ge(xT_copied, c + 2)
            b_in = T["ba"][:, :].rearrange("p (t n) -> p n t", n=16)[:, 0:HEADS, :]
            act.wait_ge(ba_copied, 1)
            act.wait_ge(small_in, 16 * 4)
            nc.scalar.activation(gw[:, 0, :].rearrange("p (h t) -> p h t", t=TT), b_in, ACT.Exp,
                                 scale=-1.0).then_inc(gates_act, 1)
            nc.scalar.activation(bias_row[:, 2 * HEADS:3 * HEADS], bias_row[:, HEADS:2 * HEADS],
                                 ACT.Exp).then_inc(gates_act, 1)
            act.wait_ge(gates_dve, 2)
            nc.scalar.activation(gw[:, 3, :], gw[:, 2, :], ACT.Exp, scale=-1.0).then_inc(gates_act, 1)
            act.wait_ge(gates_dve, 3)
            nc.scalar.activation(gw[:, 5, :], gw[:, 3, :], ACT.Ln).then_inc(gates_act, 1)
            act.wait_ge(gates_dve, 8)
            nc.scalar.activation(GT[:, :, 2, :], gw[:, 0, :].rearrange("p (h t) -> p h t", t=TT), ACT.Exp).then_inc(gates_act, 1)
            nc.scalar.activation(GT[:, :, 4, :], gw[:, 5, :].rearrange("p (h t) -> p h t", t=TT),
                                 ACT.Exp).then_inc(gates_act, 1)
            nc.scalar.activation(GT[:, :, 3, :], gw[:, 1, :].rearrange("p (h t) -> p h t", t=TT), ACT.Exp).then_inc(gates_act, 1)

        @block.vector
        def _(dve):
            for c in range(1, KC, 2):
                dve.wait_ge(xT_psum, c + 1)
                dve.wait_ge(xT_copied, c)
                nc.vector.tensor_copy(xT[:, c, :], ps[c % 4][:, :]).then_inc(xT_copied, 1)
            dve.wait_ge(cw_psum, 1)
            nc.vector.tensor_copy(cw[:, :], ps[7][:, 0:96]).then_inc(cw_ready, 1)
            dve.wait_ge(ba_psum, 1)
            nc.vector.tensor_copy(T["ba"][:, :], ps[4][:, 0:64]).then_inc(ba_copied, 1)
            dve.wait_ge(ba_copied, 1)
            dve.wait_ge(small_in, 16 * 4)
            a_in = T["ba"][:, :].rearrange("p (t n) -> p n t", n=16)[:, HEADS:2 * HEADS, :]
            v = lambda k: gw[:, k, :].rearrange("p (h t) -> p h t", t=TT)
            row = lambda k: bias_row[:, k * HEADS:(k + 1) * HEADS].unsqueeze(2).broadcast_to([P, HEADS, TT])
            nc.vector.tensor_tensor(v(1), a_in, row(0), ALU.add).then_inc(gates_dve, 1)
            dve.wait_ge(gates_dve, 1)
            nc.vector.scalar_tensor_tensor(out=gw[:, 2, :], in0=gw[:, 1, :], scalar=-1.0, in1=gw[:, 1, :],
                                           op0=ALU.mult, op1=ALU.max).then_inc(gates_dve, 1)
            dve.wait_ge(gates_act, 3)
            nc.vector.tensor_scalar(gw[:, 3, :], gw[:, 3, :], 1.0, None, ALU.add).then_inc(gates_dve, 1)
            dve.wait_ge(gates_act, 4)
            nc.vector.scalar_tensor_tensor(out=gw[:, 2, :], in0=gw[:, 1, :], scalar=0.0, in1=gw[:, 5, :],
                                           op0=ALU.max, op1=ALU.add).then_inc(gates_dve, 1)
            dve.wait_ge(gates_dve, 4)
            nc.vector.scalar_tensor_tensor(out=v(4), in0=v(2), scalar=-1.0, in1=row(2),
                                           op0=ALU.mult, op1=ALU.mult).then_inc(gates_ready, 1)
            nc.vector.tensor_scalar(gw[:, 0, :], gw[:, 0, :], 1.0, None, ALU.add).then_inc(gates_dve, 1)
            dve.wait_ge(gates_dve, 5)
            nc.vector.reciprocal(GT[:, :, 1, :], v(0)).then_inc(gates_dve, 1)
            dve.wait_ge(gates_ready, 1)
            nc.vector.tensor_copy(GT[:, :, 5, :], v(4)).then_inc(gates_ready, 1)
            dve.wait_ge(cum_psum, 1)
            dve.wait_ge(gates_dve, 6)
            nc.vector.tensor_copy(gw[:, 0, :], ps[5][:, 0:32]).then_inc(gates_dve, 1)
            dve.wait_ge(gates_dve, 7)
            nc.vector.tensor_copy(GT[:, :, 0, :], v(0)).then_inc(gates_ready, 1)
            nc.vector.tensor_copy(gw[:, 5, :], ps[6][:, 0:32]).then_inc(gates_ready, 1)
            dve.wait_ge(gates_ready, 4)
            nc.vector.tensor_tensor(gw[:, 1, :], gw[:, 5, :], gw[:, 0, :], ALU.subtract).then_inc(gates_dve, 1)


def delta_phase(nc, mem, T, ps, w_in, rel_table, rel_scratch):
    S = mem.sem
    w_ready, proj_done = T["w_ready"], T["proj_done"]
    tap_done = [mem.sems(f"tap{g}_", CONV) for g in range(3)]
    silu_done = mem.sems("silu_done", 4)
    ug_ready = S("ug_ready")
    tok_psum = mem.sems("tok_psum", 3)
    gcrow_psum = S("gcrow_psum")
    hc_ready = S("hc_ready")
    cwh_ready = S("cwh_ready")
    d_ready = S("d_ready")
    ssq_ready = S("ssq_ready")
    lnr_ready = S("lnr_ready")
    r_ready = S("r_ready")
    coef1 = S("coef1")
    coef2 = S("coef2")
    lnrk_ready = S("lnrk_ready")
    decay_ready = S("decay_ready")
    k_scaled = S("k_scaled")
    kall_scaled = S("kall_scaled")
    q_scaled = S("q_scaled")
    v_scaled = S("v_scaled")
    back_psum = mem.sems("back_psum", 3)
    back_copied = mem.sems("back_copied", 3)
    lt_psum = S("lt_psum")
    qk_psum = S("qk_psum")
    lt_ready = S("lt_ready")
    qk_raw = S("qk_raw")
    qk_ready = S("qk_ready")
    loff_ready = mem.sems("loff_ready", LEVELS)
    xt_ready = mem.sems("xt_ready", LEVELS)
    x_psum = S("x_psum")
    x_ready = mem.sems("x_ready", LEVELS)
    y_psum = mem.sems("y_psum", LEVELS)
    y_ready = mem.sems("y_ready", LEVELS)
    z_psum = mem.sems("z_psum", LEVELS)
    zt_psum = mem.sems("zt_psum", LEVELS)
    wt_psum = S("wt_psum")
    wt_ready = S("wt_ready")
    v_psum = mem.sems("v_psum", TT)
    v_ready = mem.sems("v_ready", TT)
    s_psum = mem.sems("s_psum", TT)
    s_ready = mem.sems("s_ready", TT)
    o_psum = S("o_psum")
    osq_ready = S("osq_ready")
    lno_ready = S("lno_ready")
    ro_ready = S("ro_ready")
    o_ready = S("o_ready")
    ot_psum = S("ot_psum")
    dn_done = S("dn_done")
    av_in, aq_in = S("av_in"), mem.sems("aq_in", 2)
    av_psum, av_ready = mem.sems("av_psum", TT), mem.sems("av_ready", TT)
    aq_psum = mem.sems("aq_psum", 2)
    rel_in, rel_built, rel_out, bias_in = S("rel_in"), S("rel_built"), S("rel_out"), S("bias_in")

    ident, upper, ones, masks = T["ident"], T["upper"], T["ones"], T["masks"]
    xT, GT, cw, dnT, eps = T["xT"], T["GT"], T["cw"], T["dnT"], T["eps"]
    w_head = T["w_head"]
    ch = mem.sb("by_channel", [P, 3, SEQ])
    zs = mem.sb("z_silu", [P, SEQ])
    hc = mem.sb("head_gates", [P, 6, TT])
    cwh = mem.sb("head_taps", [P, CONV * 3])
    ug = mem.sb("ug", [P, TT, P])
    dd = mem.sb("decay", [P, TT, P])
    ssq = mem.sb("ssq", [P, 2 * TT])
    lnr = mem.sb("lnr", [P, 2 * TT])
    rr = mem.sb("rr", [P, 2 * TT])
    coef = mem.sb("coef", [P, 6, TT])
    kb = mem.sb("kb", [P, TT, P])
    kbe = mem.sb("kbe", [P, TT, P])
    kd = mem.sb("kd", [P, TT, P])
    qn = mem.sb("qn", [P, TT, P])
    qd = mem.sb("qd", [P, TT, P])
    vb = mem.sb("vb", [P, TT, P])
    kbT = mem.sb("kbT", [P, TT, P])
    qnT = mem.sb("qnT", [P, TT, P])
    qdT = mem.sb("qdT", [P, TT, P])
    LT = mem.sb("LT", [P, TT, P])
    QK = mem.sb("QK", [P, TT, P])
    LO = mem.sb("LO", [P, LEVELS, TT, P])
    X = mem.sb("X", [P, TT, P])
    XT = mem.sb("XT", [P, TT, P])
    Y = mem.sb("Y", [P, TT, P])
    wTn = mem.sb("wTn", [P, TT, P])
    vn = mem.sb("vn", [P, TT, P])
    St = mem.sb("state", [P, 2, P])
    on = mem.sb("on", [P, TT, P])
    sq = mem.sb("sq_scratch", [P, 3, TT, P])
    osq = mem.sb("osq", [P, 3, TT])
    EXT = SEQ + P
    w_av = mem.sb("w_av", [P, KC, AW])
    w_pair = T["aoT"][:, :, :].rearrange("p j (b n) -> p (j b) n", n=P)
    tab = mem.sb("rel_tab", [AHEADS, 2 * CLIP + 1])
    ext = mem.sb("rel_ext", [AHEADS, EXT])
    bias, av, qkT = T["bias"], T["av"], T["qkT"]

    tiles = lambda bank: bank[:, :].rearrange("p (n i) -> p n i", n=TT)
    per_tile = lambda col: col.unsqueeze(2).broadcast_to([P, TT, P])
    all_tiles = lambda m: m.unsqueeze(1).broadcast_to([P, TT, P])
    cols = [Q0, K0, V0, Z0]

    with nc.Block() as block:

        @block.sync
        def _(sp):
            def load(g, m):
                sp.dma_start(w_head[:, g, :, :], w_in[:, bass.ds(cols[g] + m * P, P)].rearrange(
                    "(c p) n -> p c n", p=P)).then_inc(w_ready[g], 16)

            sp.dma_start(tab[:, :], rel_table).then_inc(rel_in, 16)
            for g in range(4):
                sp.wait_ge(proj_done[g], 1)
                load(g, 1)
            sp.wait_ge(rel_built, 2)
            sp.dma_start(rel_scratch[:, :], ext[:, :]).then_inc(rel_out, 16)
            sp.wait_ge(rel_out, 16)
            for h in range(AHEADS):
                window = bass.AP(tensor=rel_scratch.tensor, offset=h * EXT, ap=[[1, P], [1, SEQ]])
                sp.dma_start(bias[:, h, :], window).then_inc(bias_in, 16)
            sp.dma_start(w_av[:, :, :], w_in[:, AV0:GA0].rearrange("(c p) n -> p c n", p=P)).then_inc(av_in, 16)
            for g, at in enumerate((AQ0, AK0)):
                sp.dma_start(w_pair[:, g * KC:(g + 1) * KC, :], w_in[:, at:at + P].rearrange(
                    "(c p) n -> p c n", p=P)).then_inc(aq_in[g], 16)
            with sp.Fori(2, HEADS) as m:
                for g in range(4):
                    sp.wait_ge(proj_done[g], m)
                    load(g, m)

        @block.tensor
        def _(pe):
            def projection(g, c, head1, bank):
                if c == 0:
                    pe.wait_ge(w_ready[g], 16 * head1)
                mm = nc.tensor.matmul(bank[:, :], w_head[:, g, c, :], xT[:, c, :],
                                      start=(c == 0), stop=(c == KC - 1))
                if c == KC - 1:
                    mm.then_inc(proj_done[g], 1)

            for g in range(2, 4):
                for c in range(KC):
                    projection(g, c, 1, ps[g])

            def attention_product(g, c):
                if c == 0:
                    if g == 0:
                        pe.wait_ge(tap_done[2][3], HEADS)
                        pe.wait_ge(av_in, 16)
                    elif g == 1:
                        pe.wait_ge(silu_done[3], HEADS)
                    else:
                        pe.wait_ge(av_ready[g - 2], 1)
                    if g >= TT:
                        pe.wait_ge(aq_in[g - TT], 16)
                if g < TT:
                    mm = nc.tensor.matmul(ps[g % 2][:, :], xT[:, c, g * P:(g + 1) * P], w_av[:, c, :],
                                          start=(c == 0), stop=(c == KC - 1))
                else:
                    mm = nc.tensor.matmul(ps[g % 2][:, :], w_pair[:, (g - TT) * KC + c, :], xT[:, c, :],
                                          start=(c == 0), stop=(c == KC - 1))
                if c == KC - 1:
                    mm.then_inc(av_psum[g] if g < TT else aq_psum[g - TT], 1)

            def body(h, fillers):
                now = h + 1
                groups = 4 if fillers else TT + 2
                queue = [(g, c) for g in range(groups) for c in range(KC)]

                def fill(n):
                    for _ in range(min(n, len(queue))):
                        g, c = queue.pop(0)
                        if not fillers:
                            attention_product(g, c)
                            continue
                        if c == 0:
                            if g == 0:
                                pe.wait_ge(tap_done[2][3], now)
                            elif g == 1:
                                pe.wait_ge(silu_done[3], now)
                            elif g == 2:
                                pe.wait_ge(tap_done[0][3], now + 1)
                            else:
                                pe.wait_ge(tap_done[1][3], now + 1)
                        projection(g, c, now + 1, ps[g % 2])

                for g in range(3):
                    pe.wait_ge(silu_done[g], now)
                    for n in range(TT):
                        mm = nc.tensor.transpose(ps[2 + g][:, n * P:(n + 1) * P], ch[:, g, n * P:(n + 1) * P], ident[:, :])
                    mm.then_inc(tok_psum[g], 1)
                pe.wait_ge(ug_ready, now)
                nc.tensor.matmul(ps[5][:, :], ones[:, :], ug[:, :, :], start=True, stop=True).then_inc(gcrow_psum, 1)
                fill(4)
                for i, (src, bank, ready) in enumerate([(kb, 7, k_scaled), (qn, 2, q_scaled), (qd, 3, None)]):
                    if ready is not None:
                        pe.wait_ge(ready, now)
                    if i == 1:
                        pe.wait_ge(kall_scaled, now)
                    for n in range(TT):
                        mm = nc.tensor.transpose(ps[bank][:, n * P:(n + 1) * P], src[:, n, :], ident[:, :])
                    mm.then_inc(back_psum[i], 1)
                fill(2)
                pe.wait_ge(back_copied[0], now)
                pe.wait_ge(v_scaled, now)
                for n in range(TT):
                    mm = nc.tensor.matmul(ps[4][:, n * P:(n + 1) * P], ch[:, 1, n * P:(n + 1) * P], kbT[:, n, :],
                                          start=True, stop=True)
                mm.then_inc(lt_psum, 1)
                pe.wait_ge(back_copied[1], now)
                for n in range(TT):
                    mm = nc.tensor.matmul(ps[5][:, n * P:(n + 1) * P], ch[:, 1, n * P:(n + 1) * P], qnT[:, n, :],
                                          start=True, stop=True)
                mm.then_inc(qk_psum, 1)
                fill(2)
                pe.wait_ge(xt_ready[0], now)
                for n in range(TT):
                    mm = nc.tensor.transpose(ps[6][:, n * P:(n + 1) * P], XT[:, n, :], ident[:, :])
                mm.then_inc(x_psum, 1)
                fill(1)
                for l in range(1, LEVELS):
                    pe.wait_ge(x_ready[l - 1], now)
                    pe.wait_ge(loff_ready[l], now)
                    for n in range(TT):
                        mm = nc.tensor.matmul(ps[7][:, n * P:(n + 1) * P], LO[:, l, n, :], X[:, n, :],
                                              start=True, stop=True)
                    mm.then_inc(y_psum[l], 1)
                    fill(1)
                    pe.wait_ge(y_ready[l], now)
                    pe.wait_ge(xt_ready[l - 1], now)
                    if l == 1:
                        pe.wait_ge(back_copied[2], now)
                    if l < LEVELS - 1:
                        for n in range(TT):
                            mm = nc.tensor.matmul(ps[2][:, n * P:(n + 1) * P], XT[:, n, :], Y[:, n, :],
                                                  start=True, stop=True)
                        mm.then_inc(z_psum[l], 1)
                    for n in range(TT):
                        mm = nc.tensor.matmul(ps[3][:, n * P:(n + 1) * P], Y[:, n, :], XT[:, n, :],
                                              start=True, stop=True)
                    mm.then_inc(zt_psum[l], 1)
                    fill(1)
                pe.wait_ge(xt_ready[LEVELS - 1], now)
                for n in range(TT):
                    mm = nc.tensor.matmul(ps[4][:, n * P:(n + 1) * P], kbe[:, n, :], XT[:, n, :], start=True, stop=True)
                mm.then_inc(wt_psum, 1)
                pe.wait_ge(qk_raw, now)
                for n in range(TT):
                    at = slice(n * P, (n + 1) * P)
                    mm = nc.tensor.matmul(ps[5][:, at], XT[:, n, :], vb[:, n, :], start=True, stop=(n == 0))
                    if n:
                        if n == 1:
                            pe.wait_ge(wt_ready, now)
                        pe.wait_ge(s_ready[n - 1], now)
                        mm = nc.tensor.matmul(ps[5][:, at], wTn[:, n, :], St[:, (n - 1) % 2, :], start=False, stop=True)
                    mm.then_inc(v_psum[n], 1)
                    fill(1)
                    pe.wait_ge(v_ready[n], now)
                    if n < TT - 1:
                        nc.tensor.matmul(ps[6][:, 0:P], kd[:, n, :], vn[:, n, :], start=True, stop=True).then_inc(s_psum[n], 1)
                    if n == 0:
                        pe.wait_ge(qk_ready, now)
                    else:
                        nc.tensor.matmul(ps[7][:, at], qdT[:, n, :], St[:, (n - 1) % 2, :], start=True, stop=False)
                    mm = nc.tensor.matmul(ps[7][:, at], QK[:, n, :], vn[:, n, :], start=(n == 0), stop=True)
                    if n == TT - 1:
                        mm.then_inc(o_psum, 1)
                    fill(1)
                fill(3)
                pe.wait_ge(o_ready, now)
                for n in range(TT):
                    mm = nc.tensor.transpose(ps[6][:, n * P:(n + 1) * P], on[:, n, :], ident[:, :])
                mm.then_inc(ot_psum, 1)
                fill(len(queue))

            pe.wait_ge(tap_done[2][3], 1)
            pe.wait_ge(silu_done[3], 1)
            with pe.Fori(0, HEADS - 1) as h:
                body(h, True)
            body(HEADS - 1, False)

        @block.gpsimd
        def _(pool):
            def make_ug(h, now):
                nc.gpsimd.tensor_tensor(ug[:, :, :], all_tiles(upper[:, :]), per_tile(GT[:, h, 5, :]),
                                        ALU.mult).then_inc(ug_ready, 1)

            make_ug(0, None)

            def body(h, last):
                now = h + 1
                pool.wait_ge(lt_ready, now)
                for l in range(LEVELS):
                    nc.gpsimd.tensor_tensor(LO[:, l, :, :], LT[:, :, :], all_tiles(masks[:, l, :]),
                                            ALU.mult).then_inc(loff_ready[l], 1)
                    if l == 1:
                        pool.wait_ge(qk_raw, now)
                        nc.gpsimd.tensor_tensor(QK[:, :, :], QK[:, :, :], all_tiles(upper[:, :]),
                                                ALU.mult).then_inc(qk_ready, 1)
                if not last:
                    pool.wait_ge(gcrow_psum, now)
                    make_ug(h + 1, now)

            with pool.Fori(0, HEADS - 1) as h:
                body(h, False)
            body(HEADS - 1, True)
            pool.wait_ge(bias_in, 16 * AHEADS)
            nc.gpsimd.memset(bias[0:ACHUNK, :, 0:ACHUNK], NEG)

        @block.scalar
        def _(act):
            def silus(h, head1, first):
                for g in range(3):
                    act.wait_ge(tap_done[g][3], head1)
                    nc.scalar.activation(ch[:, g, :], ch[:, g, :], ACT.Silu).then_inc(silu_done[g], 1)
                act.wait_ge(proj_done[3], head1)
                if not first:
                    act.wait_ge(dn_done, h + 1)
                nc.scalar.activation(zs[:, :], ps[3 if first else 1][:, :], ACT.Silu).then_inc(silu_done[3], 1)
                nc.scalar.preload_act_table_set(LN_EXP)

            silus(None, 1, True)

            def copy_values(t):
                act.wait_ge(av_psum[t], 1)
                nc.scalar.copy(av[:, t, :], ps[t % 2][:, :]).then_inc(av_ready[t], 1)

            def body(h, last):
                now = h + 1
                for g in range(2):
                    act.wait_ge(tok_psum[g], now)
                    for n in range(TT):
                        a = nc.scalar.activation(sq[:, g, n, :], ps[2 + g][:, n * P:(n + 1) * P], ACT.Square,
                                                 accum_out=ssq[:, g * TT + n:g * TT + n + 1])
                a.then_inc(ssq_ready, 1)
                act.wait_ge(ssq_ready, now)
                nc.scalar.activation(lnr[:, :], ssq[:, :], ACT.Ln, bias=eps[:, 0:1]).then_inc(lnr_ready, 1)
                act.wait_ge(lnr_ready, now)
                nc.scalar.activation(rr[:, :], lnr[:, :], ACT.Exp, scale=-0.5).then_inc(r_ready, 1)
                act.wait_ge(d_ready, now)
                act.wait_ge(lnrk_ready, now)
                for n in range(TT):
                    a = nc.scalar.activation(dd[:, n, :], dd[:, n, :], ACT.Exp, bias=coef[:, 5, n:n + 1])
                a.then_inc(decay_ready, 1)
                for i, (dst, bank) in enumerate([(kbT, 7), (qnT, 2), (qdT, 3)]):
                    act.wait_ge(back_psum[i], now)
                    nc.scalar.copy(dst[:, :, :], tiles(ps[bank])).then_inc(back_copied[i], 1)
                act.wait_ge(x_psum, now)
                nc.scalar.copy(X[:, :, :], tiles(ps[6])).then_inc(x_ready[0], 1)
                for l in range(1, LEVELS):
                    act.wait_ge(y_psum[l], now)
                    nc.scalar.copy(Y[:, :, :], tiles(ps[7])).then_inc(y_ready[l], 1)
                    if last and l in (1, 5):
                        copy_values(l // 4)
                act.wait_ge(wt_psum, now)
                nc.scalar.mul(wTn[:, :, :], tiles(ps[4]), -1.0).then_inc(wt_ready, 1)
                for n in range(TT):
                    act.wait_ge(v_psum[n], now)
                    nc.scalar.copy(vn[:, n, :], ps[5][:, n * P:(n + 1) * P]).then_inc(v_ready[n], 1)
                    if last and n == 3:
                        copy_values(2)
                act.wait_ge(o_psum, now)
                for n in range(TT):
                    a = nc.scalar.activation(sq[:, 2, n, :], ps[7][:, n * P:(n + 1) * P], ACT.Square,
                                             accum_out=osq[:, 0, n:n + 1])
                a.then_inc(osq_ready, 1)
                act.wait_ge(osq_ready, now)
                nc.scalar.activation(osq[:, 1, :], osq[:, 0, :], ACT.Ln, bias=eps[:, 1:2], scale=1.0 / P).then_inc(lno_ready, 1)
                act.wait_ge(lno_ready, now)
                nc.scalar.activation(osq[:, 2, :], osq[:, 1, :], ACT.Exp, scale=-0.5).then_inc(ro_ready, 1)
                if not last:
                    silus(h, now + 1, False)

            with act.Fori(0, HEADS - 1) as h:
                body(h, False)
            body(HEADS - 1, True)
            copy_values(3)
            act.wait_ge(aq_psum[0], 1)
            nc.scalar.mul(qkT[:, 0, :], ps[0][:, :], AD ** -0.5)
            act.wait_ge(aq_psum[1], 1)
            nc.scalar.copy(qkT[:, 1, :], ps[1][:, :])

        @block.vector
        def _(dve):
            def tap(g, k, head1, first=False):
                if k == 0:
                    dve.wait_ge(proj_done[g], head1)
                else:
                    dve.wait_ge(tap_done[g][k - 1], head1)
                bank = ps[g if first else g % 2]
                w = cwh[:, (CONV - 1 - k) * 3 + g:(CONV - 1 - k) * 3 + g + 1]
                if k == 0:
                    nc.vector.tensor_scalar(ch[:, g, :], bank[:, :], w, None, ALU.mult).then_inc(tap_done[g][0], 1)
                else:
                    nc.vector.scalar_tensor_tensor(out=ch[:, g, k:SEQ], in0=bank[:, 0:SEQ - k], scalar=w,
                                                   in1=ch[:, g, k:SEQ], op0=ALU.mult, op1=ALU.add).then_inc(tap_done[g][k], 1)

            def take_taps(h, head1):
                nc.vector.tensor_copy(cwh[:, :], cw[:, :].rearrange("p (k h) -> p k h", h=HEADS)[:, :, h]).then_inc(cwh_ready, 1)
                dve.wait_ge(cwh_ready, head1)

            take_taps(0, 1)
            for g in range(3):
                for k in range(CONV):
                    tap(g, k, 1, first=True)
            dve.wait_ge(rel_in, 16)
            n_tab = CLIP + P
            nc.vector.tensor_copy(ext[:, 0:n_tab], tab[:, 0:n_tab][:, ::-1]).then_inc(rel_built, 1)
            nc.vector.tensor_copy(ext[:, n_tab:EXT], tab[:, 0:1].broadcast_to([AHEADS, EXT - n_tab])).then_inc(rel_built, 1)

            def body(h, last):
                now = h + 1
                if h is not None and not last:
                    dve.wait_ge(tap_done[2][3], now)
                    take_taps(h + 1, now + 1)
                gate = lambda k: hc[:, k, :]
                nc.vector.tensor_copy(hc[:, :, :], GT[:, h, :, :]).then_inc(hc_ready, 1)
                dve.wait_ge(hc_ready, now)
                dve.wait_ge(gcrow_psum, now)
                for n in range(TT):
                    a = nc.vector.tensor_scalar(dd[:, n, :], ps[5][:, n * P:(n + 1) * P], hc[:, 0, n:n + 1], 0.0,
                                                ALU.subtract, ALU.min)
                a.then_inc(d_ready, 1)
                dve.wait_ge(r_ready, now)
                nc.vector.tensor_scalar(coef[:, 5, :], lnr[:, TT:2 * TT], -0.5, None, ALU.mult).then_inc(lnrk_ready, 1)
                nc.vector.tensor_tensor(coef[:, 0, :], rr[:, TT:2 * TT], gate(1), ALU.mult)
                nc.vector.tensor_tensor(coef[:, 2, :], rr[:, TT:2 * TT], gate(3), ALU.mult)
                nc.vector.tensor_scalar(coef[:, 3, :], rr[:, 0:TT], P ** -0.5, None, ALU.mult).then_inc(coef1, 1)
                dve.wait_ge(coef1, now)
                nc.vector.tensor_tensor(coef[:, 1, :], coef[:, 0, :], gate(2), ALU.mult)
                nc.vector.tensor_tensor(coef[:, 4, :], coef[:, 3, :], gate(2), ALU.mult).then_inc(coef2, 1)
                nc.vector.tensor_tensor(kb[:, :, :], tiles(ps[3]), per_tile(coef[:, 0, :]), ALU.mult).then_inc(k_scaled, 1)
                dve.wait_ge(coef2, now)
                nc.vector.tensor_tensor(kbe[:, :, :], tiles(ps[3]), per_tile(coef[:, 1, :]), ALU.mult)
                nc.vector.tensor_tensor(kd[:, :, :], tiles(ps[3]), per_tile(coef[:, 2, :]), ALU.mult).then_inc(kall_scaled, 1)
                nc.vector.tensor_tensor(qn[:, :, :], tiles(ps[2]), per_tile(coef[:, 3, :]), ALU.mult)
                nc.vector.tensor_tensor(qd[:, :, :], tiles(ps[2]), per_tile(coef[:, 4, :]), ALU.mult).then_inc(q_scaled, 1)
                dve.wait_ge(tok_psum[2], now)
                nc.vector.tensor_tensor(vb[:, :, :], tiles(ps[4]), per_tile(gate(1)), ALU.mult).then_inc(v_scaled, 1)
                dve.wait_ge(lt_psum, now)
                dve.wait_ge(decay_ready, now)
                nc.vector.tensor_tensor(LT[:, :, :], tiles(ps[4]), dd[:, :, :], ALU.mult).then_inc(lt_ready, 1)
                dve.wait_ge(qk_psum, now)
                nc.vector.tensor_tensor(QK[:, :, :], tiles(ps[5]), dd[:, :, :], ALU.mult).then_inc(qk_raw, 1)
                dve.wait_ge(loff_ready[0], now)
                nc.vector.tensor_tensor(XT[:, :, :], all_tiles(ident[:, :]), LO[:, 0, :, :], ALU.subtract).then_inc(xt_ready[0], 1)
                for l in range(1, LEVELS):
                    if l < LEVELS - 1:
                        dve.wait_ge(z_psum[l], now)
                        dve.wait_ge(x_ready[l - 1], now)
                        nc.vector.tensor_tensor(X[:, :, :], X[:, :, :], tiles(ps[2]), ALU.subtract).then_inc(x_ready[l], 1)
                    dve.wait_ge(zt_psum[l], now)
                    dve.wait_ge(xt_ready[l - 1], now)
                    nc.vector.tensor_tensor(XT[:, :, :], XT[:, :, :], tiles(ps[3]), ALU.subtract).then_inc(xt_ready[l], 1)
                    if not last and l in (1, 2):
                        tap(0, 2 * l - 2, now + 1)
                        tap(0, 2 * l - 1, now + 1)
                    if not last and l in (5, 6):
                        tap(1, 2 * l - 10, now + 1)
                        tap(1, 2 * l - 9, now + 1)
                for n in range(TT):
                    if n < TT - 1:
                        dve.wait_ge(s_psum[n], now)
                        if n == 0:
                            nc.vector.tensor_copy(St[:, 0, :], ps[6][:, 0:P]).then_inc(s_ready[0], 1)
                        else:
                            dve.wait_ge(s_ready[n - 1], now)
                            nc.vector.scalar_tensor_tensor(out=St[:, n % 2, :], in0=St[:, (n - 1) % 2, :],
                                                           scalar=hc[:, 4, n:n + 1], in1=ps[6][:, 0:P],
                                                           op0=ALU.mult, op1=ALU.add).then_inc(s_ready[n], 1)
                    if not last and n in (2, 3):
                        tap(2, 2 * n - 4, now + 1)
                        tap(2, 2 * n - 3, now + 1)
                dve.wait_ge(ro_ready, now)
                nc.vector.tensor_tensor(on[:, :, :], tiles(ps[7]), per_tile(osq[:, 2, :]), ALU.mult).then_inc(o_ready, 1)
                dve.wait_ge(ot_psum, now)
                dve.wait_ge(silu_done[3], now)
                nc.vector.scalar_tensor_tensor(out=dnT[:, h, :], in0=ps[6][:, :], scalar=T["dn_w"][:, 0:1], in1=zs[:, :],
                                               op0=ALU.mult, op1=ALU.mult).then_inc(dn_done, 1)

            with dve.Fori(0, HEADS - 1) as h:
                body(h, False)
            body(HEADS - 1, True)


def attention_phase(nc, mem, T, ps, w_in):
    S = mem.sem
    pair_in = mem.sems("pair_in", 2)
    pair_psum = mem.sems("pair_psum", 2)
    pair_ready = mem.sems("pair_ready", 2)
    avh_ready = S("avh_ready")
    hi_ready = S("hi_ready")
    bp_ready = S("bp_ready")
    sc_psum = [mem.sems(f"sc_psum{e}_", TT) for e in range(2)]
    sc_ready = [mem.sems(f"sc_ready{e}_", TT) for e in range(2)]
    nm_ready = [mem.sems(f"nm_ready{e}_", TT) for e in range(2)]
    ex_ready = [mem.sems(f"ex_ready{e}_", TT) for e in range(2)]
    rs_ready = [mem.sems(f"rs_ready{e}_", TT) for e in range(2)]
    pr_ready = [mem.sems(f"pr_ready{e}_", TT) for e in range(2)]
    pt_psum = [mem.sems(f"pt_psum{e}_", TT) for e in range(2)]
    pt_ready = [mem.sems(f"pt_ready{e}_", TT) for e in range(2)]
    ao_psum = mem.sems("ao_psum", 2)
    ao_ready = mem.sems("ao_ready", 2)

    PAIRS = AHEADS // 2
    ident, xT, aoT = T["ident"], T["xT"], T["aoT"]
    w_pair = mem.sb("w_pair", [P, 2, KC, P])
    av, qkT, bias = T["av"], T["qkT"], T["bias"]
    avh = mem.sb("av_pair", [P, TT, P])
    bias_pair = mem.sb("bias_pair", [P, 2, SEQ])
    sc = mem.sb("scores", [P, 2, TT, SEQ])
    small = mem.sb("softmax_small", [P, 4, 2 * TT])
    PT = mem.sb("weightsT", [P, 2, SEQ])
    cols = [AQ0, AK0]

    with nc.Block() as block:

        @block.sync
        def _(sp):
            def load(g, j):
                sp.dma_start(w_pair[:, g, :, :], w_in[:, bass.ds(cols[g] + j * P, P)].rearrange(
                    "(c p) n -> p c n", p=P)).then_inc(pair_in[g], 16)

            for g in range(2):
                load(g, 1)
            with sp.Fori(1, PAIRS - 1) as j:
                for g in range(2):
                    sp.wait_ge(pair_psum[g], j)
                    load(g, j + 1)

        @block.gpsimd
        def _(pool):
            def split(j):
                at = bass.ds(2 * j, KC // PAIRS)
                both = ((xT, T["xh"], T["xl"]), (T["dnT"], T["dnh"], T["dnl"]))
                for full, high, _ in both:
                    nc.gpsimd.tensor_copy(high[:, at, :].bitcast(F32R), full[:, at, :]).then_inc(hi_ready, 1)
                pool.wait_ge(hi_ready, 2 * j + 2)
                for full, high, low in both:
                    nc.gpsimd.tensor_tensor(low[:, at, :].bitcast(F32R), full[:, at, :], high[:, at, :], ALU.subtract)

            nc.gpsimd.tensor_copy(bias_pair[:, :, :], bias[:, 0:2, :]).then_inc(bp_ready, 1)
            nc.gpsimd.tensor_copy(avh[:, :, :], av[:, :, 0:P]).then_inc(avh_ready, 1)
            split(0)
            with pool.Fori(1, PAIRS) as j:
                pool.wait_ge(sc_ready[1][TT - 1], j)
                nc.gpsimd.tensor_copy(bias_pair[:, :, :], bias[:, bass.ds(2 * j, 2), :]).then_inc(bp_ready, 1)
                pool.wait_ge(ao_psum[1], j)
                nc.gpsimd.tensor_copy(avh[:, :, :], av[:, :, bass.ds(j * P, P)]).then_inc(avh_ready, 1)
                split(j)

        @block.tensor
        def _(pe):
            def projection(g, c, pair):
                if c == 0:
                    pe.wait_ge(pair_in[g], 16 * pair)
                mm = nc.tensor.matmul(ps[g][:, :], w_pair[:, g, c, :], xT[:, c, :], start=(c == 0), stop=(c == KC - 1))
                if c == KC - 1:
                    mm.then_inc(pair_psum[g], 1)

            def body(j, fillers, first=False):
                now = j + 1
                queue = [(g, c) for g in range(2) for c in range(KC)] if fillers else []

                def fill(n):
                    for _ in range(min(n, len(queue))):
                        g, c = queue.pop(0)
                        if c == 0 and not first:
                            pe.wait_ge(pair_ready[g], j)
                        projection(g, c, now)

                if not first:
                    for g in range(2):
                        pe.wait_ge(pair_ready[g], j)
                for e in range(2):
                    rows = slice(AD * e, AD * e + AD)
                    for n in range(TT):
                        if n >= 2:
                            pe.wait_ge(sc_ready[e][n - 2], now)
                        elif e:
                            pe.wait_ge(sc_ready[0][n + 2], now)
                        nc.tensor.matmul(ps[2 + n % 2][:, 0:(n + 1) * P], qkT[rows, 0, n * P:(n + 1) * P],
                                         qkT[rows, 1, 0:(n + 1) * P], start=True, stop=True).then_inc(sc_psum[e][n], 1)
                        fill(1)
                for e in range(2):
                    for kt in range(TT):
                        i = e * TT + kt
                        if i >= 2:
                            pe.wait_ge(pt_ready[(i - 2) // TT][(i - 2) % TT], now)
                        for n in range(kt, TT):
                            pe.wait_ge(pr_ready[e][n], now)
                            mm = nc.tensor.transpose(ps[4 + i % 2][:, n * P:(n + 1) * P], sc[:, e, n, kt * P:(kt + 1) * P],
                                                     ident[:, :])
                        mm.then_inc(pt_psum[e][kt], 1)
                        fill(1)
                        pe.wait_ge(pt_ready[e][kt], now)
                        if kt == 0:
                            if e == 0:
                                pe.wait_ge(avh_ready, now)
                        mm = nc.tensor.matmul(ps[6 + e][AD * e:AD * e + AD, kt * P:SEQ], avh[:, kt, AD * e:AD * e + AD],
                                              PT[:, i % 2, kt * P:SEQ], start=(kt == 0), stop=(kt == TT - 1))
                    mm.then_inc(ao_psum[e], 1)
                fill(32)

            body(0, True, first=True)
            with pe.Fori(1, PAIRS - 1) as j:
                body(j, True)
            body(PAIRS - 1, False)

        @block.scalar
        def _(act):
            def body(j, first=False):
                now = j + 1
                for g in range(0 if first else 2):
                    act.wait_ge(pair_psum[g], j)
                    if g == 0:
                        nc.scalar.mul(qkT[:, 0, :], ps[0][:, :], AD ** -0.5).then_inc(pair_ready[0], 1)
                    else:
                        nc.scalar.copy(qkT[:, 1, :], ps[1][:, :]).then_inc(pair_ready[1], 1)
                for e in range(2):
                    for n in range(TT):
                        act.wait_ge(nm_ready[e][n], now)
                        s = e * TT + n
                        nc.scalar.activation(sc[:, e, n, 0:(n + 1) * P], sc[:, e, n, 0:(n + 1) * P], ACT.Exp,
                                             bias=small[:, 1, s:s + 1],
                                             accum_out=small[:, 2, s:s + 1]).then_inc(ex_ready[e][n], 1)
                for e in range(2):
                    for kt in range(TT):
                        i = e * TT + kt
                        act.wait_ge(pt_psum[e][kt], now)
                        nc.scalar.copy(PT[:, i % 2, kt * P:SEQ], ps[4 + i % 2][:, kt * P:SEQ]).then_inc(pt_ready[e][kt], 1)
                    act.wait_ge(ao_psum[e], now)
                    nc.scalar.copy(aoT[AD * e:AD * e + AD, j, :], ps[6 + e][AD * e:AD * e + AD, :]).then_inc(ao_ready[e], 1)

            body(0, first=True)
            with act.Fori(1, PAIRS) as j:
                body(j)

        @block.vector
        def _(dve):
            def body(j):
                now = j + 1
                dve.wait_ge(bp_ready, now)
                for e in range(2):
                    for n in range(TT):
                        s = e * TT + n
                        L = (n + 1) * P
                        dve.wait_ge(sc_psum[e][n], now)
                        nc.vector.tensor_tensor(sc[:, e, n, 0:L], ps[2 + n % 2][:, 0:L], bias_pair[:, e, 0:L][:, ::-1],
                                                ALU.add).then_inc(sc_ready[e][n], 1)
                        dve.wait_ge(sc_ready[e][n], now)
                        nc.vector.tensor_reduce(small[:, 1, s:s + 1], sc[:, e, n, 0:L], AX.X, ALU.max,
                                                negate=True).then_inc(nm_ready[e][n], 1)
                for e in range(2):
                    for n in range(TT):
                        s = e * TT + n
                        L = (n + 1) * P
                        dve.wait_ge(ex_ready[e][n], now)
                        nc.vector.reciprocal(small[:, 3, s:s + 1], small[:, 2, s:s + 1]).then_inc(rs_ready[e][n], 1)
                        dve.wait_ge(rs_ready[e][n], now)
                        nc.vector.tensor_scalar(sc[:, e, n, 0:L], sc[:, e, n, 0:L], small[:, 3, s:s + 1], None,
                                                ALU.mult).then_inc(pr_ready[e][n], 1)

            with dve.Fori(0, PAIRS) as j:
                body(j)


def merge_phase(nc, mem, T, ps, w_in, w_a, w_b, w_out, ln_g, ln_b, x1_rows):
    hi_ready = [mem.sems(f"mhi{p}_", 4) for p in range(2)]
    lo_ready = [mem.sems(f"mlo{p}_", 4) for p in range(2)]
    aoh_ready, ao_split = mem.sem("aoh_ready"), mem.sem("ao_split")
    w_in4 = [mem.sems(f"mw{p}_", 4) for p in range(2)]
    prod = [mem.sems(f"mprod{p}_", 4) for p in range(2)]
    sig_ready = [mem.sems(f"msig{p}_", 2) for p in range(2)]
    gated = [mem.sems(f"mgated{p}_", 2) for p in range(2)]
    merged = mem.sems("merged", 2)
    wo_in, ln_in = mem.sem("wo_in"), mem.sem("ln_in")
    mix_psum = mem.sems("mix_psum", TT)
    z_done = mem.sems("z_done", TT)
    st_done, ag_done, ln_ln, ln_rs, ln_n, ln_m, ln_done = (
        mem.sems(n, TT) for n in ("st_done", "ag_done", "ln_ln", "ln_rs", "ln_n", "ln_m", "ln_done"))
    x1_out = T["x1_out"]
    x1t_psum, x1t_ready = mem.sem("x1t_psum"), mem.sem("x1t_ready")

    xs, xT, dnT, aoT, ident, eps = T["x"], T["xT"], T["dnT"], T["aoT"], T["ident"], T["eps"]
    w_t = mem.sb("w_tile", [P, 3 * KC + AW // P, P])
    sg = T["av"][:, :, :].rearrange("p (q k) n -> p q k n", q=2)
    w_hi, w_lo = mem.sb("w_hi", [P, 2, KC, P]), mem.sb("w_lo", [P, 2, KC, P])
    aoh, aol = mem.sb("aoh", [P, AW // P, SEQ]), mem.sb("aol", [P, AW // P, SEQ])
    mT = dnT
    wo_low, wo_high = xT[:, :, :].rearrange("p (c a) n -> p c (a n)", a=2), T["bias"][:, :, :].rearrange("p (c a) n -> p c (a n)", a=2)
    wo = lambda c: (wo_low if c < KC // 2 else wo_high)[:, c % (KC // 2), :]
    g_row, b_row = (aoT[:, 2 * k:2 * k + 2, :].rearrange("p a n -> p (a n)") for k in range(2))
    stats = mem.sb("ln1_stats", [P, TT, 2, 6])
    mv = mem.sb("ln1_mv", [P, TT, 4])
    sources = [(w_in, GA0, KC), (w_a, 0, KC), (w_in, GB0, KC), (w_b, 0, AW // P)]
    moving = [(T["xh"], T["xl"]), (T["dnh"], T["dnl"]), (T["xh"], T["xl"]), (aoh, aol)]
    HALF = D // 2
    TURNS = KC // 2

    def two_on(i, p, k):
        return (i, p, k + 2) if k < 2 else (i + (p + 1) // 2, (p + 1) % 2, k - 2)

    with nc.Block() as block:

        @block.sync
        def _(sp):
            def load(p, k, start):
                src, at, n = sources[k]
                sp.dma_start(w_t[:, k * KC:k * KC + n, :], src[:, at:at + D][:, bass.ds(start, P)].rearrange(
                    "(c p) n -> p c n", p=P)).then_inc(w_in4[p][k], 16)

            for k in range(4):
                load(0, k, 0)
            for k in range(4):
                sp.wait_ge(lo_ready[0][k], 1)
                load(1, k, P)
            with sp.Fori(1, TURNS) as i:
                starts = [sp.snap((2 * i + p) * P) for p in range(2)]
                tiles_before = [i, sp.snap(i + 1)]
                for p in range(2):
                    for k in range(4):
                        if k != 1:
                            sp.wait_ge(lo_ready[1 - p][max(k, 1)], tiles_before[p])
                        load(p, k, starts[p])
            for c, part in ((0, wo_low), (KC // 2, wo_high)):
                sp.dma_start(part, w_out[c * P:(c + KC // 2) * P, :].rearrange("(c p) n -> p c n", p=P)).then_inc(wo_in, 16)
            sp.wait_ge(ao_split, 1)
            sp.dma_start(g_row, ln_g.partition_broadcast(P)).then_inc(ln_in, 16)
            sp.dma_start(b_row, ln_b.partition_broadcast(P)).then_inc(ln_in, 16)
            for t in range(TT):
                sp.wait_ge(ln_done[t], 1)
                sp.dma_start(x1_rows[t * P:(t + 1) * P, :], xs[:, t, :]).then_inc(x1_out, 16)

        @block.tensor
        def _(pe):
            def body(i, first):
                for p in range(2):
                    for k in range(4):
                        n = sources[k][2]
                        pe.wait_ge(lo_ready[p][k], i + 1)
                        if k == 3 and first and p == 0:
                            pe.wait_ge(ao_split, 1)
                        if not first:
                            pe.wait_ge(gated[p][k // 2] if k % 2 else sig_ready[p][k // 2], i)
                        wh, wl = w_hi[:, k % 2, :, :], w_lo[:, k % 2, :, :]
                        xh, xl = moving[k]
                        for c in range(n):
                            for part, (w, x) in enumerate([(wh, xh), (wh, xl), (wl, xh)]):
                                mm = nc.tensor.matmul(ps[4 * p + k][:, :], w[:, c, :].bitcast(F32R), x[:, c, :].bitcast(F32R),
                                                      start=(c == 0 and part == 0), stop=(c == n - 1 and part == 2))
                        mm.then_inc(prod[p][k], 1)

            body(0, True)
            with pe.Fori(1, TURNS) as i:
                body(i, False)
            pe.wait_ge(wo_in, 32)
            for p in range(2):
                pe.wait_ge(merged[p], TURNS)
            for t in range(TT):
                for half in range(2):
                    for c in range(KC):
                        mm = nc.tensor.matmul(ps[2 * t + half][:, :], mT[:, c, t * P:(t + 1) * P],
                                              wo(c)[:, half * HALF:(half + 1) * HALF], start=(c == 0), stop=(c == KC - 1))
                mm.then_inc(mix_psum[t], 1)
            for c in range(KC):
                for t in range(TT):
                    if c == 0:
                        pe.wait_ge(ln_done[t], 1)
                    if c >= 4:
                        pe.wait_ge(x1t_ready, c - 3)
                    mm = nc.tensor.transpose(ps[c % 4][:, t * P:(t + 1) * P], xs[:, t, c * P:(c + 1) * P], ident[:, :])
                mm.then_inc(x1t_psum, 1)

        @block.scalar
        def _(act):
            def high(i, p, k):
                n = sources[k][2]
                act.wait_ge(w_in4[p][k], 16 * i + 16)
                nc.scalar.copy(w_hi[:, k % 2, 0:n, :].bitcast(F32R), w_t[:, k * KC:k * KC + n, :]).then_inc(hi_ready[p][k], 1)

            def body(i, first=False, last=False):
                for p in range(2):
                    for k in range(4):
                        act.wait_ge(prod[p][k], i + 1)
                        if not (last and p == 1 and k >= 2):
                            high(*two_on(i, p, k))
                        if k % 2 == 0:
                            if not first:
                                act.wait_ge(merged[p], i)
                            nc.scalar.activation(sg[:, p, k // 2, :], ps[4 * p + k][:, :],
                                                 ACT.Sigmoid).then_inc(sig_ready[p][k // 2], 1)

            for k in range(2):
                high(0, 0, k)
            body(0, first=True)
            with act.Fori(1, TURNS - 1) as i:
                body(i)
            body(TURNS - 1, last=True)
            nc.scalar.preload_act_table_set(LN_EXP)
            for t in range(TT):
                act.wait_ge(ag_done[t], 1)
                nc.scalar.activation(mv[:, t, 2:3], mv[:, t, 1:2], ACT.Ln, bias=eps[:, 2:3]).then_inc(ln_ln[t], 1)
                act.wait_ge(ln_ln[t], 1)
                nc.scalar.activation(mv[:, t, 3:4], mv[:, t, 2:3], ACT.Exp, scale=-0.5).then_inc(ln_rs[t], 1)
            for c in range(KC):
                act.wait_ge(x1t_psum, c + 1)
                nc.scalar.copy(xT[:, c, :], ps[c % 4][:, :]).then_inc(x1t_ready, 1)

        @block.gpsimd
        def _(pool):
            nc.gpsimd.tensor_copy(aoh[:, :, :].bitcast(F32R), aoT[:, :, :]).then_inc(aoh_ready, 1)
            pool.wait_ge(aoh_ready, 1)
            nc.gpsimd.tensor_tensor(aol[:, :, :].bitcast(F32R), aoT[:, :, :], aoh[:, :, :], ALU.subtract).then_inc(ao_split, 1)
            pool.wait_ge(ln_in, 32)
            for t in range(TT):
                pool.wait_ge(ln_m[t], 1)
                nc.gpsimd.tensor_tensor(xs[:, t, :], xs[:, t, :], b_row, ALU.add).then_inc(ln_done[t], 1)

        @block.vector
        def _(dve):
            def low(i, p, k):
                n = sources[k][2]
                dve.wait_ge(hi_ready[p][k], i + 1)
                nc.vector.tensor_tensor(w_lo[:, k % 2, 0:n, :].bitcast(F32R), w_t[:, k * KC:k * KC + n, :], w_hi[:, k % 2, 0:n, :], ALU.subtract).then_inc(lo_ready[p][k], 1)

            def body(i, last=False):
                for p in range(2):
                    for k in range(4):
                        if not (last and p == 1 and k >= 2):
                            low(*two_on(i, p, k))
                        if k % 2:
                            dve.wait_ge(prod[p][k], i + 1)
                            dve.wait_ge(sig_ready[p][k // 2], i + 1)
                            nc.vector.tensor_tensor(sg[:, p, k // 2, :], sg[:, p, k // 2, :], ps[4 * p + k][:, :],
                                                    ALU.mult).then_inc(gated[p][k // 2], 1)
                    dve.wait_ge(gated[p][1], i + 1)
                    nc.vector.tensor_tensor(mT[:, 2 * i + p, :], sg[:, p, 0, :], sg[:, p, 1, :], ALU.add).then_inc(merged[p], 1)

            for k in range(2):
                low(0, 0, k)
            with dve.Fori(0, TURNS - 1) as i:
                body(i)
            body(TURNS - 1, last=True)
            for t in range(TT):
                dve.wait_ge(mix_psum[t], 1)
                for half in range(2):
                    at = slice(half * HALF, (half + 1) * HALF)
                    nc.vector.scalar_tensor_tensor(out=xs[:, t, at], in0=xs[:, t, at], scalar=ALPHA, in1=ps[2 * t + half][:, :],
                                                   op0=ALU.mult, op1=ALU.add).then_inc(z_done[t], 1)
                for half in range(2):
                    dve.wait_ge(z_done[t], half + 1)
                    nc.vector.bn_stats(stats[:, t, half, :], xs[:, t, half * HALF:(half + 1) * HALF]).then_inc(st_done[t], 1)
                dve.wait_ge(st_done[t], 2)
                nc.vector.bn_aggr(mv[:, t, 0:2], stats[:, t, :, :]).then_inc(ag_done[t], 1)
                if t == 0:
                    dve.wait_ge(ln_in, 32)
                dve.wait_ge(ln_rs[t], 1)
                nc.vector.tensor_scalar(xs[:, t, :], xs[:, t, :], mv[:, t, 0:1], mv[:, t, 3:4],
                                        ALU.subtract, ALU.mult).then_inc(ln_n[t], 1)
                dve.wait_ge(ln_n[t], 1)
                nc.vector.tensor_tensor(xs[:, t, :], xs[:, t, :], g_row, ALU.mult).then_inc(ln_m[t], 1)


def route_phase(nc, mem, T, ps, router_w, router_bias, ws_gu, ws_down):
    S = mem.sem
    r_in, s_in = S("r_in"), S("s_in")
    lg_psum, sc_done = S("lg_psum"), S("sc_done")
    rt = S("rt")
    gs = S("gs")
    m_ready, pos_psum = S("m_ready"), S("pos_psum")
    vals_ready = S("vals_ready")
    ov_ready, ov_psum, ov_rows = S("ov_ready"), S("ov_psum"), S("ov_rows")
    sel_ready = mem.sems("sel_ready", 2)
    sel_used = mem.sems("sel_used", 2)
    sg_psum = mem.sems("sg_psum", 4)
    sg_act = mem.sems("sg_act", 2)

    xT, ident, upper, ones = T["xT"], T["ident"], T["upper"], T["ones"]
    wr = mem.sb("wr", [P, KC, NE])
    brow = mem.sb("brow", [P, NE])
    wg = mem.sb("ws_gu", [P, KC, 2 * ED])
    wd, hT = T["ws_down"], T["shared_hT"]
    score = mem.sb("score", [P, TT, NE])
    biased = mem.sb("biased", [P, TT, NE])
    top = mem.sb("top", [P, TT, 8])
    topi = mem.sb("topi", [P, TT, 8], mybir.dt.uint32)
    topf = mem.sb("topf", [P, TT, 8])
    hot = mem.sb("hot", [P, TOPK, TT, NE])
    M = mem.sb("M", [P, TT, NE])
    kidx = mem.sb("kidx", [P, TT, NE])
    wsel = mem.sb("wsel", [P, TT, NE])
    wsum = mem.sb("wsum", [P, TT, 2])
    rest = biased
    strict = mem.sb("strict", [P, P])
    iota_e, place = mem.sb("iota_e", [P, NE]), mem.sb("place", [P, 3])
    slot = mem.sb("slot", [P, NBLK + 1, BLK])
    thr = mem.sb("thr", [P, NE, NBLK])
    e_of = mem.sb("e_of", [P, NE, NBLK])
    b_of = mem.sb("b_of", [P, NE, NBLK])
    over = mem.sb("over", [P, NE, NBLK])
    incl = mem.sb("incl", [P, NE, NBLK])
    hit = mem.sb("hit", [P, NE, NBLK])
    groups = mem.sb("groups", [P, MAXOVER // GROUP + 1])
    ov = mem.sb("ov", [P, 8])
    posm, vals, cnt = mem.sb("posm", [P, TT, NE]), mem.sb("vals", [P, TT, NE, 8], BF16), mem.sb("cnt", [P, NE])
    listed = mem.sb("listed", [P, LISTS, 8])
    work = mem.sb("list_work", [P, 3, LISTS])
    low = mem.sb("low", [P, NE // 2, 8])
    low_later = mem.sb("low_later", [BLK, LISTS - NE, 8])
    twice = mem.sb("twice", [P, P])
    halves = [slice(0, BLK), slice(BLK, P)]
    half_listed, listed_psum = S("half_listed"), S("listed_psum")
    blk_b = mem.sb("blk_b", [1, P], I32)
    blk_e, trips = mem.sb("blk_e", [1, LISTS], I32), mem.sb("trips", [1, 1], I32)
    over_from = T["over_from"]
    tile_no = mem.sb("tile_no", [P, TT])
    AT_ONCE = 4
    BATCHES = NE // (2 * AT_ONCE)
    sel = mem.sb("sel", [P, 2, TT, AT_ONCE, BLK], BF16)
    by_expert = lambda a: a.unsqueeze(1).broadcast_to([P, TT, NE])
    by_tile = lambda a: a.unsqueeze(2).broadcast_to([P, TT, NE])

    with nc.Block() as block:

        @block.sync
        def _(sp):
            sp.dma_start(wr[:, :, :], router_w.rearrange("(c p) n -> p c n", p=P)).then_inc(r_in, 16)
            sp.dma_start(brow[:, :], router_bias.partition_broadcast(P)).then_inc(r_in, 16)
            sp.dma_start(wg[:, :, :], ws_gu.rearrange("(c p) n -> p c n", p=P)).then_inc(s_in, 16)
            sp.dma_start(wd[:, :, :], ws_down.rearrange("(c p) n -> p c n", p=P)).then_inc(s_in, 16)
            for s in range(GROUP):
                T["load_gu"](sp, s, s)
                T["load_down"](sp, s, s)

        @block.gpsimd
        def _(pool):
            nc.gpsimd.iota(iota_e[:, :], pattern=[[1, NE]], base=0, channel_multiplier=0,
                           allow_small_or_imprecise_dtypes=True).then_inc(gs, 1)
            nc.gpsimd.iota(place[:, 0:1], pattern=[[0, 1]], base=0, channel_multiplier=1,
                           allow_small_or_imprecise_dtypes=True).then_inc(gs, 1)
            nc.gpsimd.iota(slot[:, :, :], pattern=[[BLK, NBLK + 1], [1, BLK]], base=0, channel_multiplier=0,
                           allow_small_or_imprecise_dtypes=True).then_inc(gs, 1)
            nc.gpsimd.iota(tile_no[:, :], pattern=[[1, TT]], base=0, channel_multiplier=0,
                           allow_small_or_imprecise_dtypes=True).then_inc(gs, 1)
            nc.gpsimd.tensor_tensor(strict[:, :], upper[:, :], ident[:, :], ALU.subtract).then_inc(gs, 1)
            for table, pattern in ((thr, [[0, NE], [BLK, NBLK]]), (e_of, [[1, NE], [0, NBLK]]),
                                   (b_of, [[0, NE], [1, NBLK]]), (groups, [[GROUP, MAXOVER // GROUP + 1]])):
                nc.gpsimd.iota(table[:], pattern=pattern, base=0, channel_multiplier=0,
                               allow_small_or_imprecise_dtypes=True).then_inc(gs, 1)

        @block.tensor
        def _(pe):
            pe.wait_ge(r_in, 32)
            for t in range(TT):
                for c in range(KC):
                    mm = nc.tensor.matmul(ps[0][:, t * NE:(t + 1) * NE], xT[:, c, t * P:(t + 1) * P], wr[:, c, :],
                                          start=(c == 0), stop=(c == KC - 1))
            mm.then_inc(lg_psum, 1)
            def shared_hidden(g):
                for c in range(KC):
                    mm = nc.tensor.matmul(ps[2 + g][:, :], wg[:, c, g * P:(g + 1) * P], xT[:, c, :],
                                          start=(c == 0), stop=(c == KC - 1))
                mm.then_inc(sg_psum[g], 1)

            pe.wait_ge(s_in, 32)
            shared_hidden(0)
            pe.wait_ge(m_ready, 1)
            pe.wait_ge(gs, 5)
            for t in range(TT):
                for u in range(t):
                    nc.tensor.matmul(ps[0][:, t * NE:(t + 1) * NE], ones[:, :], M[:, u, :], start=(u == 0), stop=False)
                nc.tensor.matmul(ps[0][:, t * NE:(t + 1) * NE], strict[:, :], M[:, t, :], start=(t == 0), stop=True)
            for u in range(TT):
                mm = nc.tensor.matmul(ps[0][:, TT * NE:(TT + 1) * NE], ones[:, :], M[:, u, :], start=(u == 0),
                                      stop=(u == TT - 1))
            mm.then_inc(pos_psum, 1)
            for g in range(1, 4):
                shared_hidden(g)
            pe.wait_ge(ov_ready, 1)
            for k in range(2):
                pe.wait_ge(sg_act[k], 1)
            nc.tensor.transpose(ps[3][0:1, 0:P], ov[:, 0:1], ident[:, :])
            nc.tensor.transpose(ps[3][0:1, P:2 * P], ov[:, 1:2], ident[:, :]).then_inc(ov_psum, 1)
            pe.wait_ge(vals_ready, 1)

            with pe.Fori(0, BATCHES) as i:
                for q in range(2):
                    pe.wait_ge(sel_ready[q], i + 1)
                    for m in range(0, AT_ONCE, 2):
                        e = 2 * AT_ONCE * i + (AT_ONCE * q + m)
                        for t in range(TT):
                            mm = nc.tensor.matmul(ps[1][:, bass.ds(8 * e, 16)],
                                                  sel[:, q, t, m:m + 2, :].rearrange("p m c -> p (m c)"),
                                                  vals[:, t, bass.ds(e, 2), :], start=(t == 0), stop=(t == TT - 1))
                    mm.then_inc(sel_used[q], 1)
            pe.wait_ge(ov_rows, 1)
            turns = pe.value_load(trips[0:1, 0:1], min_val=1, max_val=MAXOVER // GROUP + 1)
            with pe.Fori(0, turns) as i:
                for k in range(GROUP):
                    q = k % 2
                    e = pe.value_load(blk_e[0:1, bass.ds(GROUP * i + (NE + k), 1)], min_val=0, max_val=NE - 1)
                    pe.wait_ge(sel_ready[q], 2 * i + (BATCHES + k // 2 + 1))
                    for t in range(TT):
                        mm = nc.tensor.matmul(ps[2][0:BLK, bass.ds(8 * GROUP * i + 8 * k, 8)], sel[:, q, t, 0, :],
                                              vals[:, t, bass.ds(e, 1), :], start=(t == 0), stop=(t == TT - 1))
                    mm.then_inc(sel_used[q], 1)
            pe.wait_ge(half_listed, 3)
            for a in range(2):
                nc.tensor.matmul(ps[4 + a][:, 0:8 * NE // 2], twice[halves[a], :], low[halves[a], :, :],
                                 start=True, stop=True)
            nc.tensor.matmul(ps[2][:, 0:8 * (LISTS - NE)], twice[halves[0], :], low_later[:, :, :], start=True,
                             stop=True).then_inc(listed_psum, 1)

        @block.scalar
        def _(act):
            act.wait_ge(lg_psum, 1)
            nc.scalar.activation(score[:, :, :], ps[0][:, 0:TT * NE].rearrange("p (t n) -> p t n", n=NE),
                                 ACT.Sigmoid).then_inc(sc_done, 1)
            for k in range(2):
                act.wait_ge(sg_psum[k], 1)
                nc.scalar.activation(hT[:, k, :], ps[2 + k][:, :], ACT.Silu).then_inc(sg_act[k], 1)

        @block.vector
        def _(dve):
            step = [0]

            def then(instruction):
                step[0] += 1
                instruction.then_inc(rt, 1)
                dve.wait_ge(rt, step[0])

            dve.wait_ge(sc_done, 1)
            dve.wait_ge(r_in, 32)
            then(nc.vector.tensor_tensor(biased[:, :, :], score[:, :, :], by_expert(brow[:, :]), ALU.add))
            for t in range(TT):
                last = nc.vector.max(top[:, t, :], biased[:, t, :])
            then(last)
            for t in range(TT):
                last = nc.vector.max_index(topi[:, t, :], top[:, t, :], biased[:, t, :])
            then(last)
            then(nc.vector.tensor_copy(topf[:, :, :], topi[:, :, :]))
            dve.wait_ge(gs, 9)
            nc.vector.tensor_scalar(place[:, 1:2], place[:, 0:1], 1.0, None, ALU.add)
            nc.vector.tensor_scalar(place[:, 2:3], place[:, 0:1], float(BLK), None, ALU.is_ge)
            nc.vector.memset(ov[:, :], 0.0)
            for a in range(2):
                for b in range(2):
                    nc.vector.tensor_copy(twice[halves[a], halves[b]], ident[halves[a], halves[a]])
            for k in range(TOPK):
                last = nc.vector.tensor_tensor(hot[:, k, :, :], by_expert(iota_e[:, :]), by_tile(topf[:, :, k]), ALU.is_equal)
            then(last)
            then(nc.vector.tensor_tensor(M[:, :, :], hot[:, 0, :, :], hot[:, 1, :, :], ALU.add))
            for k in range(2, TOPK):
                last = nc.vector.tensor_tensor(M[:, :, :], M[:, :, :], hot[:, k, :, :], ALU.add)
                if k < TOPK - 1:
                    then(last)
            last.then_inc(m_ready, 1)
            flat = lambda a: a.rearrange("p t n -> p (t n)")
            then(nc.vector.scalar_tensor_tensor(out=flat(kidx[:, :, :]), in0=flat(hot[:, 2, :, :]), scalar=2.0,
                                                in1=flat(hot[:, 1, :, :]), op0=ALU.mult, op1=ALU.add))
            for k in range(3, TOPK):
                then(nc.vector.scalar_tensor_tensor(out=flat(kidx[:, :, :]), in0=flat(hot[:, k, :, :]), scalar=float(k),
                                                    in1=flat(kidx[:, :, :]), op0=ALU.mult, op1=ALU.add))
            dve.wait_ge(m_ready, 1)
            then(nc.vector.tensor_tensor(wsel[:, :, :], score[:, :, :], M[:, :, :], ALU.mult))
            then(nc.vector.tensor_reduce(wsum[:, :, 0], wsel[:, :, :], AX.X, ALU.add))
            then(nc.vector.reciprocal(wsum[:, :, 1], wsum[:, :, 0]))
            then(nc.vector.tensor_scalar(wsum[:, :, 0], wsum[:, :, 1], ROUTED_SCALE, None, ALU.mult))
            then(nc.vector.tensor_tensor(wsel[:, :, :], wsel[:, :, :], by_tile(wsum[:, :, 0]), ALU.mult))
            nc.vector.tensor_copy(vals[:, :, :, 0], by_tile(tile_no[:, :]))
            nc.vector.tensor_copy(vals[:, :, :, 1], place[:, 0:1].unsqueeze(2).broadcast_to([P, TT, NE]))
            nc.vector.tensor_copy(vals[:, :, :, 2], kidx[:, :, :])
            nc.vector.memset(vals[:, :, :, 3], 1.0)
            nc.vector.memset(vals[:, :, :, 7], 0.0)
            then(nc.vector.tensor_copy(vals[:, :, :, 4], wsel[:, :, :]))
            then(nc.vector.tensor_tensor(rest[:, :, :], wsel[:, :, :], vals[:, :, :, 4], ALU.subtract))
            then(nc.vector.tensor_copy(vals[:, :, :, 5], rest[:, :, :]))
            then(nc.vector.tensor_tensor(rest[:, :, :], rest[:, :, :], vals[:, :, :, 5], ALU.subtract))
            nc.vector.tensor_copy(vals[:, :, :, 6], rest[:, :, :]).then_inc(vals_ready, 1)
            dve.wait_ge(pos_psum, 1)
            nc.vector.tensor_copy(cnt[:, :], ps[0][:, TT * NE:(TT + 1) * NE])
            then(nc.vector.scalar_tensor_tensor(out=posm[:, :, :].rearrange("p t n -> p (t n)"), in0=ps[0][:, 0:TT * NE],
                                                scalar=1.0, in1=flat(M[:, :, :]), op0=ALU.add, op1=ALU.mult))
            then(nc.vector.tensor_scalar(posm[:, :, :], posm[:, :, :], -1.0, None, ALU.add))
            wide = lambda a: a.unsqueeze(2).broadcast_to([P, NE, NBLK])
            line = lambda a: a.rearrange("p e b -> p (e b)")
            then(nc.vector.tensor_tensor(over[:, :, :], wide(cnt[:, :]), thr[:, :, :], ALU.is_gt))
            then(nc.vector.memset(over[:, :, 0], 0.0))
            then(nc.vector.memset(hit[:, :, :], 1.0))
            then(nc.vector.tensor_tensor_scan(line(incl[:, :, :]), line(hit[:, :, :]), line(over[:, :, :]), 0.0,
                                              ALU.mult, ALU.add))
            then(nc.vector.tensor_tensor(over[:, :, :], over[:, :, :], incl[:, :, :], ALU.mult))
            then(nc.vector.tensor_scalar(hit[:, :, :], over[:, :, :], place[:, 1:2], None, ALU.is_equal))
            then(nc.vector.tensor_tensor(over[:, :, :], hit[:, :, :], e_of[:, :, :], ALU.mult))
            then(nc.vector.tensor_reduce(ov[:, 0:1], line(over[:, :, :]), AX.X, ALU.add))
            then(nc.vector.tensor_tensor(over[:, :, :], hit[:, :, :], b_of[:, :, :], ALU.mult))
            then(nc.vector.tensor_reduce(ov[:, 2:3], line(over[:, :, :]), AX.X, ALU.add))
            then(nc.vector.tensor_reduce(ov[:, 3:4], line(hit[:, :, :]), AX.X, ALU.add))
            then(nc.vector.tensor_scalar(ov[:, 3:4], ov[:, 3:4], -float(NBLK), float(NBLK), ALU.mult, ALU.add))
            nc.vector.tensor_tensor(ov[:, 1:2], ov[:, 2:3], ov[:, 3:4], ALU.add).then_inc(ov_ready, 1)
            then(nc.vector.tensor_scalar(groups[:, :], groups[:, :], incl[:, NE - 1, NBLK - 1:NBLK], None, ALU.is_le))
            then(nc.vector.tensor_reduce(ov[:, 4:5], groups[:, :], AX.X, ALU.add))
            then(nc.vector.tensor_copy(trips[:, :], ov[0:1, 4:5]))
            nc.vector.memset(over_from[:, 0:1], 0)
            then(nc.vector.tensor_copy(over_from[:, 1:NE + 1], incl[0:1, :, NBLK - 1]))
            def first_blocks(i, q):
                shape = [P, TT, AT_ONCE, BLK]
                where = posm[:, :, bass.ds(2 * AT_ONCE * i + AT_ONCE * q, AT_ONCE)]
                nc.vector.tensor_tensor(sel[:, q, :, :, :], slot[:, 0:1, :].unsqueeze(1).broadcast_to(shape),
                                        where.unsqueeze(3).broadcast_to(shape), ALU.is_equal).then_inc(sel_ready[q], 1)

            for q in range(2):
                first_blocks(0, q)
            dve.wait_ge(ov_psum, 1)
            then(nc.vector.tensor_copy(blk_e[:, 0:NE], iota_e[0:1, :]))
            then(nc.vector.tensor_copy(blk_e[:, NE:LISTS], ps[3][0:1, 0:LISTS - NE]))
            nc.vector.tensor_copy(blk_b[:, :], ps[3][0:1, P:2 * P]).then_inc(ov_rows, 1)
            with dve.Fori(1, BATCHES) as i:
                for q in range(2):
                    dve.wait_ge(sel_used[q], i)
                    first_blocks(i, q)
            for k in range(2):
                dve.wait_ge(sg_act[k], 1)
                dve.wait_ge(sg_psum[2 + k], 1)
                then(nc.vector.tensor_tensor(hT[:, k, :], hT[:, k, :], ps[4 + k][:, :], ALU.mult))
            dve.wait_ge(ov_rows, 1)
            turns = dve.value_load(trips[0:1, 0:1], min_val=1, max_val=MAXOVER // GROUP + 1)

            def later(i, k):
                e = dve.value_load(blk_e[0:1, bass.ds(GROUP * i + (NE + k), 1)], min_val=0, max_val=NE - 1)
                b = dve.value_load(blk_b[0:1, bass.ds(GROUP * i + k, 1)], min_val=0, max_val=NBLK)
                nc.vector.tensor_tensor(sel[:, k % 2, :, 0, :], slot[:, bass.ds(b, 1), :].broadcast_to([P, TT, BLK]),
                                        posm[:, :, bass.ds(e, 1)].broadcast_to([P, TT, BLK]),
                                        ALU.is_equal).then_inc(sel_ready[k % 2], 1)

            with dve.Fori(0, turns) as i:
                for k in range(GROUP):
                    dve.wait_ge(sel_used[k % 2], 2 * i + (BATCHES + k // 2))
                    later(i, k)
            for q in range(2):
                dve.wait_ge(sel_used[q], 2 * turns + BATCHES)
            by_block = lambda bank, n: bank[:, 0:8 * n].rearrange("p (e v) -> p e v", v=8)
            for a in range(2):
                nc.vector.tensor_copy(low[halves[a], :, :], by_block(ps[1], NE)[halves[a], bass.ds(a, NE // 2, 2), :]) \
                    .then_inc(half_listed, 1)
            nc.vector.tensor_copy(low_later[:, :, :], by_block(ps[2][0:BLK, :], LISTS - NE)).then_inc(half_listed, 1)
            dve.wait_ge(listed_psum, 1)
            for a in range(2):
                nc.vector.tensor_copy(listed[:, bass.ds(a, NE // 2, 2), :], by_block(ps[4 + a], NE // 2))
            then(nc.vector.tensor_copy(listed[:, NE:LISTS, :], by_block(ps[2], LISTS - NE)))
            col = lambda k: listed[:, :, k]
            then(nc.vector.scalar_tensor_tensor(out=work[:, 0, :], in0=col(0), scalar=float(P), in1=col(1),
                                                op0=ALU.mult, op1=ALU.add))
            then(nc.vector.tensor_scalar(work[:, 1, :], col(3), -OOB, OOB, ALU.mult, ALU.add))
            then(nc.vector.tensor_scalar(work[:, 2, :], col(2), 2.0, place[:, 2:3], ALU.mult, ALU.add))
            then(nc.vector.scalar_tensor_tensor(out=work[:, 2, :], in0=work[:, 0, :], scalar=2.0 * TOPK,
                                                in1=work[:, 2, :], op0=ALU.mult, op1=ALU.add))
            for a in range(2):
                part, every = slice(a * BLK, (a + 1) * BLK), bass.ds(a, NE // 2, 2)
                nc.vector.tensor_tensor(T["tok_idx"][part, :], work[part, 0, every], work[part, 1, every], ALU.add)
            nc.vector.tensor_tensor(T["tok_over"][:, :], work[:, 0, NE:LISTS], work[:, 1, NE:LISTS], ALU.add)
            nc.vector.tensor_tensor(T["row_idx"][:, :], work[:, 2, :], work[:, 1, :], ALU.add)
            then(nc.vector.tensor_tensor(T["slot_w"][:, :], col(4), col(5), ALU.add))
            nc.vector.tensor_tensor(T["slot_w"][:, :], T["slot_w"][:, :], col(6), ALU.add)


def experts_phase(nc, mem, T, ps, x1_rows, y_rows):
    PAIRS = GROUP // 2
    TURNS = NE // GROUP
    gu_in, dn_in = T["gu_in"], T["dn_in"]
    first_col = mem.sems("first_col", PAIRS)
    col_ready = mem.sems("col_ready", PAIRS)
    gathered = mem.sems("gathered", PAIRS)
    xt_psum = mem.sems("ext_psum", GROUP)
    xt_ready = mem.sems("ext_ready", GROUP)
    gu_psum = mem.sems("gu_psum", GROUP)
    gate_ready = mem.sems("gate_ready", GROUP)
    h_ready = mem.sems("h_ready", GROUP)
    h_psum = mem.sems("h_psum", GROUP)
    ht_ready = mem.sems("ht_ready", GROUP)
    y_psum = mem.sems("ey_psum", GROUP)
    y_ready = mem.sems("ey_ready", GROUP)
    col2_ready = mem.sems("col2_ready", GROUP)
    scattered = mem.sems("scattered", GROUP)
    blank = mem.sem("blank")
    first_over_col, over_col = mem.sem("first_over_col"), mem.sem("over_col")
    over_gathered = mem.sem("over_gathered")
    over_xt_psum, over_xt_ready = mem.sem("over_xt_psum"), mem.sem("over_xt_ready")
    over_gu_psum, over_gate, over_h = mem.sem("over_gu_psum"), mem.sem("over_gate"), mem.sem("over_h")
    over_h_psum, over_ht, over_y_psum = mem.sem("over_h_psum"), mem.sem("over_ht"), mem.sem("over_y_psum")
    over_y, over_col2 = mem.sem("over_y"), mem.sem("over_col2")
    sd_psum, sd_done = mem.sem("sd_psum"), mem.sem("sd_done")
    over_free = mem.sem("over_free")

    ident, wgu, wdn = T["ident"], T["wgu"], T["wdn"]
    tok_idx, tok_over, row_idx, slot_w, over_from = (T[n] for n in ("tok_idx", "tok_over", "row_idx", "slot_w", "over_from"))
    x1_out = T["x1_out"]
    xg = mem.sb("gathered_x", [P, PAIRS, D])
    xgT = mem.sb("gathered_xT", [P, PAIRS, KC, P])
    gate = mem.sb("gate", [P, 2, P])
    h = mem.sb("hidden", [P, 2, P])
    hT = mem.sb("hiddenT", [P, 2, P])
    y = mem.sb("expert_y", [P, GROUP, D // 2])
    col = mem.sb("tok_col", [P, PAIRS], I32)
    col2 = mem.sb("row_col", [P, GROUP], I32)
    xo = mem.sb("over_x", [BLK, D])
    xoT = mem.sb("over_xT", [P, KC, BLK])
    gate_o, h_o, hT_o = (mem.sb(n, [P, P]) for n in ("over_gate", "over_hidden", "over_hiddenT"))
    yo = mem.sb("over_y", [P, D // 2])
    col_o, col2_o = mem.sb("over_tok_col", [P, 1], I32), mem.sb("over_row_col", [P, 1], I32)
    parts = [slice(0, BLK), slice(BLK, P)]
    HALF = D // 2
    xs = T["x"]
    shared = ps[5]

    def block_at(i, s):
        return s % GROUP, i + (s // GROUP + 1)

    def later_blocks(engine, i, s):
        return tuple(engine.value_load(over_from[0:1, bass.ds(GROUP * i + (s + k), 1)], min_val=0, max_val=MAXOVER)
                     for k in range(2))

    with nc.Block() as block:

        @block.sync
        def _(sp):
            with sp.Fori(1, TURNS) as i:
                for s in range(GROUP + 1):
                    if s < GROUP:
                        T["load_gu"](sp, s, GROUP * i + s, lambda: sp.wait_ge(gu_psum[s], i))
                    if s:
                        T["load_down"](sp, s - 1, GROUP * i + (s - 1), lambda: sp.wait_ge(y_psum[s - 1], i))

        @block.gpsimd
        def _(pool):
            nc.gpsimd.memset(xg[:, :, :], 0.0).then_inc(blank, 1)
            nc.gpsimd.memset(xo[:, :], 0.0).then_inc(blank, 1)
            pool.wait_ge(x1_out, 16 * TT)
            pool.dma_start(yo[:, :], x1_rows[0:P, 0:D // 2]).then_inc(over_free, 16)
            pool.wait_ge(blank, 2)
            last_token, last_row = pool.to_reg(SEQ - 1), pool.to_reg(2 * SEQ * TOPK - 1)

            def gather(i, q, first=False):
                if not first:
                    for a in range(2):
                        pool.wait_ge(xt_psum[2 * q + a], i)
                copied = first_col[q] if first else col_ready[q]
                nc.gpsimd.tensor_copy(col[:, q:q + 1], tok_idx[:, bass.ds(PAIRS * i + q, 1)]).then_inc(copied, 1)
                pool.wait_ge(x1_out, 16 * TT)
                pool.wait_ge(copied, 1 if first else i)
                nc.gpsimd.indirect_dma_start(
                    out=xg[:, q, :], out_offset=None, in_=x1_rows[:, :],
                    in_offset=bass.IndirectOffsetOnAxis(ap=col[:, q:q + 1], axis=0),
                    bounds_check=last_token, oob_is_err=False).then_inc(gathered[q], 16)

            def scatter(i, s):
                k, now = block_at(i, s)
                pool.wait_ge(y_ready[k], now)
                nc.gpsimd.tensor_copy(col2[:, k:k + 1], row_idx[:, bass.ds(GROUP * i + s, 1)]).then_inc(col2_ready[k], 1)
                pool.wait_ge(blank, 2)
                pool.wait_ge(col2_ready[k], now)
                nc.gpsimd.indirect_dma_start(
                    out=y_rows[:, :], out_offset=bass.IndirectOffsetOnAxis(ap=col2[:, k:k + 1], axis=0),
                    in_=y[:, k, :], in_offset=None,
                    bounds_check=last_row, oob_is_err=False).then_inc(scattered[k], 16)

            def gather_later(j, now, first=False):
                copied = first_over_col if first else over_col
                nc.gpsimd.tensor_copy(col_o[:, :], tok_over[:, bass.ds(j, 1)]).then_inc(copied, 1)
                pool.wait_ge(x1_out, 16 * TT)
                pool.wait_ge(copied, now)
                nc.gpsimd.indirect_dma_start(
                    out=xo[:, :], out_offset=None, in_=x1_rows[:, :],
                    in_offset=bass.IndirectOffsetOnAxis(ap=col_o[0:BLK, :], axis=0),
                    bounds_check=last_token, oob_is_err=False).then_inc(over_gathered, 16)

            def later(i, s):
                start, end = later_blocks(pool, i, s)
                with pool.If(start < end):
                    with pool.Fori(start, end) as j:
                        pool.wait_ge(over_xt_psum, j + 1)
                        gather_later(j + 1, j + 1)
                        pool.wait_ge(over_y, j + 1)
                        nc.gpsimd.tensor_copy(col2_o[:, :], row_idx[:, bass.ds(j + NE, 1)]).then_inc(over_col2, 1)
                        pool.wait_ge(blank, 2)
                        pool.wait_ge(over_col2, j + 1)
                        nc.gpsimd.indirect_dma_start(
                            out=y_rows[:, :], out_offset=bass.IndirectOffsetOnAxis(ap=col2_o[:, :], axis=0),
                            in_=yo[:, :], in_offset=None, bounds_check=last_row, oob_is_err=False).then_inc(over_free, 16)

            def turn(i, first=False, last=False):
                for s in range(GROUP):
                    later(i, s)
                    if not (first and s == 0):
                        scatter(i, s - 1)
                    if s % 2 == 0 and not last:
                        gather(i + 1, s // 2)

            for q in range(PAIRS):
                gather(0, q, True)
            gather_later(0, 1, True)
            turn(0, first=True)
            with pool.Fori(1, TURNS - 1) as i:
                turn(i)
            turn(TURNS - 1, last=True)
            scatter(TURNS - 1, GROUP - 1)
            for k in range(GROUP):
                pool.wait_ge(scattered[k], 16 * TURNS)
            blocks = pool.value_load(over_from[0:1, NE:NE + 1], min_val=0, max_val=MAXOVER)
            pool.wait_ge(over_free, 16 * blocks + 16)
            pool.wait_ge(over_gathered, 16 * blocks + 16)

        @block.tensor
        def _(pe):

            def transposes(i, q, a, first=False):
                pe.wait_ge(gathered[q], 16 * i + 16)
                if not first:
                    before, then_ = (q - 1) % PAIRS, i + (q - 1) // PAIRS + 1
                    pe.wait_ge(xt_ready[2 * before + a], then_)
                for c in range(KC // 2):
                    chunk = a * KC // 2 + c
                    mm = nc.tensor.transpose(ps[2 + a][:, c * P:(c + 1) * P], xg[:, q, chunk * P:(chunk + 1) * P], ident[:, :])
                mm.then_inc(xt_psum[2 * q + a], 1)

            def gate_up_products(bank, x, k, part):
                for c in range(KC):
                    halves = wgu[:, k, c, :].rearrange("p (g a n) -> p a g n", g=2, a=2)
                    for a in range(2):
                        mm = nc.tensor.matmul(bank[parts[a], 0:2 * P], x[:, c, part], halves[:, a, :, :],
                                              start=(c == 0), stop=(c == KC - 1))
                return mm

            def down_products(bank, hidden_t, k):
                for c in range(2):
                    for a in range(2):
                        mm = nc.tensor.matmul(bank[parts[a], :], hidden_t[:, c * BLK:(c + 1) * BLK],
                                              wdn[:, k, c, a * (D // 2):(a + 1) * (D // 2)], start=(c == 0), stop=(c == 1))
                return mm

            def later(i, s):
                start, end = later_blocks(pe, i, s)
                with pe.If(start < end):
                    with pe.Fori(start, end) as j:
                        pe.wait_ge(gu_in[s], 16 * i + 16)
                        pe.wait_ge(dn_in[s], 16 * i + 16)
                        pe.wait_ge(over_free, 16 * j + 16)
                        pe.wait_ge(over_gathered, 16 * j + 16)
                        for c in range(KC):
                            mm = nc.tensor.matmul(shared[:, c * BLK:(c + 1) * BLK], xo[:, c * P:(c + 1) * P],
                                                  ident[0:BLK, 0:BLK], start=True, stop=True)
                        mm.then_inc(over_xt_psum, 1)
                        pe.wait_ge(over_xt_ready, j + 1)
                        gate_up_products(shared, xoT, s, slice(0, BLK)).then_inc(over_gu_psum, 1)
                        pe.wait_ge(over_h, j + 1)
                        nc.tensor.transpose(shared[:, 0:P], h_o[:, :], ident[:, :]).then_inc(over_h_psum, 1)
                        pe.wait_ge(over_ht, j + 1)
                        down_products(shared, hT_o, s).then_inc(over_y_psum, 1)

            def gate_up(i, s, first=False):
                k, now = block_at(i, s)
                pe.wait_ge(gu_in[k], 16 * now)
                if s % 2 == 0:
                    for a in range(2):
                        pe.wait_ge(xt_ready[s + a], now)
                if not first:
                    before, then_ = block_at(i, s - 2)
                    pe.wait_ge(h_ready[before], then_)
                gate_up_products(ps[k % 2], xgT[:, s // 2, :, :], k, parts[s % 2]).then_inc(gu_psum[k], 1)

            def hidden(i, s, first=False):
                k, now = block_at(i, s)
                pe.wait_ge(h_ready[k], now)
                nc.tensor.transpose(ps[4][:, k % 2 * P:k % 2 * P + P], h[:, k % 2, :], ident[:, :]).then_inc(h_psum[k], 1)

            def down(i, s, first=False):
                k, now = block_at(i, s)
                pe.wait_ge(dn_in[k], 16 * now)
                pe.wait_ge(ht_ready[k], now)
                if not first:
                    before, then_ = block_at(i, s - 2)
                    pe.wait_ge(y_ready[before], then_)
                down_products(ps[6 + k % 2], hT[:, k % 2, :], k).then_inc(y_psum[k], 1)

            def shared_down(t):
                if t >= 2:
                    pe.wait_ge(y_ready[t - 2], 1)
                for half in range(2):
                    if half:
                        pe.wait_ge(sd_done, 2 * t + 1)
                    for k in range(2):
                        mm = nc.tensor.matmul(ps[6 + t % 2][:, :], T["shared_hT"][:, k, t * P:(t + 1) * P],
                                              T["ws_down"][:, k, half * HALF:(half + 1) * HALF],
                                              start=(k == 0), stop=(k == 1))
                    mm.then_inc(sd_psum, 1)

            def turn(i, first=False, last=False):
                for s in range(GROUP):
                    later(i, s)
                    if first and s:
                        pe.wait_ge(sd_done, 2 * s)
                    gate_up(i, s, first and s < 2)
                    if not (last and s >= GROUP - 2):
                        q = s // 2 + 1
                        transposes(i + q // PAIRS, q % PAIRS, s % 2)
                    if not (first and s == 0):
                        down(i, s - 1, first and s < 3)
                    hidden(i, s, first and s < 2)
                    if first:
                        shared_down(s)

            for a in range(2):
                transposes(0, 0, a, True)
            turn(0, first=True)
            pe.wait_ge(sd_done, 2 * TT)
            with pe.Fori(1, TURNS - 1) as i:
                turn(i)
            turn(TURNS - 1, last=True)
            down(TURNS - 1, GROUP - 1)

        @block.scalar
        def _(act):

            def later(i, s):
                start, end = later_blocks(act, i, s)
                with act.If(start < end):
                    with act.Fori(start, end) as j:
                        act.wait_ge(over_gu_psum, j + 1)
                        nc.scalar.activation(gate_o[:, :], shared[:, 0:P], ACT.Silu).then_inc(over_gate, 1)
                        act.wait_ge(over_h_psum, j + 1)
                        nc.scalar.copy(hT_o[:, :], shared[:, 0:P]).then_inc(over_ht, 1)
                        act.wait_ge(over_y_psum, j + 1)
                        act.wait_ge(over_free, 16 * j + 16)
                        nc.scalar.copy(yo[:, :], shared[:, :]).then_inc(over_y, 1)

            def turn(i, first=False, unused=False):
                for s in range(GROUP):
                    later(i, s)
                    k, now = block_at(i, s)
                    act.wait_ge(gu_psum[k], now)
                    nc.scalar.activation(gate[:, k % 2, :], ps[k % 2][:, 0:P], ACT.Silu).then_inc(gate_ready[k], 1)
                    if not (first and s == 0):
                        b, then_ = block_at(i, s - 1)
                        act.wait_ge(y_psum[b], then_)
                        if not (first or unused and s == 0):
                            act.wait_ge(scattered[b], 16 * (then_ - 1))
                        nc.scalar.copy(y[:, b, :], ps[6 + b % 2][:, :]).then_inc(y_ready[b], 1)
                    act.wait_ge(h_psum[k], now)
                    nc.scalar.copy(hT[:, k % 2, :], ps[4][:, k % 2 * P:k % 2 * P + P]).then_inc(ht_ready[k], 1)

            turn(0, first=True)
            turn(1, unused=True)
            with act.Fori(2, TURNS) as i:
                turn(i)
            b, then_ = block_at(TURNS - 1, GROUP - 1)
            act.wait_ge(y_psum[b], then_)
            act.wait_ge(scattered[b], 16 * (then_ - 1))
            nc.scalar.copy(y[:, b, :], ps[6 + b % 2][:, :]).then_inc(y_ready[b], 1)

        @block.vector
        def _(dve):

            def copy_x(i, q, a):
                dve.wait_ge(xt_psum[2 * q + a], i + 1)
                nc.vector.tensor_copy(xgT[:, q, a * KC // 2:(a + 1) * KC // 2, :],
                                      ps[2 + a][:, :].rearrange("p (c n) -> p c n", n=P)).then_inc(xt_ready[2 * q + a], 1)

            def weighted(out, silu, up, number):
                return nc.vector.scalar_tensor_tensor(out=out, in0=silu, scalar=slot_w[:, bass.ds(number, 1)], in1=up,
                                                      op0=ALU.mult, op1=ALU.mult)

            def later(i, s):
                start, end = later_blocks(dve, i, s)
                with dve.If(start < end):
                    with dve.Fori(start, end) as j:
                        dve.wait_ge(over_xt_psum, j + 1)
                        nc.vector.tensor_copy(xoT[:, :, :], shared[:, :].rearrange("p (c n) -> p c n", n=BLK)) \
                            .then_inc(over_xt_ready, 1)
                        dve.wait_ge(over_gate, j + 1)
                        weighted(h_o[:, :], gate_o[:, :], shared[:, P:2 * P], j + NE).then_inc(over_h, 1)

            def turn(i, first=False, last=False):
                for s in range(GROUP):
                    later(i, s)
                    k, now = block_at(i, s)
                    dve.wait_ge(gate_ready[k], now)
                    weighted(h[:, k % 2, :], gate[:, k % 2, :], ps[k % 2][:, P:2 * P], GROUP * i + s).then_inc(h_ready[k], 1)
                    if not (last and s >= GROUP - 2):
                        q = s // 2 + 1
                        copy_x(i + q // PAIRS, q % PAIRS, s % 2)
                    if first:
                        for half in range(2):
                            at = slice(half * HALF, (half + 1) * HALF)
                            dve.wait_ge(sd_psum, 2 * s + half + 1)
                            nc.vector.scalar_tensor_tensor(out=xs[:, s, at], in0=xs[:, s, at], scalar=ALPHA,
                                                           in1=ps[6 + s % 2][:, :], op0=ALU.mult,
                                                           op1=ALU.add).then_inc(sd_done, 1)

            for a in range(2):
                copy_x(0, 0, a)
            dve.wait_ge(x1_out, 16 * TT)
            turn(0, first=True)
            with dve.Fori(1, TURNS - 1) as i:
                turn(i)
            turn(TURNS - 1, last=True)


def final_phase(nc, mem, T, ps, ln_g, ln_b, y_rows, out):
    y_in = [mem.sems(f"y_in{t}_", TOPK) for t in range(TT)]
    s_done, pair_done = mem.sems("s_done", TT), mem.sems("pair_done", TT)
    ln_in = mem.sem("fln_in")
    st_done, ag_done, ln_ln, ln_rs, ln_n, ln_m, ln_done, out_done = (
        mem.sems(n, TT) for n in ("fst", "fag", "fll", "frs", "fln", "flm", "fld", "out_done"))
    xs, eps = T["x"], T["eps"]
    yt = mem.sb("choices", [P, TT, TOPK, D])
    g_row, b_row = mem.sb("ln2_g_row", [P, D]), mem.sb("ln2_b_row", [P, D])
    stats = mem.sb("ln2_stats", [P, TT, 2, 6])
    mv = mem.sb("ln2_mv", [P, TT, 4])
    rows = y_rows.rearrange("(t p k a) c -> t p k (a c)", t=TT, p=P, k=TOPK)

    with nc.Block() as block:

        @block.sync
        def _(sp):
            for t in range(TT):
                for k in (4, 5, 0, 1, 2, 3):
                    sp.dma_start(yt[:, t, k, :], rows[t, :, k, :]).then_inc(y_in[t][k], 16)
            for t in range(TT):
                sp.wait_ge(ln_done[t], 1)
                sp.dma_start(out[0, t * P:(t + 1) * P, :], xs[:, t, :]).then_inc(out_done[t], 16)
            for t in range(TT):
                sp.wait_ge(out_done[t], 16)

        @block.scalar
        def _(act):
            act.dma_start(g_row[:, :], ln_g.partition_broadcast(P)).then_inc(ln_in, 16)
            act.dma_start(b_row[:, :], ln_b.partition_broadcast(P)).then_inc(ln_in, 16)
            nc.scalar.preload_act_table_set(LN_EXP)
            for t in range(TT):
                act.wait_ge(ag_done[t], 1)
                nc.scalar.activation(mv[:, t, 2:3], mv[:, t, 1:2], ACT.Ln, bias=eps[:, 2:3]).then_inc(ln_ln[t], 1)
                act.wait_ge(ln_ln[t], 1)
                nc.scalar.activation(mv[:, t, 3:4], mv[:, t, 2:3], ACT.Exp, scale=-0.5).then_inc(ln_rs[t], 1)

        @block.gpsimd
        def _(pool):
            for t in range(TT):
                for k in (4, 5):
                    pool.wait_ge(y_in[t][k], 16)
                nc.gpsimd.tensor_tensor(yt[:, t, 4, :], yt[:, t, 4, :], yt[:, t, 5, :], ALU.add).then_inc(pair_done[t], 1)
            pool.wait_ge(ln_in, 32)
            for t in range(TT):
                pool.wait_ge(ln_m[t], 1)
                nc.gpsimd.tensor_tensor(xs[:, t, :], xs[:, t, :], b_row[:, :], ALU.add).then_inc(ln_done[t], 1)

        @block.vector
        def _(dve):
            HALF = D // 2
            for t in range(TT):
                for i, k in enumerate((4, 0, 1, 2, 3)):
                    dve.wait_ge(*((pair_done[t], 1) if k == 4 else (y_in[t][k], 16)))
                    if i:
                        dve.wait_ge(s_done[t], i)
                    nc.vector.tensor_tensor(xs[:, t, :], xs[:, t, :], yt[:, t, k, :], ALU.add).then_inc(s_done[t], 1)
                dve.wait_ge(s_done[t], 5)
                for half in range(2):
                    nc.vector.bn_stats(stats[:, t, half, :], xs[:, t, half * HALF:(half + 1) * HALF]).then_inc(st_done[t], 1)
                dve.wait_ge(st_done[t], 2)
                nc.vector.bn_aggr(mv[:, t, 0:2], stats[:, t, :, :]).then_inc(ag_done[t], 1)
                if t == 0:
                    dve.wait_ge(ln_in, 32)
                dve.wait_ge(ln_rs[t], 1)
                nc.vector.tensor_scalar(xs[:, t, :], xs[:, t, :], mv[:, t, 0:1], mv[:, t, 3:4],
                                        ALU.subtract, ALU.mult).then_inc(ln_n[t], 1)
                dve.wait_ge(ln_n[t], 1)
                nc.vector.tensor_tensor(xs[:, t, :], xs[:, t, :], g_row[:, :], ALU.mult).then_inc(ln_m[t], 1)


def program(nc, x, w_in, conv_w, a_log, dt_bias, dn_norm_w, rel_table, w_branch_a, w_branch_b, w_out, ln1_g, ln1_b,
            router_w, router_bias, expert_w_gate_up, expert_w_down, shared_w_gate_up, shared_w_down, ln2_g, ln2_b,
            out):
    with ExitStack() as ctx:
        mem = Memory(nc, ctx)
        ps = [ctx.enter_context(nc.psum_tensor(f"bank{i}", [P, 512], F32)) for i in range(8)]
        branches = ctx.enter_context(ExitStack())
        front = Memory(nc, branches)
        T = {
            "ident": mem.sb("ident", [P, P]),
            "upper": mem.sb("upper", [P, P]),
            "ones": mem.sb("ones", [P, P]),
            "eps": mem.sb("eps", [P, 3]),
            "x": mem.sb("x_rows", [P, TT, D]),
            "xT": mem.sb("xT", [P, KC, SEQ]),
            "masks": front.sb("masks", [P, LEVELS, P]),
            "GT": front.sb("gate_table", [P, HEADS, 6, TT]),
            "gate_work": front.sb("gate_work", [P, 6, HEADS * TT]),
            "bias_row": front.sb("bias_row", [P, 3 * HEADS]),
            "w_ba": front.sb("w_ba", [P, KC, 2 * HEADS]),
            "ba": front.sb("ba", [P, TT * 2 * HEADS]),
            "cw_rows": front.sb("cw_rows", [CONV * 3 * HEADS, P]),
            "cw": front.sb("cw", [P, CONV * 3 * HEADS]),
            "dn_w": front.sb("dn_w", [P, 1]),
            "dnT": front.sb("dnT", [P, HEADS, SEQ]),
            "aoT": front.sb("aoT", [P, AHEADS // 2, SEQ]),
        }
        w_in, conv_w, rel_table = w_in[0], conv_w[0], rel_table[0]
        rel_scratch = nc.dram_tensor("rel_scratch", [AHEADS, SEQ + P], F32, kind="Internal").ap()
        x1_rows = nc.dram_tensor("x1_rows", [SEQ, D], F32, kind="Internal").ap()
        attention = ctx.enter_context(ExitStack())
        shared = Memory(nc, attention)
        T["av"], T["qkT"] = shared.sb("av", [P, TT, AW]), shared.sb("attn_qk", [P, 2, SEQ])
        T["bias"] = shared.sb("rel_bias", [P, AHEADS, SEQ])
        heads = ctx.enter_context(ExitStack())
        T["w_head"] = Memory(nc, heads).sb("w_head", [P, 4, KC, P])
        T["w_ready"], T["proj_done"] = mem.sems("w_ready", 4), mem.sems("proj_done", 4)
        run_phase(nc, setup_phase, T, ps, x, w_in, conv_w, a_log, dt_bias, dn_norm_w)
        run_phase(nc, delta_phase, T, ps, w_in, rel_table, rel_scratch)
        heads.close()
        parts = ctx.enter_context(ExitStack())
        split = Memory(nc, parts)
        T["xh"], T["xl"] = split.sb("xh", [P, KC, SEQ]), split.sb("xl", [P, KC, SEQ])
        T["dnh"], T["dnl"] = split.sb("dnh", [P, HEADS, SEQ]), split.sb("dnl", [P, HEADS, SEQ])
        run_phase(nc, attention_phase, T, ps, w_in)
        T["x1_out"] = mem.sem("x1_out")
        run_phase(nc, merge_phase, T, ps, w_in, w_branch_a[0], w_branch_b[0], w_out[0], ln1_g[0:1, :], ln1_b[0:1, :],
                  x1_rows)
        parts.close()
        attention.close()
        branches.close()
        expert_buffers = ctx.enter_context(ExitStack())
        experts = Memory(nc, expert_buffers)
        T["wgu"] = experts.sb("expert_gu", [P, GROUP, KC, 2 * ED])
        T["wdn"] = experts.sb("expert_down", [P, GROUP, ED // P, D])
        T["ws_down"] = experts.sb("ws_down", [P, ED // P, D])
        T["shared_hT"] = experts.sb("shared_hT", [P, ED // P, SEQ])
        T["over_from"] = experts.sb("over_from", [1, NE + 1], I32)
        T["tok_idx"] = experts.sb("tok_idx", [P, NE // 2], I32)
        T["tok_over"] = experts.sb("tok_over", [P, LISTS - NE], I32)
        T["row_idx"] = experts.sb("row_idx", [P, LISTS], I32)
        T["slot_w"] = experts.sb("slot_w", [P, LISTS])
        T["gu_in"], T["dn_in"] = mem.sems("gu_in", GROUP), mem.sems("dn_in", GROUP)

        def load_gu(sp, s, e, free=None):
            part = expert_w_gate_up[0][bass.ds(e, 1)].rearrange("e (c p) n -> p (e c) n", p=P)
            if free:
                free()
            sp.dma_start(T["wgu"][:, s, :, :], part).then_inc(T["gu_in"][s], 16)

        def load_down(sp, s, e, free=None):
            part = expert_w_down[0][bass.ds(e, 1)].rearrange("e (c p) n -> p (e c) n", p=P)
            if free:
                free()
            sp.dma_start(T["wdn"][:, s, :, :], part).then_inc(T["dn_in"][s], 16)

        T["load_gu"], T["load_down"] = load_gu, load_down
        y_rows = nc.dram_tensor("y_rows", [2 * SEQ * TOPK, D // 2], F32, kind="Internal").ap()
        run_phase(nc, route_phase, T, ps, router_w[0], router_bias[0:1, :], shared_w_gate_up[0], shared_w_down[0])
        run_phase(nc, experts_phase, T, ps, x1_rows, y_rows)
        expert_buffers.close()
        run_phase(nc, final_phase, T, ps, ln2_g[0:1, :], ln2_b[0:1, :], y_rows, out)


_INS = ["x", "w_in", "conv_w", "a_log", "dt_bias", "dn_norm_w", "rel_table", "w_branch_a", "w_branch_b", "w_out",
        "ln1_g", "ln1_b", "router_w", "router_bias", "expert_w_gate_up", "expert_w_down", "shared_w_gate_up",
        "shared_w_down", "ln2_g", "ln2_b"]
_OUTS = [((1, SEQ, D), "float32")]


def kernel(**inputs):
    import numpy as _np
    import concourse.bacc as _bacc
    from concourse import mybir as _mybir
    from concourse.bass_utils import run_bass_kernel_spmd as _run

    nc = _bacc.Bacc("TRN2", target_bir_lowering=False, num_devices=1)
    arrays, args = {}, []
    for name in _INS:
        a = _np.ascontiguousarray(inputs[name])
        arrays[f"in_{name}_dram"] = a
        args.append(nc.dram_tensor(f"in_{name}_dram", a.shape, _mybir.dt.from_np(a.dtype), kind="ExternalInput").ap())
    for i, (shape, dtype) in enumerate(_OUTS):
        dt = _mybir.dt.from_np(_np.dtype(dtype))
        args.append(nc.dram_tensor(f"out_{i}_dram", shape, dt, kind="ExternalOutput").ap())
    program(nc, *args)
    r = _run(nc, [arrays], core_ids=[0])
    got = tuple(r.results[0][f"out_{i}_dram"] for i in range(len(_OUTS)))
    return got[0]
```
